# Optimizing a Trainium2 kernel written in Bass

```python
import math
import jax, jax.numpy as jnp
from jax import lax
import numpy as np

D_MODEL = 1024
BATCH = 1
SEQ = 256
DEPTH = 1

CHUNK = 64
Q_BLOCK = 128
EPS = 1e-6

DIFF_HEADS = 4
DIFF_HEAD_DIM = 64
DIFF_V_DIM = 2 * DIFF_HEAD_DIM
DIFF_QK_WIDTH = DIFF_HEADS * 2 * DIFF_HEAD_DIM
DIFF_V_WIDTH = DIFF_HEADS * DIFF_V_DIM

GDN_HEADS = 4
GDN_K_DIM = 128
GDN_V_DIM = 128
GDN_K_WIDTH = GDN_HEADS * GDN_K_DIM
GDN_V_WIDTH = GDN_HEADS * GDN_V_DIM
CONV_K = 4
GDN_CONV_WIDTH = 2 * GDN_K_WIDTH + GDN_V_WIDTH

MOE_GROUPS = 4
MOE_EXPERTS_PER_GROUP = 8
MOE_EXPERTS = MOE_GROUPS * MOE_EXPERTS_PER_GROUP
MOE_TOP_K = 2
MOE_HIDDEN = 256

IN_SPLITS = (DIFF_QK_WIDTH, DIFF_QK_WIDTH, DIFF_V_WIDTH, GDN_K_WIDTH, GDN_K_WIDTH, GDN_V_WIDTH, GDN_HEADS, GDN_HEADS, GDN_V_WIDTH, D_MODEL, D_MODEL)
IN_WIDTH = 3 * 512 + 3 * 512 + 2 * GDN_HEADS + GDN_V_WIDTH + 2 * D_MODEL

kernel_name = 'hybrid_diffattn_gdn_hmoe_block'

def rms_norm(x, gain):
    xf = x.astype(jnp.float32)
    y = xf * lax.rsqrt(jnp.mean(xf * xf, axis=-1, keepdims=True) + EPS)
    return (y * gain.astype(jnp.float32)).astype(x.dtype)

def l2_normalize(t):
    return t * lax.rsqrt(jnp.sum(t * t, axis=-1, keepdims=True) + EPS)

def causal_depthwise_conv(x, w):
    s = x.shape[1]
    xp = jnp.pad(x, ((0, 0), (CONV_K - 1, 0), (0, 0)))
    out = xp[:, 0:s] * w[0]
    for j in range(1, CONV_K):
        out = out + xp[:, j:j + s] * w[j]
    return out

def diff_attention(q, k, v, lam, subln_gain, lambda_init):
    b, s = q.shape[0], q.shape[1]
    nb = s // Q_BLOCK
    scale = DIFF_HEAD_DIM ** -0.5
    kf = k.astype(jnp.float32)
    vf = v.astype(jnp.float32)
    qb = q.astype(jnp.float32).reshape(b, nb, Q_BLOCK, DIFF_HEADS, 2, DIFF_HEAD_DIM).transpose(1, 0, 2, 3, 4, 5)
    key_chunk = jnp.arange(s) // CHUNK

    def block(args):
        q_blk, bidx = args
        sc = jnp.einsum('bqhcd,bkhcd->bhcqk', q_blk, kf) * scale
        q_chunk = (bidx * Q_BLOCK + jnp.arange(Q_BLOCK)) // CHUNK
        mask = key_chunk[None, :] <= q_chunk[:, None]
        sc = jnp.where(mask, sc, -jnp.inf)
        p = jax.nn.softmax(sc, axis=-1)
        a = p[:, :, 0] - lam * p[:, :, 1]
        return jnp.einsum('bhqk,bkhv->bqhv', a, vf)

    o = lax.map(block, (qb, jnp.arange(nb)))
    o = o.transpose(1, 0, 2, 3, 4).reshape(b, s, DIFF_HEADS, DIFF_V_DIM)
    o = rms_norm(o, subln_gain) * (1.0 - lambda_init)
    return o.reshape(b, s, DIFF_V_WIDTH)

def gated_delta_net(q, k, v, beta, g, norm_gain, gate):
    b, s = q.shape[0], q.shape[1]
    nc = s // CHUNK
    q = l2_normalize(q) * (GDN_K_DIM ** -0.5)
    k = l2_normalize(k)

    def to_chunks(t):
        return t.reshape(b, nc, CHUNK, GDN_HEADS, -1).transpose(0, 3, 1, 2, 4)

    qc, kc, vc = to_chunks(q), to_chunks(k), to_chunks(v)
    bc = beta.reshape(b, nc, CHUNK, GDN_HEADS).transpose(0, 3, 1, 2)
    gc = g.reshape(b, nc, CHUNK, GDN_HEADS).transpose(0, 3, 1, 2)
    gcum = jnp.cumsum(gc, axis=-1)
    causal = jnp.tril(jnp.ones((CHUNK, CHUNK), dtype=bool))
    strict = jnp.tril(jnp.ones((CHUNK, CHUNK), dtype=bool), -1)
    diff = gcum[..., :, None] - gcum[..., None, :]
    decay_mat = jnp.exp(jnp.where(causal, diff, -jnp.inf))
    kb = kc * bc[..., None]
    vb = vc * bc[..., None]
    a_low = jnp.where(strict, jnp.einsum('bhncd,bhnjd->bhncj', kb, kc) * decay_mat, 0.0)
    eye = jnp.eye(CHUNK, dtype=jnp.float32)
    rhs = jnp.concatenate([vb, kb * jnp.exp(gcum)[..., None]], axis=-1)
    sol = lax.linalg.triangular_solve(eye + a_low, rhs, left_side=True, lower=True, unit_diagonal=True)
    u, w = sol[..., :GDN_V_DIM], sol[..., GDN_V_DIM:]
    intra = jnp.einsum('bhncd,bhnjd->bhncj', qc, kc) * decay_mat
    q_dec = qc * jnp.exp(gcum)[..., None]
    k_dec = kc * jnp.exp(gcum[..., -1:] - gcum)[..., None]
    g_last = jnp.exp(gcum[..., -1])
    xs = tuple(jnp.moveaxis(t, 2, 0) for t in (q_dec, k_dec, u, w, intra, g_last))

    def step(state, inp):
        q_d, k_d, u_c, w_c, a_c, gl = inp
        v_new = u_c - jnp.einsum('bhck,bhkv->bhcv', w_c, state)
        o_c = jnp.einsum('bhck,bhkv->bhcv', q_d, state) + jnp.einsum('bhcj,bhjv->bhcv', a_c, v_new)
        state = state * gl[..., None, None] + jnp.einsum('bhck,bhcv->bhkv', k_d, v_new)
        return state, o_c

    s0 = jnp.zeros((b, GDN_HEADS, GDN_K_DIM, GDN_V_DIM), jnp.float32)
    _, o = lax.scan(step, s0, xs)
    o = o.transpose(1, 0, 3, 2, 4).reshape(b, s, GDN_HEADS, GDN_V_DIM)
    o = rms_norm(o, norm_gain) * jax.nn.silu(gate.astype(jnp.float32)).reshape(b, s, GDN_HEADS, GDN_V_DIM)
    return o.reshape(b, s, GDN_V_WIDTH)

def hier_moe(h, w_group, b_group, w_expert, b_expert, w_gate, w_up, w_down):
    b, s, d = h.shape
    t = h.reshape(b * s, d)
    tf = t.astype(jnp.float32)
    grp_logits = tf @ w_group.astype(jnp.float32) + b_group.astype(jnp.float32)
    grp_prob = jax.nn.softmax(grp_logits, axis=-1)
    grp_idx = jnp.argmax(grp_logits, axis=-1)
    grp_w = jnp.max(grp_prob, axis=-1, keepdims=True)
    exp_logits = (tf @ w_expert.astype(jnp.float32) + b_expert.astype(jnp.float32)).reshape(-1, MOE_GROUPS, MOE_EXPERTS_PER_GROUP)
    in_grp = jnp.einsum('tg,tge->te', jax.nn.one_hot(grp_idx, MOE_GROUPS, dtype=jnp.float32), exp_logits)
    top_val, top_idx = lax.top_k(in_grp, MOE_TOP_K)
    top_w = jax.nn.softmax(top_val, axis=-1) * grp_w
    expert_id = grp_idx[:, None] * MOE_EXPERTS_PER_GROUP + top_idx
    combine = jnp.einsum('tk,tke->te', top_w, jax.nn.one_hot(expert_id, MOE_EXPERTS, dtype=jnp.float32))
    hg = jnp.einsum('td,edf->tef', t, w_gate)
    hu = jnp.einsum('td,edf->tef', t, w_up)
    act = jax.nn.silu(hg) * hu * combine[..., None].astype(t.dtype)
    y = jnp.einsum('tef,efd->td', act, w_down)
    return y.reshape(b, s, d)

def setup_inputs(seed: int = 0) -> dict:
    key = jax.random.key(seed)
    ks = jax.random.split(key, 24)
    nrm = jax.random.normal
    f32 = jnp.float32
    dt = jnp.exp(jax.random.uniform(ks[9], (DEPTH, GDN_HEADS), f32, math.log(1e-3), math.log(1e-1)))
    return {
        'x': nrm(ks[0], (BATCH, SEQ, D_MODEL), f32),
        'norm_mix_gain': 1.0 + 0.02 * nrm(ks[1], (DEPTH, D_MODEL), f32),
        'w_in': nrm(ks[2], (DEPTH, D_MODEL, IN_WIDTH), f32) * D_MODEL ** -0.5,
        'diff_lambda_q1': 0.1 * nrm(ks[3], (DEPTH, DIFF_HEAD_DIM), f32),
        'diff_lambda_k1': 0.1 * nrm(ks[4], (DEPTH, DIFF_HEAD_DIM), f32),
        'diff_lambda_q2': 0.1 * nrm(ks[5], (DEPTH, DIFF_HEAD_DIM), f32),
        'diff_lambda_k2': 0.1 * nrm(ks[6], (DEPTH, DIFF_HEAD_DIM), f32),
        'diff_subln_gain': 1.0 + 0.02 * nrm(ks[7], (DEPTH, DIFF_V_DIM), f32),
        'gdn_conv_w': nrm(ks[8], (DEPTH, CONV_K, GDN_CONV_WIDTH), f32) * CONV_K ** -0.5,
        'gdn_a_log': jnp.log(jax.random.uniform(ks[10], (DEPTH, GDN_HEADS), f32, 1.0, 16.0)),
        'gdn_dt_bias': dt + jnp.log(-jnp.expm1(-dt)),
        'gdn_norm_gain': 1.0 + 0.02 * nrm(ks[11], (DEPTH, GDN_V_DIM), f32),
        'w_branch_attn': nrm(ks[12], (DEPTH, DIFF_V_WIDTH, D_MODEL), f32) * DIFF_V_WIDTH ** -0.5,
        'w_branch_gdn': nrm(ks[13], (DEPTH, GDN_V_WIDTH, D_MODEL), f32) * GDN_V_WIDTH ** -0.5,
        'w_out': nrm(ks[14], (DEPTH, D_MODEL, D_MODEL), f32) * D_MODEL ** -0.5,
        'norm_ffn_gain': 1.0 + 0.02 * nrm(ks[15], (DEPTH, D_MODEL), f32),
        'moe_w_group': nrm(ks[16], (DEPTH, D_MODEL, MOE_GROUPS), f32) * D_MODEL ** -0.5,
        'moe_b_group': 0.01 * nrm(ks[17], (DEPTH, MOE_GROUPS), f32),
        'moe_w_expert': nrm(ks[18], (DEPTH, D_MODEL, MOE_EXPERTS), f32) * D_MODEL ** -0.5,
        'moe_b_expert': 0.01 * nrm(ks[19], (DEPTH, MOE_EXPERTS), f32),
        'moe_w_gate': nrm(ks[20], (DEPTH, MOE_EXPERTS, D_MODEL, MOE_HIDDEN), f32) * D_MODEL ** -0.5,
        'moe_w_up': nrm(ks[21], (DEPTH, MOE_EXPERTS, D_MODEL, MOE_HIDDEN), f32) * D_MODEL ** -0.5,
        'moe_w_down': nrm(ks[22], (DEPTH, MOE_EXPERTS, MOE_HIDDEN, D_MODEL), f32) * MOE_HIDDEN ** -0.5,
        'norm_final_gain': 1.0 + 0.02 * nrm(ks[23], (D_MODEL,), f32),
    }

def reference(x, norm_mix_gain, w_in, diff_lambda_q1, diff_lambda_k1, diff_lambda_q2, diff_lambda_k2, diff_subln_gain, gdn_conv_w, gdn_a_log, gdn_dt_bias, gdn_norm_gain, w_branch_attn, w_branch_gdn, w_out, norm_ffn_gain, moe_w_group, moe_b_group, moe_w_expert, moe_b_expert, moe_w_gate, moe_w_up, moe_w_down, norm_final_gain):
    b, s, _ = x.shape
    points = [int(p) for p in np.cumsum(IN_SPLITS)[:-1]]
    for layer in range(DEPTH):
        lambda_init = 0.8 - 0.6 * math.exp(-0.3 * layer)
        h = rms_norm(x, norm_mix_gain[layer])
        proj = h @ w_in[layer]
        (dq, dk, dv, gq, gk, gv, g_beta, g_dec, g_gate, m_gate_a, m_gate_b) = jnp.split(proj, points, axis=-1)
        lam = (jnp.exp(jnp.sum(diff_lambda_q1[layer].astype(jnp.float32) * diff_lambda_k1[layer].astype(jnp.float32)))
               - jnp.exp(jnp.sum(diff_lambda_q2[layer].astype(jnp.float32) * diff_lambda_k2[layer].astype(jnp.float32)))
               + lambda_init)
        y_a = diff_attention(dq.reshape(b, s, DIFF_HEADS, 2, DIFF_HEAD_DIM),
                             dk.reshape(b, s, DIFF_HEADS, 2, DIFF_HEAD_DIM),
                             dv.reshape(b, s, DIFF_HEADS, DIFF_V_DIM),
                             lam, diff_subln_gain[layer], lambda_init)
        qkv = jax.nn.silu(causal_depthwise_conv(jnp.concatenate([gq, gk, gv], axis=-1).astype(jnp.float32), gdn_conv_w[layer].astype(jnp.float32)))
        cq, ck, cv = jnp.split(qkv, [GDN_K_WIDTH, 2 * GDN_K_WIDTH], axis=-1)
        beta = jax.nn.sigmoid(g_beta.astype(jnp.float32))
        g_log = -jnp.exp(gdn_a_log[layer].astype(jnp.float32)) * jax.nn.softplus(g_dec.astype(jnp.float32) + gdn_dt_bias[layer].astype(jnp.float32))
        y_b = gated_delta_net(cq.reshape(b, s, GDN_HEADS, GDN_K_DIM), ck.reshape(b, s, GDN_HEADS, GDN_K_DIM),
                              cv.reshape(b, s, GDN_HEADS, GDN_V_DIM), beta, g_log, gdn_norm_gain[layer], g_gate)
        merged = (jax.nn.sigmoid(m_gate_a) * (y_a.astype(x.dtype) @ w_branch_attn[layer])
                  + jax.nn.sigmoid(m_gate_b) * (y_b.astype(x.dtype) @ w_branch_gdn[layer]))
        x = x + merged @ w_out[layer]
        h2 = rms_norm(x, norm_ffn_gain[layer])
        x = x + hier_moe(h2, moe_w_group[layer], moe_b_group[layer], moe_w_expert[layer], moe_b_expert[layer],
                         moe_w_gate[layer], moe_w_up[layer], moe_w_down[layer])
    return rms_norm(x, norm_final_gain)


_drawn_inputs = setup_inputs


def setup_inputs(seed=0):
    import zlib

    import numpy as np

    out = dict(_drawn_inputs(seed))
    spreads = {}
    factors = {'diff_lambda_q2': 200.0,
     'gdn_norm_gain': 33.446,
     'moe_b_group': 52.496,
     'moe_b_expert': 30.164,
     'norm_final_gain': 24.405,
     'diff_lambda_q1': 4.044,
     'diff_lambda_k1': 2.877,
     'diff_subln_gain': 24.293,
     'norm_ffn_gain': 7.967}
    for name, (base, spread) in spreads.items():
        noise = np.random.default_rng([zlib.crc32(name.encode()), seed]).standard_normal(out[name].shape)
        drawn = base * np.exp(spread * noise) if base else spread * noise
        out[name] = __import__('jax').numpy.asarray(drawn.astype(out[name].dtype))
    for name, factor in factors.items():
        out[name] = (out[name] * factor).astype(out[name].dtype)
    return out
```

```python
from contextlib import ExitStack

import concourse.bass as bass
from concourse import mybir

F32 = mybir.dt.float32
I32 = mybir.dt.int32
ALU = mybir.AluOpType
ACT = mybir.ActivationFunctionType
AX_X = mybir.AxisListType.X

P = 128
D = 1024
TOK = 256
NT = TOK // P
KD = D // P
EPS = 1e-6
H = 4
DH = 64
W4 = H * P
CHUNK = 64
TAPS = 4
GROUPS, PER_GROUP = 4, 8
EXPERTS = GROUPS * PER_GROUP
HID = 256
SLOTS = 2 * TOK
NARROW, WIDE = 64, TOK
RING = 4
EXP_F = 3 * D * HID // P
BIG = 1e30
LAMBDA_INIT = 0.2

CHUNKS = [("gk", 2048, 512, "T"), ("gq", 1536, 512, "T"), ("bdg", 3072, 520, "N"), ("gv", 2560, 512, "T"),
          ("dq", 0, 512, "T"), ("dk", 512, 512, "T"), ("dv", 1024, 512, "N"),
          ("ma0", 3592, 512, "T"), ("ma1", 4104, 512, "T"), ("mb0", 4616, 512, "T"), ("mb1", 5128, 512, "T")]
NCH = len(CHUNKS)
CI = {c[0]: i for i, c in enumerate(CHUNKS)}
PARTS = [4 if c[3] == "T" else 2 for c in CHUNKS]

LEVELS = 5
SIDE = [("consts", 1), ("bd", 1), ("ss", 1), ("rnk", 1), ("rnq", 1), ("gsum", 1), ("grow", 1), ("gram", 1),
        ("intra", 1), ("ktok", 1), ("vtok", 1), ("b1", 1)]
for _l in range(1, LEVELS + 1):
    SIDE += [(f"Y{_l}", 1), (f"TT{_l}", 1)] + ([(f"T{_l}", 1)] if _l < LEVELS else [])
SIDE += [("u", 1), ("wT", 1), ("s00", 1), ("s01", 1), ("so0", 1), ("aT0", 1), ("ws1", 1), ("oa0", 1), ("so1", 1),
         ("s10", 1), ("s11", 1), ("ws2", 1), ("so2", 1), ("aT1", 1), ("ws3", 1), ("oa1", 1), ("so3", 1),
         ("yaT", 1), ("ybT", 1)]
SI = {n: i for i, (n, _) in enumerate(SIDE)}


def side_pair(name):
    return SI[name] % 2


def side_reuse(name):
    i = SI[name]
    return sum(c for j, (_, c) in enumerate(SIDE[:i]) if j % 2 == i % 2)


def parts_before(i):
    return sum(PARTS[:i])


class Core:
    pass


def lay_out(nc, ctx):
    c = Core()
    stage_f = KD * 520
    names = {}

    def sb(name, shape, dt=F32):
        return ctx.enter_context(nc.sbuf_tensor(name, shape, dt))

    ring = sb("ring", [P, RING - 1, EXP_F])
    sizes = [("x", 2048), ("hT", 2048), ("stage0", stage_f), ("stage1", stage_f),
             ("qT", 1024), ("kT", 1024), ("dv", 1024), ("ck", 1024), ("cv", 1024), ("wrhs", 1024), ("vb", 1024),
             ("cq", 1024), ("kdec", 1024), ("F", 1024), ("gate", 1024), ("S", 512), ("vn", 1024),
             ("A", 1024), ("T", 1024), ("TT", 1024), ("Yb", 1024), ("attnT", 1024), ("EwT", 1024)]
    total = sum(n for _, n in sizes)
    arena = sb("arena", [P, total])
    off = 0
    for n, size in sizes:
        names[n] = off
        off += size

    def at(name, size, extra=0):
        return arena[:, names[name] + extra:names[name] + extra + size]

    c.ring = [ring[:, i, :] for i in range(RING - 1)] + [at("A", EXP_F)]
    c.gate_w = [r[:, 0:2048].rearrange("p (k f) -> p k f", k=KD) for r in c.ring]
    c.up_w = [r[:, 2048:4096].rearrange("p (k f) -> p k f", k=KD) for r in c.ring]
    c.down_w = [r[:, 4096:6144].rearrange("p (k d) -> p k d", k=2) for r in c.ring]
    c.gate_flat = [r[:, 0:2048] for r in c.ring]
    c.up_flat = [r[:, 2048:4096] for r in c.ring]
    c.down_flat = [r[:, 4096:6144] for r in c.ring]

    def v3(ap, a):
        return ap.rearrange("p (a b) -> p a b", a=a)

    c.x = v3(at("x", 2048), NT)
    c.h = v3(at("A", 2048), NT)
    c.hT = v3(at("hT", 2048), KD)
    c.stage = [at("stage0", stage_f), at("stage1", stage_f)]
    c.qT, c.kT = v3(at("qT", 1024), H), v3(at("kT", 1024), H)
    c.dv = v3(at("dv", 1024), NT)
    c.cq, c.ck, c.cv = (v3(at(n, 1024), H) for n in ("cq", "ck", "cv"))
    c.sig = {"gk": v3(at("F", 1024), H), "gq": v3(at("TT", 1024), H), "gv": v3(at("Yb", 1024), H)}
    c.sqk, c.sqq = v3(at("A", 1024), H), v3(at("T", 1024), H)
    c.gate = v3(at("gate", 1024), NT)

    def prob(name):
        return at(name, 1024).rearrange("p (t h f) -> p t h f", t=NT, h=H)
    c.A, c.T, c.TT, c.Yb, c.attnT, c.E, c.wT = (prob(n) for n in ("A", "T", "TT", "Yb", "attnT", "EwT", "EwT"))
    c.Dm = c.T
    c.wrhs, c.vb, c.kdec, c.qdec, c.u = (prob(n) for n in ("wrhs", "vb", "kdec", "cq", "cv"))
    c.flat = {n: at(n, 1024) for n in ("A", "T", "TT", "Yb", "attnT", "EwT", "wrhs", "vb", "kdec", "cq", "ck", "cv",
                                       "F", "gate", "qT", "kT", "dv")}
    c.S = v3(at("S", 512), H)
    c.vn = [v3(at("vn", 512, 512 * i), H) for i in range(2)]
    c.ob = v3(at("TT", 1024), NT)
    c.oa = v3(at("F", 1024), NT)
    c.es = v3(at("A", 2048), 2 * H)
    c.aT = at("Yb", 1024)
    c.yaT, c.ybT = v3(at("qT", 1024), H), v3(at("kT", 1024), H)
    c.tmp = at("wrhs", 1024)
    c.mg = [at(n, 1024) for n in ("ck", "vb", "wrhs", "gate")]

    c.h2 = v3(at("hT", 2048), NT)
    base2 = names["stage0"]

    def at2(off2, size):
        return arena[:, base2 + off2:base2 + off2 + size]
    pad = SLOTS + WIDE
    o2 = 0
    c.h2T = v3(at2(o2, 2048), KD)
    c.Ys = v3(ring[:, 1, 0:4096], SLOTS // P)
    c.ST = v3(ring[:, 0, 0:1024], SLOTS // P)
    o2 += 2048
    c.onehot = v3(at2(o2, 1024), NT)
    o2 += 1024
    c.HgT = at2(o2, KD * pad).rearrange("p (k s) -> p k s", k=KD)
    o2 += KD * pad
    c.YT = at2(o2, KD * pad).rearrange("p (k s) -> p k s", k=KD)
    o2 += KD * pad
    c.comb = v3(at2(o2, 1024), NT)
    o2 += 1024
    c.r = at2(o2, 520)
    o2 += 520
    c.iota = at2(o2, SLOTS)
    o2 += SLOTS
    assert base2 + o2 <= names["F"], (base2 + o2, names["F"])
    c.gffn = at("F", 1024)
    c.gfin = at("gate", 1024)
    c.y = v3(at("hT", 2048), NT)
    c.window = [at("hT", 2048), at2(0, 2048)]
    c.act = [at("S", 512), at("vn", 512)]
    c.sg = [at("vn", 512, 512), at("F", 512)]

    m = sb("masks", [P, 14, P])
    c.ident, c.upper, c.lower, c.chunk, c.half0, c.half1, c.ones, c.m1 = (m[:, i, :] for i in range(8))
    c.levelT = [m[:, 8 + i, :] for i in range(LEVELS)]
    c.before = m[:, 13, :]
    c.masks = m
    c.small = sb("small", [P, 448])
    so = [0]

    def sm(n):
        so[0] += n
        assert so[0] <= 448
        return c.small[:, so[0] - n:so[0]]
    c.cst_in = sb("cst_in", [56, P])
    c.cst = sm(56)
    c.ssx, c.rx = sm(2), sm(2)
    c.alog, c.dtb, c.nea = sm(4), sm(4), sm(4)
    c.beta, c.z, c.zm, c.sp, c.g = (sm(8) for _ in range(5))
    c.rn = sm(16)
    c.run_sum, c.chunk_sum, c.bexp = sm(8), sm(8), sm(8)
    c.GL = sm(16)
    c.sums_exp = sm(32)
    c.sums_in = sm(32)
    c.negmax, c.esum, c.coef = sm(16), sm(16), sm(16)
    c.lam = sm(4)
    c.lamw = sm(2)
    c.ss8, c.rb = sm(8), sm(8)
    c.ra = sm(8)
    c.rbias = sm(36)
    c.lamrows = sb("lamrows", [P, 4, DH])
    c.subln, c.gdng = sb("subln", [P, P]), sb("gdng", [P, P])
    c.rw = sb("rw", [P, KD, GROUPS + EXPERTS])
    c.offs = sb("offs", [1, EXPERTS + 1], I32)
    c.ps = ctx.enter_context(nc.psum_tensor("ps", [P, 8, 512], F32))

    c.side = [c.ps[:, 4:6, :].rearrange("p b f -> p (b f)"), c.ps[:, 6:8, :].rearrange("p b f -> p (b f)")]
    c.pair = [c.ps[:, 0:2, :].rearrange("p b f -> p (b f)"), c.ps[:, 2:4, :].rearrange("p b f -> p (b f)")]

    def sem(name):
        return ctx.enter_context(nc.semaphore(name))
    for_names = """x_loaded consts_loaded vectors_loaded lambda_loaded router_loaded gffn_loaded gfin_loaded out_stored
        ident_ready masks_ready iota_ready squares_ready
        ssx_ready rx_root h_ready h_transposed hT_ready cst_ready
        stage_used proj_ready side_ready
        conv_ready conv_sig qkv_ready gate_sig gate_ready beta_ready dec_exp g_in g_ready rn_root rn_ready
        q_normed k_normed gsum_ready gsum_exp g_scaled grow_pre grow_exp qdec_ready a_ready attnT_ready
        tok_ready b1_ready Y_ready TT_ready T_ready u_ready wT_ready
        dq_ready dk_ready dv_ready mg_ready
        negmax_ready exps_ready lam_in lam_exp aT_in aT_ready oa_out oa_squares oa_root ya_ready yaT_ready
        S_ready vn_ready ob_out ob_squares ob_root yb_ready ybT_ready
        branch_ready branch_used merged_ready mix_out x1_ready ss1_ready r1_root h2_ready h2_transposed h2T_ready
        logits_ready gexp_in gexp_out texp_in texp_out picks_ready ranks_ready offsets_ready onehot_ready comb_ready
        gathered HgT_ready
        window_ready up_ready gate_sigmoid act_ready gu_free down_ready y_free experts_used
        yT_turned Ys_ready comb_turned ST_ready y_ready ss2_in ss2_ready r2_root out_ready
        dve_chain act_chain pool_chain side_free0 side_free1 pair_free0 pair_free1 stage_loaded0 stage_loaded1""".split()
    c.s = {n: sem(n) for n in for_names}
    for i in range(RING):
        c.s[f"gateup{i}"] = sem(f"gateup{i}")
        c.s[f"down{i}"] = sem(f"down{i}")
    return c


def sync_program(sp, c, io):
    s = c.s
    sp.dma_start(c.x, io["x"].rearrange("b (t p) d -> p (b t) d", p=P)).then_inc(s["x_loaded"], 16)
    w_in = io["w_in"][0].rearrange("(k p) n -> p k n", p=P)

    def stage_free(i):
        if i >= 2:
            sp.wait_ge(s["stage_used"], i - 1)

    def load_chunk(i):
        _, col, n, _ = CHUNKS[i]
        stage_free(i)
        sp.dma_start(c.stage[i % 2][:, 0:KD * n].rearrange("p (k n) -> p k n", k=KD),
                     w_in[:, :, col:col + n]).then_inc(s[f"stage_loaded{i % 2}"], 16)

    def load_expert(e):
        slot = e % RING
        for flat, name, sem in ((c.gate_flat, "moe_w_gate", "gateup"), (c.up_flat, "moe_w_up", "gateup"),
                                (c.down_flat, "moe_w_down", "down")):
            k = 2 if name == "moe_w_down" else KD
            sp.dma_start(flat[slot], io[name][0, e].rearrange("(p k) f -> p (k f)", k=k)).then_inc(s[f"{sem}{slot}"], 16)

    for i in range(4):
        load_chunk(i)
    load_expert(0)
    load_chunk(4)
    load_expert(1)
    load_chunk(5)
    load_expert(2)
    for i in range(6, NCH):
        load_chunk(i)
    for j, name in enumerate(("w_branch_attn", "w_branch_gdn")):
        i = NCH + j
        stage_free(i)
        sp.dma_start(c.stage[i % 2][:, 0:4096].rearrange("p (k n) -> p k n", k=H),
                     io[name][0].rearrange("(k p) n -> p k n", p=P)).then_inc(s[f"stage_loaded{i % 2}"], 16)
    for j in range(2):
        i = NCH + 2 + j
        stage_free(i)
        sp.dma_start(c.stage[i % 2][:, 0:4096].rearrange("p (k n) -> p k n", k=KD),
                     io["w_out"][0].rearrange("(k p) n -> p k n", p=P)[:, :, j * 512:(j + 1) * 512])\
            .then_inc(s[f"stage_loaded{i % 2}"], 16)
    sp.wait_ge(s["ybT_ready"], 1)
    sp.wait_ge(s["side_ready"], len(SIDE))
    sp.wait_ge(s["yaT_ready"], 1)
    sp.dma_start(c.gffn, io["norm_ffn_gain"][0:1, :].partition_broadcast(P).rearrange("p a d -> p (a d)"))\
        .then_inc(s["gffn_loaded"], 16)
    load_expert(3)
    gate_d = io["moe_w_gate"][0].rearrange("e (p k) f -> p e (k f)", k=KD)
    up_d = io["moe_w_up"][0].rearrange("e (p k) f -> p e (k f)", k=KD)
    down_d = io["moe_w_down"][0].rearrange("e (p k) d -> p e (k d)", k=2)
    with sp.Fori(0, EXPERTS // RING - 1) as it:
        for j in range(RING):
            sp.wait_ge(s["experts_used"], it * RING + (j + 1))
            e = it * RING + (RING + j)
            for flat, src, sem in ((c.gate_flat, gate_d, "gateup"), (c.up_flat, up_d, "gateup"),
                                   (c.down_flat, down_d, "down")):
                sp.dma_start(flat[j], src[:, bass.ds(e, 1), :].rearrange("p a f -> p (a f)")).then_inc(s[f"{sem}{j}"], 16)
    outv = io["out"].rearrange("b (t p) d -> p (b t) d", p=P)
    for t in range(NT):
        sp.wait_ge(s["out_ready"], t + 1)
        sp.dma_start(outv[:, t, :], c.y[:, t, :]).then_inc(s["out_stored"], 16)
    sp.wait_ge(s["out_stored"], 16 * NT)


def gpsimd_program(pool, c, io):
    s = c.s
    n = [0]

    def settle(ins):
        n[0] += 1
        ins.then_inc(s["pool_chain"], 1)
        pool.wait_ge(s["pool_chain"], n[0])
    settle(pool.memset(c.masks[:, :, :], 0.0))
    pool.affine_select(out=c.ident, in_=c.ident, compare_op=ALU.not_equal, fill=1.0, base=0,
                       pattern=[[-1, P]], channel_multiplier=1).then_inc(s["ident_ready"], 1)
    odd = c.m1.rearrange("p (a b) -> p a b", b=2)[:, :, 0]
    settle(pool.affine_select(out=odd, in_=odd, compare_op=ALU.not_equal, fill=1.0, base=-1,
                              pattern=[[-2, P // 2]], channel_multiplier=1))
    for v in (c.upper, c.lower, c.chunk, c.half0, c.half1, c.ones, c.before):
        pool.memset(v, 1.0)
    tops = []
    for lv in range(LEVELS):
        w = 2 << lv
        top = c.levelT[lv].rearrange("p (a b f) -> p a b f", b=2, f=w)[:, :, 1, :]
        pool.memset(top, 1.0)
        tops.append((top, w))
    settle(pool.memset(c.vn[0], 0.0))
    settle(pool.memset(c.vn[1], 0.0))

    def keep(v, pattern, base, mult):
        return pool.affine_select(out=v, in_=v, compare_op=ALU.is_ge, fill=0.0, base=base, pattern=pattern,
                                  channel_multiplier=mult)
    nc2 = P // CHUNK
    for v in (c.upper, c.lower, c.chunk):
        keep(v.rearrange("p (a f) -> p a f", a=nc2), [[-CHUNK, nc2], [0, CHUNK]], 0, 1)
    for top, w in tops:
        keep(top, [[-2 * w, P // (2 * w)], [0, w]], 0, 1)
    keep(c.half0, [[0, P]], CHUNK - 1, -1)
    keep(c.half1, [[0, P]], -CHUNK, 1)
    settle(keep(c.before, [[1, P]], -1, -1))
    for v in (c.upper, c.lower, c.chunk):
        keep(v.rearrange("p (a f) -> p a f", a=nc2), [[CHUNK, nc2], [0, CHUNK]], CHUNK - 1, -1)
    for top, w in tops:
        last = keep(top, [[2 * w, P // (2 * w)], [0, w]], w - 1, -1)
    settle(last)
    keep(c.upper, [[1, P]], 0, -1)
    keep(c.lower, [[-1, P]], -1, 1).then_inc(s["masks_ready"], 1)
    pool.wait_ge(s["h_transposed"], 1)
    for i, (src, dst) in enumerate(((c.ck, c.sqk), (c.cq, c.sqq))):
        pool.wait_ge(s["qkv_ready"], i + 1)
        pool.tensor_tensor(dst, src, src, ALU.mult).then_inc(s["squares_ready"], 1)
    pool.wait_ge(s["merged_ready"], 2)
    pool.iota(c.iota[:, :], [[1, SLOTS]], base=0, channel_multiplier=0,
              allow_small_or_imprecise_dtypes=True).then_inc(s["iota_ready"], 1)


def scalar_program(act, c, io):
    s = c.s
    n = [0]

    def chain(ins):
        n[0] += 1
        ins.then_inc(s["act_chain"], 1)

    def settle():
        act.wait_ge(s["act_chain"], n[0])

    act.dma_start(c.cst_in[0:8, :], io["norm_mix_gain"][0].rearrange("(k p) -> k p", p=P)).then_inc(s["consts_loaded"], 16)
    act.dma_start(c.cst_in[8:56, :], io["gdn_conv_w"][0].rearrange("j (b p) -> (j b) p", p=P)).then_inc(s["consts_loaded"], 16)

    def row(dst, src, sem):
        act.dma_start(dst, src.partition_broadcast(P).rearrange("p a d -> p (a d)")).then_inc(s[sem], 16)
    row(c.alog, io["gdn_a_log"][0:1, :], "vectors_loaded")
    row(c.dtb, io["gdn_dt_bias"][0:1, :], "vectors_loaded")
    row(c.subln[:, :], io["diff_subln_gain"][0:1, :], "vectors_loaded")
    row(c.gdng[:, :], io["gdn_norm_gain"][0:1, :], "vectors_loaded")
    for i, nm in enumerate(("q1", "k1", "q2", "k2")):
        row(c.lamrows[:, i, :], io[f"diff_lambda_{nm}"][0:1, :], "lambda_loaded")
    row(c.rbias[:, 0:GROUPS], io["moe_b_group"][0:1, :], "router_loaded")
    row(c.rbias[:, GROUPS:], io["moe_b_expert"][0:1, :], "router_loaded")
    act.dma_start(c.rw[:, :, 0:GROUPS], io["moe_w_group"][0].rearrange("(k p) g -> p k g", p=P)).then_inc(s["router_loaded"], 16)
    act.dma_start(c.rw[:, :, GROUPS:], io["moe_w_expert"][0].rearrange("(k p) g -> p k g", p=P)).then_inc(s["router_loaded"], 16)

    act.wait_ge(s["x_loaded"], 16)
    for t in range(NT):
        act.activation(c.hT[:, 0:4, :] if t == 0 else c.hT[:, 4:8, :], c.x[:, t, :].rearrange("p (a b) -> p a b", a=4),
                       ACT.Square, accum_out=c.ssx[:, t:t + 1]).then_inc(s["ssx_ready"], 1)
    act.wait_ge(s["ss2_in"], 1)
    act.activation(c.rx, c.ssx, ACT.Sqrt).then_inc(s["rx_root"], 1)
    act.wait_ge(s["cst_ready"], 1)
    act.wait_ge(s["h_transposed"], 1)
    act.wait_ge(s["ssx_ready"], NT)
    for k in (2, 3, 6, 7):
        act.activation(c.hT[:, k, :], c.ps[:, k // 2, (k % 2) * 256:(k % 2 + 1) * 256], ACT.Copy, scale=c.cst[:, k:k + 1]).then_inc(s["hT_ready"], 1)

    def conv_sigmoid(i, name, src):
        act.wait_ge(s["conv_ready"], i + 1)
        act.activation(c.sig[name], src, ACT.Sigmoid).then_inc(s["conv_sig"], 1)
    conv_sigmoid(0, "gk", c.ck)
    conv_sigmoid(1, "gq", c.cq)
    i = CI["bdg"]
    act.wait_ge(s["proj_ready"], parts_before(i) + PARTS[i])
    act.activation(c.flat["gate"], c.pair[i % 2], ACT.Sigmoid).then_inc(s["gate_sig"], 1)
    act.wait_ge(s["side_ready"], SI["bd"] + 1)
    bd = c.side[side_pair("bd")][:, 0:16].rearrange("p (t a h) -> p t a h", t=NT, a=2)
    act.activation(c.beta.rearrange("p (t h) -> p t h", t=NT), bd[:, :, 0, :], ACT.Sigmoid).then_inc(s["beta_ready"], 1)
    act.wait_ge(s["rn_root"], 1)
    act.activation(c.rn, c.rn, ACT.Sqrt).then_inc(s["rn_root"], 1)
    act.wait_ge(s["g_in"], 1)
    act.activation(c.z, c.z, ACT.Exp).then_inc(s["dec_exp"], 1)
    act.wait_ge(s["vectors_loaded"], 64)
    act.activation(c.nea, c.alog, ACT.Exp).then_inc(s["dec_exp"], 1)
    act.wait_ge(s["dec_exp"], 2)
    act.activation(c.z, c.z, ACT.Ln, bias=1.0).then_inc(s["dec_exp"], 1)
    act.wait_ge(s["lam_in"], 1)
    act.activation(c.lam[:, 2:4], c.lam[:, 0:2], ACT.Exp).then_inc(s["lam_exp"], 1)
    conv_sigmoid(2, "gv", c.cv)
    act.wait_ge(s["gsum_ready"], 1)
    act.activation(c.sums_exp, c.sums_in, ACT.Exp).then_inc(s["gsum_exp"], 1)
    act.wait_ge(s["grow_pre"], 2)
    act.activation(c.flat["EwT"], c.side[side_pair("grow")], ACT.Exp).then_inc(s[f"side_free{side_pair('grow')}"], 1)
    act.wait_ge(s["grow_pre"], 1)
    act.activation(c.flat["T"], c.flat["T"], ACT.Exp, scale=-1.0).then_inc(s["grow_exp"], 1)
    act.wait_ge(s["grow_pre"], 2)
    act.activation(c.flat["attnT"], c.flat["attnT"], ACT.Exp).then_inc(s["grow_exp"], 1)

    def evacuate(name, dst, sem, func):
        i = CI[name]
        act.wait_ge(s["proj_ready"], parts_before(i) + PARTS[i])
        act.activation(dst, c.pair[i % 2], func).then_inc(s[sem], 1)
        act.wait_ge(s[sem], {"dq_ready": 1, "dk_ready": 1, "dv_ready": 1}.get(sem, 0) or [None, "ma0", "ma1", "mb0", "mb1"].index(name))
        act.sem_inc(s[f"pair_free{i % 2}"], 1)
    evacuate("dq", c.flat["qT"], "dq_ready", ACT.Copy)
    evacuate("dk", c.flat["kT"], "dk_ready", ACT.Copy)
    evacuate("dv", c.flat["dv"], "dv_ready", ACT.Copy)
    evacuate("ma0", c.mg[0], "mg_ready", ACT.Sigmoid)

    def exps(qt):
        nk = P * (qt + 1)
        for m in range(2):
            act.wait_ge(s["negmax_ready"], 2 * qt + m + 1)
            pair = c.side[side_pair(f"s{qt}{m}")].rearrange("p (h k) -> p h k", h=H)
            for h in range(H):
                j = m * H + h
                ins = act.activation(c.es[:, j, 0:nk], pair[:, h, 0:nk], ACT.Exp, bias=c.negmax[:, 8 * qt + j:8 * qt + j + 1],
                                     scale=DH ** -0.5, accum_out=c.esum[:, 8 * qt + j:8 * qt + j + 1])
                ins.then_inc(s["exps_ready"], 1)
            act.wait_ge(s["exps_ready"], H * (2 * qt + m + 1))
            act.sem_inc(s[f"side_free{side_pair(f's{qt}{m}')}"], 1)
    act.wait_ge(s["TT_ready"], LEVELS + 1)
    exps(0)
    act.wait_ge(s["side_ready"], SI["wT"] + 1)
    evacuate("ma1", c.mg[1], "mg_ready", ACT.Sigmoid)
    act.wait_ge(s["aT_in"], 1)
    act.wait_ge(s["side_ready"], SI["aT0"] + 1)
    exps(1)
    evacuate("mb0", c.mg[2], "mg_ready", ACT.Sigmoid)

    def squares_root(src, sq, ss, ready, out_sem, root, rt):
        act.wait_ge(s[ready], 1)
        act.activation(sq, src, ACT.Square).then_inc(s[out_sem], 1)
        act.wait_ge(s[root], 1)
        act.activation(rt, ss, ACT.Sqrt).then_inc(s[root], 1)
    act.wait_ge(s["oa_out"], NT)
    act.activation(c.flat["Yb"], c.flat["F"], ACT.Square).then_inc(s["oa_squares"], 1)
    act.wait_ge(s["oa_root"], 1)
    act.activation(c.ra, c.ra, ACT.Sqrt).then_inc(s["oa_root"], 1)
    act.wait_ge(s["gate_ready"], 2)
    act.wait_ge(s["ob_out"], 4)
    act.activation(c.flat["A"], c.flat["TT"], ACT.Square).then_inc(s["ob_squares"], 1)
    act.wait_ge(s["ob_root"], 1)
    act.activation(c.rb, c.rb, ACT.Sqrt).then_inc(s["ob_root"], 1)
    act.wait_ge(s["yb_ready"], 1)
    evacuate("mb1", c.mg[3], "mg_ready", ACT.Sigmoid)
    act.wait_ge(s["side_ready"], SI["ybT"] + 1)
    act.activation(c.flat["kT"], c.side[side_pair("ybT")], ACT.Copy).then_inc(s["ybT_ready"], 1)

    for t in range(NT):
        act.wait_ge(s["x1_ready"], t + 1)
        act.activation(c.flat[("qT", "kT")[t]], c.x[:, t, :], ACT.Square, accum_out=c.ssx[:, t:t + 1])\
            .then_inc(s["ss1_ready"], 1)
    act.wait_ge(s["r1_root"], 1)
    act.activation(c.rx, c.ssx, ACT.Sqrt).then_inc(s["r1_root"], 1)
    act.wait_ge(s["ss1_ready"], 2)
    act.wait_ge(s["h2_transposed"], 1)
    for b in (1, 3):
        act.activation(c.h2T[:, 2 * b:2 * b + 2, :].rearrange("p a b -> p (a b)"), c.ps[:, 4 + b, :], ACT.Copy).then_inc(s["h2T_ready"], 1)
    act.wait_ge(s["gexp_in"], 1)
    act.activation(c.r[:, 72:80], c.r[:, 72:80], ACT.Exp).then_inc(s["gexp_out"], 1)
    act.wait_ge(s["texp_in"], 1)
    act.activation(c.r[:, 144:146], c.r[:, 144:146], ACT.Exp).then_inc(s["texp_out"], 1)
    for k in range(1, KD, 2):
        act.wait_ge(s["gathered"], k + 1)
        act.activation(c.HgT[:, k, 0:SLOTS], c.ps[:, k, :], ACT.Copy).then_inc(s["HgT_ready"], 1)

    act.wait_ge(s["offsets_ready"], 1)
    act.wait_ge(s["HgT_ready"], KD + 1)
    wide = act.value_load(c.offs[0:1, EXPERTS:EXPERTS + 1], min_val=0, max_val=TOK)

    def windows(w):
        def copy_window(n, buf):
            off = act.value_load(c.offs[0:1, n], min_val=0, max_val=SLOTS)
            act.activation(c.window[buf][:, 0:KD * w].rearrange("p (k s) -> p k s", k=KD), c.HgT[:, :, bass.ds(off, w)],
                           ACT.Copy).then_inc(s["window_ready"], 1)
        copy_window(slice(0, 1), 0)
        with act.Fori(0, EXPERTS // RING) as it:
            for j in range(RING):
                act.wait_ge(s["up_ready"], it * RING + (j + 1))
                act.wait_ge(s["act_ready"], it * RING + (j + 1))
                act.activation(c.sg[j % 2][:, 0:2 * w], gate_up(c, j, w)[:, 0:2 * w], ACT.Sigmoid).then_inc(s["gate_sigmoid"], 1)
                copy_window(bass.ds(it * RING + (j + 1), 1), (j + 1) % 2)
    with act.If(wide <= NARROW):
        windows(NARROW)
    with act.Else():
        windows(WIDE)

    for m in range(1, SLOTS // P * 2, 2):
        act.wait_ge(s["yT_turned"], m + 1)
        act.activation(c.Ys[:, m // 2, 512:1024], c.ps[:, m, :], ACT.Copy).then_inc(s["Ys_ready"], 1)
    for t in range(NT):
        act.wait_ge(s["ss2_in"], t + 2)
        act.activation(c.YT[:, 0:2, 0:512] if t == 0 else c.YT[:, 2:4, 0:512],
                       c.x[:, t, :].rearrange("p (a b) -> p a b", a=2), ACT.Square, accum_out=c.ssx[:, t:t + 1])\
            .then_inc(s["ss2_ready"], 1)
        act.wait_ge(s["r2_root"], 2 * t + 1)
        act.activation(c.rx[:, t:t + 1], c.ssx[:, t:t + 1], ACT.Sqrt).then_inc(s["r2_root"], 1)


def gate_up(c, j, w):
    return c.pair[j % 2][:, 0:4 * w]


def tensor_program(pe, c, io):
    s = c.s
    T4 = [(t, h) for t in range(NT) for h in range(H)]

    def side(name):
        v = side_reuse(name)
        if v:
            pe.wait_ge(s[f"side_free{side_pair(name)}"], v)
        return c.side[side_pair(name)]

    def blk(ap, i, n=P):
        return ap[:, i * n:(i + 1) * n]

    pe.wait_ge(s["ident_ready"], 1)
    pe.wait_ge(s["consts_loaded"], 32)
    ps = side("consts")
    pe.transpose(ps[:, 0:56], c.cst_in[:, :], c.ident[0:56, 0:56]).then_inc(s["side_ready"], 1)
    for t in range(NT):
        pe.wait_ge(s["h_ready"], t + 1)
        for k in range(KD):
            last = pe.transpose(c.ps[:, k // 2, (k % 2) * 256 + t * P:(k % 2) * 256 + (t + 1) * P],
                                c.h[:, t, k * P:(k + 1) * P], c.ident)
    last.then_inc(s["h_transposed"], 1)

    def project(name, part):
        i = CI[name]
        _, _, n, kind = CHUNKS[i]
        w = c.stage[i % 2][:, 0:KD * n].rearrange("p (k n) -> p k n", k=KD)
        if part == 0:
            pe.wait_ge(s[f"stage_loaded{i % 2}"], 16 * (i // 2 + 1))
            if i >= 2:
                pe.wait_ge(s[f"pair_free{i % 2}"], i // 2)
        for k in range(KD):
            if kind == "T":
                out, lhs, rhs = blk(c.pair[i % 2], part, TOK), w[:, k, part * P:(part + 1) * P], c.hT[:, k, :]
            else:
                out, lhs, rhs = blk(c.pair[i % 2], part, 512), c.hT[:, k, part * P:(part + 1) * P], w[:, k, n - 512:n]
            last = pe.matmul(out, lhs, rhs, start=(k == 0), stop=(k == KD - 1))
        last.then_inc(s["proj_ready"], 1)
        if part == PARTS[i] - 1 and name != "bdg":
            pe.wait_ge(s["proj_ready"], parts_before(i) + PARTS[i])
            pe.sem_inc(s["stage_used"], 1)

    def turn(name, src):
        ps = side(name)
        for i in range(8):
            last = pe.transpose(blk(ps, i), src(i), c.ident)
        last.then_inc(s["side_ready"], 1)

    def each(name, lhs, rhs):
        ps = side(name)
        for i, (t, h) in enumerate(T4):
            last = pe.matmul(blk(ps, i), lhs(t, h), rhs(t, h), start=True, stop=True)
        last.then_inc(s["side_ready"], 1)

    def tile(ap, h, t):
        return ap[:, h, t * P:(t + 1) * P]

    pe.wait_ge(s["hT_ready"], KD)
    for name in ("gk", "gq"):
        for b in range(4):
            project(name, b)
    project("bdg", 0)
    project("bdg", 1)
    i = CI["bdg"]
    wbd = c.stage[i % 2][:, 0:KD * 520].rearrange("p (k n) -> p k n", k=KD)
    ps = side("bd")
    for t in range(NT):
        for k in range(KD):
            last = pe.matmul(ps[:, 8 * t:8 * t + 8], c.hT[:, k, t * P:(t + 1) * P], wbd[:, k, 0:8],
                             start=(k == 0), stop=(k == KD - 1))
    last.then_inc(s["side_ready"], 1)
    pe.wait_ge(s["side_ready"], SI["bd"] + 1)
    pe.sem_inc(s["stage_used"], 1)
    project("gv", 0)
    project("gv", 1)
    ps = side("ss")
    pe.wait_ge(s["masks_ready"], 1)
    for j, sq in enumerate((c.sqk, c.sqq)):
        pe.wait_ge(s["squares_ready"], j + 1)
        for i, (t, h) in enumerate(T4):
            last = pe.matmul(ps[:, 8 * j + i:8 * j + i + 1], tile(sq, h, t), c.ones[:, 0:1], start=True, stop=True)
    last.then_inc(s["side_ready"], 1)
    project("gv", 2)
    pe.wait_ge(s["rn_ready"], 1)
    for j, name in enumerate(("rnk", "rnq")):
        each(name, lambda t, h, j=j: c.rn[:, 8 * j + 4 * t + h:8 * j + 4 * t + h + 1].to_broadcast([P, P]), lambda t, h: c.ident)
    project("gv", 3)
    ps = side("gsum")
    pe.wait_ge(s["g_ready"], 1)
    for t in range(NT):
        g = c.g[:, 4 * t:4 * t + 4]
        pe.matmul(ps[:, 4 * t:4 * t + 4], c.upper, g, start=True, stop=True)
        pe.matmul(ps[:, 8 + 4 * t:12 + 4 * t], c.chunk, g, start=True, stop=True)
        pe.matmul(ps[:, 16 + 8 * t:20 + 8 * t], c.half0, g, start=True, stop=True)
        last = pe.matmul(ps[:, 20 + 8 * t:24 + 8 * t], c.half1, g, start=True, stop=True)
    last.then_inc(s["side_ready"], 1)
    each("grow", lambda t, h: c.g[:, 4 * t + h:4 * t + h + 1].to_broadcast([P, P]), lambda t, h: c.upper)
    project("dq", 0)
    pe.wait_ge(s["k_normed"], 1)
    each("gram", lambda t, h: tile(c.ck, h, t), lambda t, h: tile(c.ck, h, t))
    project("dq", 1)
    pe.wait_ge(s["q_normed"], 1)
    each("intra", lambda t, h: tile(c.ck, h, t), lambda t, h: tile(c.cq, h, t))
    project("dq", 2)
    turn("ktok", lambda i: tile(c.ck, i % 4, i // 4))
    project("dq", 3)
    pe.wait_ge(s["qkv_ready"], 3)
    turn("vtok", lambda i: tile(c.cv, i % 4, i // 4))
    project("dk", 0)
    pe.wait_ge(s["b1_ready"], 1)
    turn("b1", lambda i: c.Yb[:, i // 4, i % 4, :])
    project("dk", 1)

    def level_y(lv):
        pe.wait_ge(s["TT_ready"], lv)
        each(f"Y{lv}", lambda t, h: c.A[:, t, h, :], lambda t, h: c.TT[:, t, h, :])

    def level_t(lv):
        pe.wait_ge(s["Y_ready"], lv)
        pe.wait_ge(s["T_ready"], lv)
        each(f"TT{lv}", lambda t, h: c.T[:, t, h, :], lambda t, h: c.Yb[:, t, h, :])
        if lv < LEVELS:
            each(f"T{lv}", lambda t, h: c.Yb[:, t, h, :], lambda t, h: c.T[:, t, h, :])
    level_y(1)
    project("dk", 2)
    level_t(1)
    project("dk", 3)
    level_y(2)
    project("dv", 0)
    level_t(2)
    project("dv", 1)
    level_y(3)
    project("ma0", 0)
    level_t(3)
    project("ma0", 1)
    level_y(4)
    project("ma0", 2)
    level_t(4)
    project("ma0", 3)
    level_y(5)
    project("ma1", 0)
    level_t(5)
    project("ma1", 1)
    pe.wait_ge(s["TT_ready"], LEVELS + 1)
    pe.wait_ge(s["tok_ready"], 3)
    each("u", lambda t, h: c.TT[:, t, h, :], lambda t, h: c.vb[:, t, h, :])
    each("wT", lambda t, h: c.wrhs[:, t, h, :], lambda t, h: c.TT[:, t, h, :])

    def scores(qt):
        pe.wait_ge(s["dq_ready"], 1)
        pe.wait_ge(s["dk_ready"], 1)
        for m in range(2):
            ps = side(f"s{qt}{m}").rearrange("p (h k) -> p h k", h=H)
            rows = slice(DH * m, DH * (m + 1))
            for h in range(H):
                last = pe.matmul(ps[:, h, 0:P * (qt + 1)], c.qT[rows, h, qt * P:(qt + 1) * P],
                                 c.kT[rows, h, 0:P * (qt + 1)], start=True, stop=True)
            last.then_inc(s["side_ready"], 1)

    def turn_probs(qt):
        ps = side(f"aT{qt}")
        pe.wait_ge(s["aT_in"], qt + 1)
        for h in range(H):
            for kt in range(qt + 1):
                last = pe.transpose(blk(ps, h * (qt + 1) + kt), c.es[:, h, kt * P:(kt + 1) * P], c.ident)
        last.then_inc(s["side_ready"], 1)

    def weigh_values(qt):
        ps = side(f"oa{qt}")
        pe.wait_ge(s["aT_ready"], qt + 1)
        pe.wait_ge(s["dv_ready"], 1)
        for h in range(H):
            for kt in range(qt + 1):
                last = pe.matmul(blk(ps, h), blk(c.aT, h * (qt + 1) + kt), c.dv[:, kt, h * P:(h + 1) * P],
                                 start=(kt == 0), stop=(kt == qt))
        last.then_inc(s["side_ready"], 1)

    def state_in(n):
        ps = side(f"ws{n}")
        pe.wait_ge(s["S_ready"], n)
        for h in range(H):
            last = pe.matmul(blk(ps, h), c.wT[:, n // 2, h, :], c.S[:, h, :], start=True, stop=True)
        last.then_inc(s["side_ready"], 1)

    def state_out(n):
        t = n // 2
        ps = side(f"so{n}")
        pe.wait_ge(s["vn_ready"], n + 1)
        for h in range(H):
            if n:
                pe.matmul(blk(ps, h), c.qdec[:, t, h, :], c.S[:, h, :], start=True, stop=False)
            last = pe.matmul(blk(ps, h), c.attnT[:, t, h, :], c.vn[n % 2][:, h, :], start=(n == 0), stop=True)
        if n < 3:
            for h in range(H):
                last = pe.matmul(blk(ps, H + h), c.kdec[:, t, h, :], c.vn[n % 2][:, h, :], start=True, stop=True)
        last.then_inc(s["side_ready"], 1)

    scores(0)
    project("ma1", 2)
    pe.wait_ge(s["wT_ready"], 1)
    state_out(0)
    project("ma1", 3)
    turn_probs(0)
    state_in(1)
    project("mb0", 0)
    weigh_values(0)
    state_out(1)
    project("mb0", 1)
    scores(1)
    state_in(2)
    project("mb0", 2)
    state_out(2)
    turn_probs(1)
    project("mb0", 3)
    state_in(3)
    weigh_values(1)
    project("mb1", 0)
    state_out(3)
    project("mb1", 1)
    pe.wait_ge(s["ya_ready"], 1)
    turn("yaT", lambda i: c.oa[:, i % 2, (i // 2) * P:(i // 2 + 1) * P])
    project("mb1", 2)
    project("mb1", 3)
    pe.wait_ge(s["yb_ready"], 1)
    turn("ybT", lambda i: c.ob[:, i % 2, (i // 2) * P:(i // 2 + 1) * P])

    for j, yT in enumerate((c.yaT, c.ybT)):
        i = NCH + j
        w = c.stage[i % 2][:, 0:4096].rearrange("p (k n) -> p k n", k=H)
        pe.wait_ge(s[f"stage_loaded{i % 2}"], 16 * (i // 2 + 1))
        pe.wait_ge(s["yaT_ready" if j == 0 else "ybT_ready"], 1)
        if j == 0:
            for q in range(2):
                pe.wait_ge(s[f"pair_free{q}"], (NCH + 1 - q) // 2)
        for half in range(2):
            n = 2 * j + half
            if n >= 2:
                pe.wait_ge(s["branch_used"], n - 1)
            for b in range(4):
                for k in range(H):
                    last = pe.matmul(blk(c.pair[half], b, TOK), w[:, k, (4 * half + b) * P:(4 * half + b + 1) * P], yT[:, k, :],
                                     start=(k == 0), stop=(k == H - 1))
            last.then_inc(s["branch_ready"], 1)
        pe.wait_ge(s["branch_ready"], 2 * j + 2)
        pe.sem_inc(s["stage_used"], 1)
    pe.wait_ge(s["ybT_ready"], 1)
    pe.wait_ge(s["yaT_ready"], 1)
    pe.wait_ge(s["merged_ready"], 2)
    for half in range(2):
        i = NCH + 2 + half
        w = c.stage[i % 2][:, 0:4096].rearrange("p (k n) -> p k n", k=KD)
        pe.wait_ge(s[f"stage_loaded{i % 2}"], 16 * (i // 2 + 1))
        for t in range(NT):
            for k in range(KD):
                mg = c.mg[k // 4][:, (k % 4) * TOK + t * P:(k % 4) * TOK + (t + 1) * P]
                last = pe.matmul(c.ps[:, 4 + 2 * t + half, :], mg, w[:, k, :], start=(k == 0), stop=(k == KD - 1))
            last.then_inc(s["mix_out"], 1)

    for t in range(NT):
        pe.wait_ge(s["h2_ready"], t + 1)
        for k in range(KD):
            last = pe.transpose(c.ps[:, 4 + k // 2, (k % 2) * 256 + t * P:(k % 2) * 256 + (t + 1) * P],
                                c.h2[:, t, k * P:(k + 1) * P], c.ident)
    last.then_inc(s["h2_transposed"], 1)
    pe.wait_ge(s["h2T_ready"], 4)
    pe.wait_ge(s["router_loaded"], 64)
    for t in range(NT):
        for k in range(KD):
            last = pe.matmul(c.ps[:, 0, 36 * t:36 * (t + 1)], c.h2T[:, k, t * P:(t + 1) * P], c.rw[:, k, :],
                             start=(k == 0), stop=(k == KD - 1))
    last.then_inc(s["logits_ready"], 1)
    pe.wait_ge(s["picks_ready"], 1)
    picks = c.r[:, 240:304]
    pe.matmul(c.ps[:, 1, 0:32], c.before, picks[:, 0:32], start=True, stop=True)
    pe.matmul(c.ps[:, 1, 32:64], c.before, picks[:, 32:64], start=True, stop=False)
    pe.matmul(c.ps[:, 1, 32:64], c.ones, picks[:, 0:32], start=False, stop=True)
    pe.matmul(c.ps[:, 1, 64:96], c.ones, picks[:, 0:32], start=True, stop=False)
    pe.matmul(c.ps[:, 1, 64:96], c.ones, picks[:, 32:64], start=False, stop=True).then_inc(s["ranks_ready"], 1)
    pe.wait_ge(s["onehot_ready"], 2)
    for k in range(KD):
        for t in range(NT):
            last = pe.matmul(c.ps[:, k, :], c.h2[:, t, k:D:KD], c.onehot[:, t, :], start=(t == 0), stop=(t == NT - 1))
        last.then_inc(s["gathered"], 1)

    pe.wait_ge(s["HgT_ready"], KD + 1)
    wide = pe.value_load(c.offs[0:1, EXPERTS:EXPERTS + 1], min_val=0, max_val=TOK)

    def windows(w):
        with pe.Fori(0, EXPERTS // RING) as it:
            for j in range(RING):
                pe.wait_ge(s["window_ready"], it * RING + (j + 1))
                pe.wait_ge(s[f"gateup{j}"], it * 32 + 32)
                pe.wait_ge(s["gu_free"], it * RING + (j + 1))
                gu = gate_up(c, j, w)
                for b, wt in enumerate((c.gate_w[j], c.gate_w[j], c.up_w[j], c.up_w[j])):
                    for k in range(KD):
                        last = pe.matmul(gu[:, b * w:(b + 1) * w], wt[:, k, b % 2:HID:2], c.window[j % 2][:, k * w:(k + 1) * w],
                                         start=(k == 0), stop=(k == KD - 1))
                last.then_inc(s["up_ready"], 1)
                pe.wait_ge(s[f"down{j}"], it * 16 + 16)
                pe.wait_ge(s["act_ready"], it * RING + (j + 3))
                pe.wait_ge(s["y_free"], it * RING + (j + 1))
                for b in range(KD):
                    for k in range(2):
                        last = pe.matmul(down_out(c, w)[:, b, :], c.down_w[j][:, k, b * P:(b + 1) * P],
                                         c.act[j % 2][:, k * w:(k + 1) * w], start=(k == 0), stop=(k == 1))
                last.then_inc(s["down_ready"], 1)
                pe.wait_ge(s["down_ready"], it * RING + (j + 1))
                pe.sem_inc(s["experts_used"], 1)
    with pe.If(wide <= NARROW):
        windows(NARROW)
    with pe.Else():
        windows(WIDE)

    pe.wait_ge(s["y_free"], EXPERTS + 1)
    for m in range(SLOTS // P):
        for half in range(2):
            for b in range(4):
                last = pe.transpose(c.ps[:, 2 * m + half, b * P:(b + 1) * P], c.YT[:, 4 * half + b, m * P:(m + 1) * P], c.ident)
            last.then_inc(s["yT_turned"], 1)
    pe.wait_ge(s["comb_ready"], 1)
    pe.wait_ge(s["Ys_ready"], 8)
    for m in range(SLOTS // P):
        for t in range(NT):
            last = pe.transpose(c.pair[0][:, m * TOK + t * P:m * TOK + (t + 1) * P], c.comb[:, t, m * P:(m + 1) * P], c.ident)
    last.then_inc(s["comb_turned"], 1)
    pe.wait_ge(s["ST_ready"], 1)
    for t in range(NT):
        for half in range(2):
            for m in range(SLOTS // P):
                last = pe.matmul(c.ps[:, 2 * t + half, :], c.ST[:, m, t * P:(t + 1) * P], c.Ys[:, m, half * 512:(half + 1) * 512],
                                 start=(m == 0), stop=(m == SLOTS // P - 1))
        last.then_inc(s["y_ready"], 1)


def down_out(c, w):
    banks = KD * w // 512
    return c.ps[:, 4:4 + banks, :].rearrange("p b f -> p (b f)").rearrange("p (k w) -> p k w", k=KD)


def vector_program(v, c, io):
    s = c.s
    n = [0]

    def chain(ins):
        n[0] += 1
        ins.then_inc(s["dve_chain"], 1)

    def settle():
        v.wait_ge(s["dve_chain"], n[0])

    def col(ap, i):
        return ap[:, i:i + 1]

    def blk(ap, i, w=P):
        return ap[:, i * w:(i + 1) * w]

    def side(name):
        v.wait_ge(s["side_ready"], SI[name] + 1)
        return c.side[side_pair(name)]

    def side_done(name, ins):
        ins.then_inc(s[f"side_free{side_pair(name)}"], 1)

    v.wait_ge(s["ssx_ready"], NT)
    v.tensor_scalar(c.ssx, c.ssx, 1.0 / D, EPS, ALU.mult, ALU.add).then_inc(s["ss2_in"], 1)
    v.wait_ge(s["rx_root"], 1)
    chain(v.reciprocal(c.rx, c.rx))
    settle()
    for t in range(NT):
        v.tensor_scalar(c.h[:, t, :], c.x[:, t, :], col(c.rx, t), None, ALU.mult).then_inc(s["h_ready"], 1)
    ps = side("consts")
    v.tensor_copy(c.cst, ps[:, 0:56]).then_inc(s["cst_ready"], 1)
    v.wait_ge(s["cst_ready"], 1)
    v.sem_inc(s[f"side_free{side_pair('consts')}"], 1)
    v.wait_ge(s["h_transposed"], 1)
    for k in (0, 1, 4, 5):
        v.tensor_scalar(c.hT[:, k, :], c.ps[:, k // 2, (k % 2) * 256:(k % 2 + 1) * 256], col(c.cst, k), None, ALU.mult).then_inc(s["hT_ready"], 1)

    def conv(name, dst, first):
        i = CI[name]
        v.wait_ge(s["proj_ready"], parts_before(i) + 4)
        src = c.pair[i % 2]
        for back in range(TAPS):
            for b in range(4):
                w = col(c.cst, 8 + 12 * (TAPS - 1 - back) + first + b)
                if back == 0:
                    ins = v.tensor_scalar(dst[:, b, :], blk(src, b, TOK), w, None, ALU.mult)
                else:
                    o = dst[:, b, back:TOK]
                    ins = v.scalar_tensor_tensor(out=o, in0=src[:, b * TOK:(b + 1) * TOK - back], scalar=w, in1=o,
                                                 op0=ALU.mult, op1=ALU.add)
                if back == TAPS - 1 and b == 3:
                    ins.then_inc(s[f"pair_free{i % 2}"], 1)
                else:
                    chain(ins)
            if back < TAPS - 1:
                settle()
        v.wait_ge(s[f"pair_free{i % 2}"], i // 2 + 1)
        settle()
        v.sem_inc(s["conv_ready"], 1)

    def silu(j, name, dst):
        v.wait_ge(s["conv_sig"], j + 1)
        v.tensor_tensor(dst, dst, c.sig[name], ALU.mult).then_inc(s["qkv_ready"], 1)
    conv("gk", c.ck, 4)
    silu(0, "gk", c.ck)
    conv("gq", c.cq, 0)
    silu(1, "gq", c.cq)
    i = CI["bdg"]
    v.wait_ge(s["gate_sig"], 1)
    v.tensor_tensor(c.flat["gate"], c.flat["gate"], c.pair[i % 2], ALU.mult).then_inc(s["gate_ready"], 1)
    v.wait_ge(s["gate_ready"], 1)
    v.sem_inc(s[f"pair_free{i % 2}"], 1)
    v.wait_ge(s["vectors_loaded"], 64)
    bd = side("bd")[:, 0:16].rearrange("p (t a h) -> p t a h", t=NT, a=2)
    v.wait_ge(s["beta_ready"], 1)
    for t in range(NT):
        chain(v.tensor_tensor(blk(c.z, t, 4), bd[:, t, 1, :], c.dtb, ALU.add))
    settle()
    v.sem_inc(s[f"side_free{side_pair('bd')}"], 1)
    chain(v.tensor_scalar(c.zm, c.z, 0.0, None, ALU.max))
    settle()
    v.scalar_tensor_tensor(out=c.z, in0=c.zm, scalar=-2.0, in1=c.z, op0=ALU.mult, op1=ALU.add).then_inc(s["g_in"], 1)
    v.wait_ge(s["lambda_loaded"], 64)
    chain(v.tensor_tensor(c.lamrows[:, 0, :], c.lamrows[:, 0, :], c.lamrows[:, 1, :], ALU.mult))
    chain(v.tensor_tensor(c.lamrows[:, 2, :], c.lamrows[:, 2, :], c.lamrows[:, 3, :], ALU.mult))
    settle()
    v.tensor_reduce(c.lam[:, 0:2], c.lamrows[:, 0:4:2, :], AX_X, ALU.add).then_inc(s["lam_in"], 1)
    ps = side("ss")
    v.tensor_scalar(c.rn, ps[:, 0:16], EPS, None, ALU.add).then_inc(s["rn_root"], 1)
    v.wait_ge(s["rn_root"], 2)
    chain(v.reciprocal(c.rn, c.rn))
    settle()
    v.tensor_scalar(c.rn[:, 8:16], c.rn[:, 8:16], float(P) ** -0.5, None, ALU.mult).then_inc(s["rn_ready"], 1)
    v.sem_inc(s[f"side_free{side_pair('ss')}"], 1)
    v.wait_ge(s["dec_exp"], 3)
    chain(v.tensor_tensor(c.sp, c.zm, c.z, ALU.add))
    settle()
    for t in range(NT):
        last = v.scalar_tensor_tensor(out=blk(c.g, t, 4), in0=blk(c.sp, t, 4), scalar=-1.0, in1=c.nea, op0=ALU.mult, op1=ALU.mult)
        if t == 0:
            chain(last)
    last.then_inc(s["g_ready"], 1)
    conv("gv", c.cv, 8)
    silu(2, "gv", c.cv)
    for name, dst, sem in (("rnk", c.ck, "k_normed"), ("rnq", c.cq, "q_normed")):
        ps = side(name).rearrange("p (t h f) -> p t h f", t=NT, h=H)
        for t in range(NT):
            d = dst[:, :, t * P:(t + 1) * P]
            last = v.tensor_tensor(d, d, ps[:, t], ALU.mult)
            if t == 0:
                chain(last)
        side_done(name, last)
        v.wait_ge(s[f"side_free{side_pair(name)}"], side_reuse(name) + 1)
        settle()
        v.sem_inc(s[sem], 1)
    ps = side("gsum")
    chain(v.tensor_copy(c.run_sum, ps[:, 0:8]))
    chain(v.tensor_copy(c.chunk_sum, ps[:, 8:16]))
    chain(v.tensor_copy(c.sums_in[:, 0:8], ps[:, 0:8]))
    side_done("gsum", v.tensor_copy(c.sums_in[:, 16:32], ps[:, 16:32]))
    settle()
    v.wait_ge(s[f"side_free{side_pair('gsum')}"], side_reuse("gsum") + 1)
    v.tensor_tensor(c.sums_in[:, 8:16], c.chunk_sum, c.run_sum, ALU.subtract).then_inc(s["gsum_ready"], 1)
    ps = side("grow")
    v.wait_ge(s["squares_ready"], 2)
    v.wait_ge(s["side_ready"], SI["ss"] + 1)
    for j, (buf, op) in enumerate((("T", ALU.max), ("attnT", ALU.min))):
        for i in range(8):
            last = v.tensor_scalar(blk(c.flat[buf], i), blk(ps, i), col(c.run_sum, i), 0.0, ALU.subtract, op)
            if i < 7:
                chain(last)
        last.then_inc(s["grow_pre"], 1)
    def masked(buf, mask):
        return v.tensor_tensor(c.flat[buf].rearrange("p (a f) -> p a f", a=8), c.flat[buf].rearrange("p (a f) -> p a f", a=8),
                               mask.rearrange("p (a f) -> p a f", a=1).to_broadcast([P, 8, P]), ALU.mult)
    v.wait_ge(s["grow_exp"], 1)
    v.wait_ge(s["masks_ready"], 1)
    chain(masked("T", c.lower))
    v.wait_ge(s["grow_exp"], 2)
    chain(masked("attnT", c.upper))
    settle()
    v.wait_ge(s["gsum_exp"], 1)
    chain(v.tensor_tensor(c.bexp, c.beta, c.sums_exp[:, 0:8], ALU.mult))
    ps = side("gram")
    for i in range(8):
        last = v.scalar_tensor_tensor(out=blk(c.flat["A"], i), in0=blk(ps, i), scalar=col(c.beta, i), in1=blk(c.flat["T"], i),
                                      op0=ALU.mult, op1=ALU.mult)
        if i < 7:
            chain(last)
    side_done("gram", last)
    ps = side("intra")
    side_done("intra", v.tensor_tensor(c.flat["attnT"], c.flat["attnT"], ps, ALU.mult))
    v.wait_ge(s[f"side_free{side_pair('gram')}"], side_reuse("gram") + 1)
    settle()
    A8, Y8 = (c.flat[x].rearrange("p (a f) -> p a f", a=8) for x in ("A", "Yb"))
    T8, TT8 = (c.flat[x].rearrange("p (a f) -> p a f", a=8) for x in ("T", "TT"))

    def all8(m):
        return m.rearrange("p (a f) -> p a f", a=1).to_broadcast([P, 8, P])
    v.tensor_tensor(Y8, A8, all8(c.m1), ALU.mult).then_inc(s["b1_ready"], 1)
    cq4 = c.cq.rearrange("p h (t f) -> p h t f", t=NT)
    ps = side("ktok")
    for i in range(8):
        chain(v.tensor_scalar(blk(c.flat["wrhs"], i), blk(ps, i), col(c.bexp, i), None, ALU.mult))
    for i in range(8):
        last = v.tensor_scalar(blk(c.flat["kdec"], i), blk(ps, i), col(c.sums_exp, 8 + i), None, ALU.mult)
        if i < 7:
            chain(last)
    side_done("ktok", last)
    v.wait_ge(s[f"side_free{side_pair('ktok')}"], side_reuse("ktok") + 1)
    settle()
    v.sem_inc(s["tok_ready"], 2)
    ps = side("vtok")
    for i in range(8):
        last = v.tensor_scalar(blk(c.flat["vb"], i), blk(ps, i), col(c.beta, i), None, ALU.mult)
        if i < 7:
            chain(last)
    side_done("vtok", last)
    v.wait_ge(s[f"side_free{side_pair('vtok')}"], side_reuse("vtok") + 1)
    settle()
    v.sem_inc(s["tok_ready"], 1)
    v.wait_ge(s["b1_ready"], 1)
    v.tensor_tensor(T8, all8(c.ident), Y8, ALU.subtract).then_inc(s["T_ready"], 1)
    ps = side("b1")
    last = v.tensor_tensor(TT8, all8(c.ident), ps.rearrange("p (a f) -> p a f", a=8), ALU.subtract)
    last.then_inc(s["TT_ready"], 1)
    v.wait_ge(s["TT_ready"], 1)
    v.sem_inc(s[f"side_free{side_pair('b1')}"], 1)
    for lv in range(1, LEVELS + 1):
        ps = side(f"Y{lv}").rearrange("p (a f) -> p a f", a=8)
        v.tensor_tensor(Y8, ps, all8(c.levelT[lv - 1]), ALU.mult).then_inc(s["Y_ready"], 1)
        v.wait_ge(s["Y_ready"], lv)
        v.sem_inc(s[f"side_free{side_pair(f'Y{lv}')}"], 1)
        ps = side(f"TT{lv}")
        v.tensor_tensor(c.flat["TT"], c.flat["TT"], ps, ALU.subtract).then_inc(s["TT_ready"], 1)
        v.wait_ge(s["TT_ready"], lv + 1)
        v.sem_inc(s[f"side_free{side_pair(f'TT{lv}')}"], 1)
        if lv < LEVELS:
            ps = side(f"T{lv}")
            v.tensor_tensor(c.flat["T"], c.flat["T"], ps, ALU.subtract).then_inc(s["T_ready"], 1)
            v.wait_ge(s["T_ready"], lv + 1)
            v.sem_inc(s[f"side_free{side_pair(f'T{lv}')}"], 1)
        if lv == 1:
            for t in range(NT):
                chain(v.tensor_tensor(c.E[:, t], c.E[:, t], c.cq[:, :, t * P:(t + 1) * P], ALU.mult))
            settle()
            v.tensor_copy(c.flat["cq"], c.flat["EwT"]).then_inc(s["qdec_ready"], 1)
    side_done("u", v.tensor_copy(c.flat["cv"], side("u")))
    v.wait_ge(s["qdec_ready"], 1)
    side_done("wT", v.tensor_copy(c.flat["EwT"], side("wT")))
    v.wait_ge(s[f"side_free{side_pair('wT')}"], side_reuse("wT") + 1)
    v.wait_ge(s[f"side_free{side_pair('u')}"], side_reuse("u") + 1)
    v.sem_inc(s["wT_ready"], 1)

    def maxima(qt):
        nk = P * (qt + 1)
        for m in range(2):
            ps = side(f"s{qt}{m}").rearrange("p (h k) -> p h k", h=H)
            chain(v.memset(ps[0:CHUNK, :, nk - CHUNK:nk], -BIG))
            settle()
            nm = c.negmax[:, 8 * qt + 4 * m:8 * qt + 4 * m + 4]
            chain(v.tensor_reduce(nm, ps[:, :, 0:nk], AX_X, ALU.max))
            settle()
            v.tensor_scalar(nm, nm, -DH ** -0.5, None, ALU.mult).then_inc(s["negmax_ready"], 1)

    def combine(qt):
        nk = P * (qt + 1)
        v.wait_ge(s["exps_ready"], 8 * (qt + 1))
        cf = c.coef[:, 8 * qt:8 * qt + 8]
        chain(v.reciprocal(cf, c.esum[:, 8 * qt:8 * qt + 8]))
        settle()
        chain(v.tensor_scalar(cf[:, 4:8], cf[:, 4:8], c.lamw[:, 0:1], None, ALU.mult))
        settle()
        for h in range(H):
            chain(v.tensor_scalar(c.es[:, 4 + h, 0:nk], c.es[:, 4 + h, 0:nk], col(cf, 4 + h), None, ALU.mult))
        settle()
        for h in range(H):
            last = v.scalar_tensor_tensor(out=c.es[:, h, 0:nk], in0=c.es[:, h, 0:nk], scalar=col(cf, h), in1=c.es[:, 4 + h, 0:nk],
                                          op0=ALU.mult, op1=ALU.add)
            if h < H - 1:
                chain(last)
        last.then_inc(s["aT_in"], 1)

    def probs_turned(qt):
        w = 512 * (qt + 1)
        v.tensor_copy(c.aT[:, 0:w], side(f"aT{qt}")[:, 0:w]).then_inc(s["aT_ready"], 1)
        v.wait_ge(s["aT_ready"], qt + 1)
        v.sem_inc(s[f"side_free{side_pair(f'aT{qt}')}"], 1)

    def attended(qt):
        v.tensor_copy(c.oa[:, qt, :], side(f"oa{qt}")[:, 0:512]).then_inc(s["oa_out"], 1)
        v.wait_ge(s["oa_out"], qt + 1)
        v.sem_inc(s[f"side_free{side_pair(f'oa{qt}')}"], 1)

    def new_values(n_):
        rows = slice(CHUNK * (n_ % 2), CHUNK * (n_ % 2) + CHUNK)
        dst = c.vn[n_ % 2][rows]
        u = c.u[rows, n_ // 2]
        if n_ == 0:
            v.tensor_copy(dst, u).then_inc(s["vn_ready"], 1)
        else:
            ps = side(f"ws{n_}")[rows, 0:512].rearrange("p (h f) -> p h f", h=H)
            v.tensor_tensor(dst, u, ps, ALU.subtract).then_inc(s["vn_ready"], 1)
            v.wait_ge(s["vn_ready"], n_ + 1)
            v.sem_inc(s[f"side_free{side_pair(f'ws{n_}')}"], 1)

    def new_state(n_):
        rows = slice(CHUNK * (n_ % 2), CHUNK * (n_ % 2) + CHUNK)
        ps = side(f"so{n_}")
        if n_ < 3:
            if n_ == 0:
                chain(v.tensor_copy(c.S.rearrange("p h f -> p (h f)"), ps[:, 512:1024]))
            else:
                for h in range(H):
                    chain(v.scalar_tensor_tensor(out=c.S[:, h, :], in0=c.S[:, h, :], scalar=col(c.sums_exp, 16 + 4 * n_ + h),
                                                 in1=blk(ps, H + h), op0=ALU.mult, op1=ALU.add))
            settle()
            v.sem_inc(s["S_ready"], 1)
        v.tensor_copy(c.ob[rows, n_ // 2, :], ps[rows, 0:512]).then_inc(s["ob_out"], 1)
        v.wait_ge(s["ob_out"], n_ + 1)
        v.sem_inc(s[f"side_free{side_pair(f'so{n_}')}"], 1)

    v.wait_ge(s["lam_exp"], 1)
    chain(v.tensor_tensor(c.lamw[:, 0:1], c.lam[:, 3:4], c.lam[:, 2:3], ALU.subtract))
    settle()
    chain(v.tensor_scalar(c.lamw[:, 0:1], c.lamw[:, 0:1], LAMBDA_INIT, None, ALU.subtract))
    new_values(0)
    maxima(0)
    new_state(0)
    combine(0)
    probs_turned(0)
    new_values(1)
    attended(0)
    new_state(1)
    maxima(1)
    new_values(2)
    combine(1)
    new_state(2)
    probs_turned(1)
    new_values(3)
    attended(1)
    new_state(3)

    def head_norm(squares, ss, sq_flat, root, buf, gain, name):
        v.wait_ge(s[squares], 1)
        chain(v.tensor_reduce(ss, sq_flat.rearrange("p (a f) -> p a f", a=8), AX_X, ALU.add))
        settle()
        v.tensor_scalar(ss, ss, 1.0 / P, EPS, ALU.mult, ALU.add).then_inc(s[root], 1)
        v.wait_ge(s[root], 2)
        chain(v.reciprocal(ss, ss))
        settle()
    chain(v.tensor_scalar(c.subln[:, :], c.subln[:, :], 1.0 - LAMBDA_INIT, None, ALU.mult))
    head_norm("oa_squares", c.ra, c.flat["Yb"], "oa_root", None, None, None)
    for i in range(8):
        b = blk(c.flat["F"], i)
        last = v.scalar_tensor_tensor(out=b, in0=b, scalar=col(c.ra, i), in1=c.subln[:, :], op0=ALU.mult, op1=ALU.mult)
        if i < 7:
            chain(last)
    last.then_inc(s["ya_ready"], 1)
    g8 = c.flat["gate"].rearrange("p (a f) -> p a f", a=8)
    v.tensor_tensor(g8, g8, all8(c.gdng[:, :]), ALU.mult).then_inc(s["gate_ready"], 1)
    head_norm("ob_squares", c.rb, c.flat["A"], "ob_root", None, None, None)
    v.wait_ge(s["gate_ready"], 2)
    for i in range(8):
        b = blk(c.flat["TT"], i)
        last = v.scalar_tensor_tensor(out=b, in0=b, scalar=col(c.rb, i), in1=blk(c.flat["gate"], i), op0=ALU.mult, op1=ALU.mult)
        if i < 7:
            chain(last)
    last.then_inc(s["yb_ready"], 1)
    side_done("yaT", v.tensor_copy(c.flat["qT"], side("yaT")))
    v.wait_ge(s[f"side_free{side_pair('yaT')}"], side_reuse("yaT") + 1)
    v.sem_inc(s["yaT_ready"], 1)

    v.wait_ge(s["mg_ready"], 4)
    for q in range(4):
        v.wait_ge(s["branch_ready"], q + 1)
        v.tensor_tensor(c.mg[q], c.mg[q], c.pair[q % 2], ALU.mult).then_inc(s["branch_used"], 1)
        if q >= 2:
            v.wait_ge(s["branch_used"], q + 1)
            v.tensor_tensor(c.mg[q - 2], c.mg[q - 2], c.mg[q], ALU.add).then_inc(s["merged_ready"], 1)
    for t in range(NT):
        v.wait_ge(s["mix_out"], 3 + t)
        v.tensor_tensor(c.x[:, t, :], c.x[:, t, :], c.ps[:, 4 + 2 * t:6 + 2 * t, :].rearrange("p b f -> p (b f)"), ALU.add)\
            .then_inc(s["x1_ready"], 1)
    v.wait_ge(s["ss1_ready"], NT)
    v.tensor_scalar(c.ssx, c.ssx, 1.0 / D, EPS, ALU.mult, ALU.add).then_inc(s["r1_root"], 1)
    v.wait_ge(s["r1_root"], 2)
    chain(v.reciprocal(c.rx, c.rx))
    settle()
    v.wait_ge(s["gffn_loaded"], 16)
    v.wait_ge(s["x1_ready"], NT)
    for t in range(NT):
        v.scalar_tensor_tensor(out=c.h2[:, t, :], in0=c.x[:, t, :], scalar=col(c.rx, t), in1=c.gffn, op0=ALU.mult, op1=ALU.mult)\
            .then_inc(s["h2_ready"], 1)
    v.wait_ge(s["h2_transposed"], 1)
    for b in (0, 2):
        v.tensor_copy(c.h2T[:, 2 * b:2 * b + 2, :].rearrange("p a b -> p (a b)"), c.ps[:, 4 + b, :]).then_inc(s["h2T_ready"], 1)

    route(v, c, chain, settle)

    for k in range(0, KD, 2):
        v.wait_ge(s["gathered"], k + 1)
        v.tensor_copy(c.HgT[:, k, 0:SLOTS], c.ps[:, k, :]).then_inc(s["HgT_ready"], 1)
    pos, wk = c.r[:, 480:484], c.r[:, 484:488]
    for t in range(NT):
        chain(v.tensor_scalar(c.comb[:, t, :], c.iota[:, :], col(pos, t), col(wk, t), ALU.is_equal, ALU.mult))
    v.wait_ge(s["gathered"], KD)
    for t in range(NT):
        chain(v.tensor_scalar(c.onehot[:, t, :], c.iota[:, :], col(pos, 2 + t), col(wk, 2 + t), ALU.is_equal, ALU.mult))
    settle()
    for t in range(NT):
        last = v.tensor_tensor(c.comb[:, t, :], c.comb[:, t, :], c.onehot[:, t, :], ALU.add)
        if t == 0:
            chain(last)
    last.then_inc(s["comb_ready"], 1)

    v.sem_inc(s["gu_free"], 2)
    v.sem_inc(s["act_ready"], 2)
    v.sem_inc(s["y_free"], 1)
    wide = v.value_load(c.offs[0:1, EXPERTS:EXPERTS + 1], min_val=0, max_val=TOK)

    def windows(w):
        with v.Fori(0, EXPERTS // RING) as it:
            for j in range(RING):
                gu = gate_up(c, j, w)
                act = c.act[j % 2][:, 0:2 * w]
                sg = c.sg[j % 2][:, 0:2 * w]
                v.wait_ge(s["gate_sigmoid"], it * RING + (j + 1))
                v.tensor_tensor(act, gu[:, 0:2 * w], sg, ALU.mult).then_inc(s["TT_ready"], 1)
                v.wait_ge(s["TT_ready"], it * RING + (j + 2 + LEVELS))
                v.tensor_tensor(act, act, gu[:, 2 * w:4 * w], ALU.mult).then_inc(s["act_ready"], 1)
                v.wait_ge(s["act_ready"], it * RING + (j + 3))
                v.sem_inc(s["gu_free"], 1)
                off = v.value_load(c.offs[0:1, bass.ds(it * RING + j, 1)], min_val=0, max_val=SLOTS)
                v.wait_ge(s["down_ready"], it * RING + (j + 1))
                v.wait_ge(s["y_free"], it * RING + (j + 1))
                v.tensor_copy(c.YT[:, :, bass.ds(off, w)], down_out(c, w)).then_inc(s["y_free"], 1)
    with v.If(wide <= NARROW):
        windows(NARROW)
    with v.Else():
        windows(WIDE)
    for m in range(0, SLOTS // P * 2, 2):
        v.wait_ge(s["yT_turned"], m + 1)
        v.tensor_copy(c.Ys[:, m // 2, 0:512], c.ps[:, m, :]).then_inc(s["Ys_ready"], 1)
    v.wait_ge(s["comb_turned"], 1)
    v.tensor_copy(c.ST.rearrange("p a b -> p (a b)"), c.pair[0]).then_inc(s["ST_ready"], 1)
    v.wait_ge(s["gfin_loaded"], 16)
    for t in range(NT):
        v.wait_ge(s["y_ready"], t + 1)
        v.tensor_tensor(c.x[:, t, :], c.x[:, t, :], c.pair[t], ALU.add).then_inc(s["ss2_in"], 1)
        v.wait_ge(s["ss2_ready"], t + 1)
        v.tensor_scalar(col(c.ssx, t), col(c.ssx, t), 1.0 / D, EPS, ALU.mult, ALU.add).then_inc(s["r2_root"], 1)
        v.wait_ge(s["r2_root"], 2 * t + 2)
        chain(v.reciprocal(col(c.rx, t), col(c.rx, t)))
        settle()
        v.scalar_tensor_tensor(out=c.y[:, t, :], in0=c.x[:, t, :], scalar=col(c.rx, t), in1=c.gfin, op0=ALU.mult, op1=ALU.mult)\
            .then_inc(s["out_ready"], 1)


def route(v, c, chain, settle):
    s = c.s
    r = c.r
    lg = r[:, 0:72].rearrange("p (t n) -> p t n", t=NT)
    gsh = r[:, 72:80].rearrange("p (t n) -> p t n", t=NT)
    one = {"g": r[:, 80:88].rearrange("p (t n) -> p t n", t=NT), 0: r[:, 88:104].rearrange("p (t n) -> p t n", t=NT),
           1: r[:, 104:120].rearrange("p (t n) -> p t n", t=NT)}
    cand = {4: r[:, 120:128].rearrange("p (t n) -> p t n", t=NT), 8: r[:, 120:136].rearrange("p (t n) -> p t n", t=NT)}
    mx = {"g": r[:, 136:138], 0: r[:, 138:140], 1: r[:, 140:142]}
    low = r[:, 142:144]
    dif = r[:, 144:146]
    gw = r[:, 146:148]
    ing = r[:, 152:168].rearrange("p (t n) -> p t n", t=NT)
    prod = r[:, 168:232].rearrange("p (t e g) -> p t e g", t=NT, e=PER_GROUP)
    picks = r[:, 240:304]
    pick = {0: r[:, 304:368], 1: r[:, 368:432]}
    scan = r[:, 432:464]
    pos, wk = r[:, 480:484], r[:, 484:488]
    base = r[:, 168:232]
    counts = r[:, 488:520]

    def over(ap, n):
        return ap.rearrange("p (t a) -> p t a", a=1).to_broadcast([P, NT, n])

    def ids(n):
        return c.iota[:, 0:n].rearrange("p (a n) -> p a n", a=1).to_broadcast([P, NT, n])

    def link(ins):
        chain(ins)
        settle()

    def first_max(vals, n, key):
        link(v.tensor_reduce(mx[key], vals, AX_X, ALU.max))
        link(v.tensor_tensor(cand[n], vals, over(mx[key], n), ALU.is_equal))
        for t in range(NT):
            chain(v.scalar_tensor_tensor(out=cand[n][:, t, :], in0=cand[n][:, t, :], scalar=-1000.0, in1=c.iota[:, 0:n],
                                         op0=ALU.mult, op1=ALU.add))
        settle()
        link(v.tensor_reduce(low, cand[n], AX_X, ALU.min))
        link(v.tensor_tensor(one[key], cand[n], over(low, n), ALU.is_equal))
    v.wait_ge(s["logits_ready"], 1)
    v.wait_ge(s["iota_ready"], 1)
    v.wait_ge(s["router_loaded"], 64)
    link(v.tensor_tensor(lg, c.ps[:, 0, 0:72].rearrange("p (t n) -> p t n", t=NT),
                         c.rbias.rearrange("p (a n) -> p a n", a=1).to_broadcast([P, NT, 36]), ALU.add))
    first_max(lg[:, :, 0:GROUPS], GROUPS, "g")
    v.tensor_tensor(gsh, lg[:, :, 0:GROUPS], over(mx["g"], GROUPS), ALU.subtract).then_inc(s["gexp_in"], 1)
    for t in range(NT):
        chain(v.tensor_tensor(prod[:, t], lg[:, t, GROUPS:].rearrange("p (g e) -> p e g", g=GROUPS),
                              one["g"][:, t, :].rearrange("p (a g) -> p a g", a=1).to_broadcast([P, PER_GROUP, GROUPS]), ALU.mult))
    settle()
    link(v.tensor_reduce(ing, prod, AX_X, ALU.add))
    first_max(ing, PER_GROUP, 0)
    link(v.scalar_tensor_tensor(out=ing, in0=one[0], scalar=-BIG, in1=ing, op0=ALU.mult, op1=ALU.add))
    first_max(ing, PER_GROUP, 1)
    for k in range(2):
        for t in range(NT):
            chain(v.tensor_tensor(pick[k][:, 32 * t:32 * (t + 1)].rearrange("p (g e) -> p g e", g=GROUPS),
                                  one["g"][:, t, :].rearrange("p (g a) -> p g a", a=1).to_broadcast([P, GROUPS, PER_GROUP]),
                                  one[k][:, t, :].rearrange("p (a e) -> p a e", a=1).to_broadcast([P, GROUPS, PER_GROUP]), ALU.mult))
    v.tensor_tensor(dif, mx[1], mx[0], ALU.subtract).then_inc(s["texp_in"], 1)
    settle()
    v.tensor_tensor(picks, pick[0], pick[1], ALU.add).then_inc(s["picks_ready"], 1)
    v.wait_ge(s["gexp_out"], 1)
    link(v.tensor_reduce(gw, gsh, AX_X, ALU.add))
    link(v.reciprocal(gw, gw))
    v.wait_ge(s["texp_out"], 1)
    link(v.tensor_scalar(wk[:, 0:2], dif, 1.0, None, ALU.add))
    link(v.reciprocal(wk[:, 0:2], wk[:, 0:2]))
    link(v.tensor_tensor(wk[:, 0:2], wk[:, 0:2], gw, ALU.mult))
    chain(v.tensor_tensor(wk[:, 2:4], wk[:, 0:2], dif, ALU.mult))
    v.wait_ge(s["ranks_ready"], 1)
    chain(v.tensor_copy(counts, c.ps[:, 1, 64:96]))
    settle()
    chain(v.tensor_tensor_scan(scan, counts, counts, 0.0, ALU.add, ALU.bypass))
    chain(v.tensor_reduce(low[:, 0:1], counts, AX_X, ALU.max))
    settle()
    link(v.tensor_tensor(scan, scan, counts, ALU.subtract))
    link(v.tensor_tensor(base.rearrange("p (t e) -> p t e", t=NT), c.ps[:, 1, 0:64].rearrange("p (t e) -> p t e", t=NT),
                         scan.rearrange("p (a e) -> p a e", a=1).to_broadcast([P, NT, EXPERTS]), ALU.add))
    for k in range(2):
        chain(v.tensor_tensor(pick[k], pick[k], base, ALU.mult))
    settle()
    for k in range(2):
        chain(v.tensor_reduce(pos[:, 2 * k:2 * k + 2], pick[k].rearrange("p (t e) -> p t e", t=NT), AX_X, ALU.add))
    chain(v.tensor_copy(c.offs[:, 0:EXPERTS], scan[0:1, :]))
    settle()
    v.tensor_copy(c.offs[:, EXPERTS:EXPERTS + 1], low[0:1, 0:1]).then_inc(s["offsets_ready"], 1)
    for t in range(NT):
        chain(v.tensor_scalar(c.onehot[:, t, :], c.iota[:, :], pos[:, t:t + 1], None, ALU.is_equal))
    settle()
    for t in range(NT):
        v.scalar_tensor_tensor(out=c.onehot[:, t, :], in0=c.iota[:, :], scalar=pos[:, 2 + t:3 + t], in1=c.onehot[:, t, :],
                               op0=ALU.is_equal, op1=ALU.add).then_inc(s["onehot_ready"], 1)
    v.memset(c.HgT[:, :, SLOTS:SLOTS + WIDE], 0.0).then_inc(s["HgT_ready"], 1)


def build(nc, io):
    with ExitStack() as ctx:
        c = lay_out(nc, ctx)
        block = ctx.enter_context(nc.Block())

        @block.sync
        def _(sp):
            sync_program(sp, c, io)

        @block.gpsimd
        def _(pool):
            gpsimd_program(pool, c, io)
            pool.wait_ge(c.s["gathered"], KD)
            pool.dma_start(c.gfin, io["norm_final_gain"].rearrange("(a d) -> a d", a=1).partition_broadcast(P)
                           .rearrange("p a d -> p (a d)")).then_inc(c.s["gfin_loaded"], 16)

        @block.scalar
        def _(act):
            scalar_program(act, c, io)

        @block.tensor
        def _(pe):
            tensor_program(pe, c, io)

        @block.vector
        def _(v):
            vector_program(v, c, io)


_INS = ["x", "norm_mix_gain", "w_in", "diff_lambda_q1", "diff_lambda_k1", "diff_lambda_q2", "diff_lambda_k2",
        "diff_subln_gain", "gdn_conv_w", "gdn_a_log", "gdn_dt_bias", "gdn_norm_gain", "w_branch_attn", "w_branch_gdn",
        "w_out", "norm_ffn_gain", "moe_w_group", "moe_b_group", "moe_w_expert", "moe_b_expert", "moe_w_gate",
        "moe_w_up", "moe_w_down", "norm_final_gain"]


def kernel(**inputs):
    import numpy as _np
    import concourse.bacc as _bacc
    from concourse import mybir as _mybir
    from concourse.bass_utils import run_bass_kernel_spmd as _run

    nc = _bacc.Bacc("TRN2", target_bir_lowering=False, num_devices=1)
    arrays, io = {}, {}
    for name in _INS:
        a = _np.ascontiguousarray(inputs[name])
        arrays[f"in_{name}"] = a
        io[name] = nc.dram_tensor(f"in_{name}", a.shape, _mybir.dt.from_np(a.dtype), kind="ExternalInput").ap()
    io["out"] = nc.dram_tensor("out_y", (1, TOK, D), _mybir.dt.from_np(_np.dtype("float32")), kind="ExternalOutput").ap()
    build(nc, io)
    r = _run(nc, [arrays], core_ids=[0])
    return r.results[0]["out_y"]
```

```python
from contextlib import ExitStack

import concourse.bass as bass
from concourse import mybir

F32 = mybir.dt.float32
I32 = mybir.dt.int32
ALU = mybir.AluOpType
ACT = mybir.ActivationFunctionType
AX_X = mybir.AxisListType.X

P = 128
D = 1024
TOK = 256
NT = TOK // P
KD = D // P
EPS = 1e-6
H = 4
DH = 64
W4 = H * P
CHUNK = 64
TAPS = 4
GROUPS, PER_GROUP = 4, 8
EXPERTS = GROUPS * PER_GROUP
HID = 256
SLOTS = 2 * TOK
PATHS = [(32, 1), (64, 1), (128, 2)]
RING = 4
EXP_F = 3 * D * HID // P
BIG = 1e30
LAMBDA_INIT = 0.2

CHUNKS = [("gk", 2048, 512, "T"), ("gq", 1536, 512, "T"), ("bdg", 3072, 520, "N"), ("gv", 2560, 512, "T"),
          ("dq", 0, 512, "T"), ("dk", 512, 512, "T"), ("dv", 1024, 512, "N"),
          ("ma0", 3592, 512, "T"), ("ma1", 4104, 512, "T"), ("mb0", 4616, 512, "T"), ("mb1", 5128, 512, "T")]
NCH = len(CHUNKS)
CI = {c[0]: i for i, c in enumerate(CHUNKS)}
PARTS = [4 if c[3] == "T" else 2 for c in CHUNKS]

LEVELS = 5
SIDE = [("consts", 1), ("bd", 1), ("ss", 1), ("rnk", 1), ("rnq", 1), ("gsum", 1), ("grow", 1), ("gram", 1),
        ("intra", 1), ("ktok", 1), ("vtok", 1), ("b1", 1)]
for _l in range(1, LEVELS + 1):
    SIDE += [(f"Y{_l}", 1), (f"TT{_l}", 1)] + ([(f"T{_l}", 1)] if _l < LEVELS else [])
SIDE += [("u", 1), ("wT", 1), ("s00", 1), ("s01", 1), ("so0", 1), ("aT0", 1), ("ws1", 1), ("oa0", 1), ("so1", 1),
         ("s10", 1), ("s11", 1), ("ws2", 1), ("so2", 1), ("aT1", 1), ("ws3", 1), ("oa1", 1), ("so3", 1),
         ("yaT", 1), ("ybT", 1)]
SI = {n: i for i, (n, _) in enumerate(SIDE)}


def side_pair(name):
    return SI[name] % 2


def side_reuse(name):
    i = SI[name]
    return sum(c for j, (_, c) in enumerate(SIDE[:i]) if j % 2 == i % 2)


def parts_before(i):
    return sum(PARTS[:i])


class Core:
    pass


def lay_out(nc, ctx):
    c = Core()
    stage_f = KD * 520
    names = {}

    def sb(name, shape, dt=F32):
        return ctx.enter_context(nc.sbuf_tensor(name, shape, dt))

    ring = sb("ring", [P, RING - 1, EXP_F])
    sizes = [("x", 2048), ("hT", 2048), ("stage0", stage_f), ("stage1", stage_f),
             ("qT", 1024), ("kT", 1024), ("dv", 1024), ("ck", 1024), ("cv", 1024), ("wrhs", 1024), ("vb", 1024),
             ("cq", 1024), ("kdec", 1024), ("F", 1024), ("gate", 1024), ("S", 512), ("vn", 1024),
             ("A", 1024), ("T", 1024), ("TT", 1024), ("Yb", 1024), ("attnT", 1024), ("EwT", 1024)]
    total = sum(n for _, n in sizes)
    arena = sb("arena", [P, total])
    off = 0
    for n, size in sizes:
        names[n] = off
        off += size

    def at(name, size, extra=0):
        return arena[:, names[name] + extra:names[name] + extra + size]

    c.ring = [ring[:, i, :] for i in range(RING - 1)] + [at("A", EXP_F)]
    c.gate_w = [r[:, 0:2048].rearrange("p (k f) -> p k f", k=KD) for r in c.ring]
    c.up_w = [r[:, 2048:4096].rearrange("p (k f) -> p k f", k=KD) for r in c.ring]
    c.gu_w = [r[:, 0:4096].rearrange("p (g k f) -> p g k f", g=2, k=KD) for r in c.ring]
    c.down_w = [r[:, 4096:6144].rearrange("p (k d) -> p k d", k=2) for r in c.ring]
    c.gate_flat = [r[:, 0:2048] for r in c.ring]
    c.up_flat = [r[:, 2048:4096] for r in c.ring]
    c.down_flat = [r[:, 4096:6144] for r in c.ring]

    def v3(ap, a):
        return ap.rearrange("p (a b) -> p a b", a=a)

    c.x = v3(at("x", 2048), NT)
    c.h = v3(at("A", 2048), NT)
    c.hT = v3(at("hT", 2048), KD)
    c.stage = [at("stage0", stage_f), at("stage1", stage_f)]
    c.qT, c.kT = v3(at("qT", 1024), H), v3(at("kT", 1024), H)
    c.dv = v3(at("dv", 1024), NT)
    c.cq, c.ck, c.cv = (v3(at(n, 1024), H) for n in ("cq", "ck", "cv"))
    c.sig = {"gk": v3(at("F", 1024), H), "gq": v3(at("TT", 1024), H), "gv": v3(at("Yb", 1024), H)}
    c.sqk, c.sqq = v3(at("A", 1024), H), v3(at("T", 1024), H)
    c.gate = v3(at("gate", 1024), NT)

    def prob(name):
        return at(name, 1024).rearrange("p (t h f) -> p t h f", t=NT, h=H)
    c.A, c.T, c.TT, c.Yb, c.attnT, c.E, c.wT = (prob(n) for n in ("A", "T", "TT", "Yb", "attnT", "EwT", "EwT"))
    c.Dm = c.T
    c.wrhs, c.vb, c.kdec, c.qdec, c.u = (prob(n) for n in ("wrhs", "vb", "kdec", "cq", "cv"))
    c.flat = {n: at(n, 1024) for n in ("A", "T", "TT", "Yb", "attnT", "EwT", "wrhs", "vb", "kdec", "cq", "ck", "cv",
                                       "F", "gate", "qT", "kT", "dv")}
    c.S = v3(at("S", 512), H)
    c.vn = [v3(at("vn", 512, 512 * i), H) for i in range(2)]
    c.ob = v3(at("TT", 1024), NT)
    c.oa = v3(at("F", 1024), NT)
    c.es = v3(at("A", 2048), 2 * H)
    c.aT = at("Yb", 1024)
    c.yaT, c.ybT = v3(at("qT", 1024), H), v3(at("kT", 1024), H)
    c.tmp = at("wrhs", 1024)
    c.mg = [at(n, 1024) for n in ("ck", "vb", "wrhs", "gate")]

    c.h2 = v3(at("hT", 2048), NT)
    base2 = names["stage0"]

    def at2(off2, size):
        return arena[:, base2 + off2:base2 + off2 + size]
    pad = SLOTS + TOK
    o2 = 0
    c.h2T = v3(at2(o2, 2048), KD)
    o2 += 2048
    c.onehot = v3(at2(o2, 1024), NT)
    o2 += 1024
    c.HgT = at2(o2, KD * pad).rearrange("p (k s) -> p k s", k=KD)
    o2 += KD * pad
    c.rows = at2(o2, 1024)
    o2 += 1024
    c.S_e = [at2(o2 + 256 * i, 256) for i in range(2)]
    o2 += 512
    c.S_tmp = at2(o2, 512)
    o2 += 512
    c.Y = [at2(o2 + 1024 * i, 1024) for i in range(2)]
    o2 += 2048
    c.act = [at2(o2 + 256 * i, 256) for i in range(2)]
    c.actT = [at2(o2 + 512 + 256 * i, 256) for i in range(2)]
    c.sg = [at2(o2 + 1024 + 256 * i, 256) for i in range(2)]
    o2 += 1536
    c.slot_of = at2(o2, 2 * EXPERTS)
    c.slot_at = at2(o2 + 2 * EXPERTS, 2 * EXPERTS)
    o2 += 4 * EXPERTS
    c.r = at2(o2, 520)
    o2 += 520
    c.iota = at2(o2, SLOTS)
    o2 += SLOTS
    assert base2 + o2 <= names["F"], (base2 + o2, names["F"])
    c.gffn = at("F", 1024)
    c.gfin = at("gate", 1024)
    c.y = v3(at("hT", 2048), NT)
    c.window = [at2(0, 1024), at2(1024, 1024)]

    m = sb("masks", [P, 14, P])
    c.ident, c.upper, c.lower, c.chunk, c.half0, c.half1, c.ones, c.m1 = (m[:, i, :] for i in range(8))
    c.levelT = [m[:, 8 + i, :] for i in range(LEVELS)]
    c.before = m[:, 13, :]
    c.masks = m
    c.small = sb("small", [P, 448])
    so = [0]

    def sm(n):
        so[0] += n
        assert so[0] <= 448
        return c.small[:, so[0] - n:so[0]]
    c.cst_in = sb("cst_in", [56, P])
    c.cst = sm(56)
    c.ssx, c.rx = sm(2), sm(2)
    c.alog, c.dtb, c.nea = sm(4), sm(4), sm(4)
    c.beta, c.z, c.zm, c.sp, c.g = (sm(8) for _ in range(5))
    c.rn = sm(16)
    c.run_sum, c.chunk_sum, c.bexp = sm(8), sm(8), sm(8)
    c.GL = sm(16)
    c.sums_exp = sm(32)
    c.sums_in = sm(32)
    c.negmax, c.esum, c.coef = sm(16), sm(16), sm(16)
    c.lam = sm(4)
    c.lamw = sm(2)
    c.row_in = {m: sm(1) for m, _ in PATHS}
    c.ss8, c.rb = sm(8), sm(8)
    c.ra = sm(8)
    c.rbias = sm(36)
    c.lamrows = sb("lamrows", [P, 4, DH])
    c.subln, c.gdng = sb("subln", [P, P]), sb("gdng", [P, P])
    c.rw = sb("rw", [P, KD, GROUPS + EXPERTS])
    c.offs = sb("offs", [1, EXPERTS + 1], I32)
    c.ps = ctx.enter_context(nc.psum_tensor("ps", [P, 8, 512], F32))

    c.side = [c.ps[:, 4:6, :].rearrange("p b f -> p (b f)"), c.ps[:, 6:8, :].rearrange("p b f -> p (b f)")]
    c.pair = [c.ps[:, 0:2, :].rearrange("p b f -> p (b f)"), c.ps[:, 2:4, :].rearrange("p b f -> p (b f)")]

    def sem(name):
        return ctx.enter_context(nc.semaphore(name))
    for_names = """x_loaded consts_loaded vectors_loaded lambda_loaded router_loaded gffn_loaded gfin_loaded out_stored
        ident_ready masks_ready iota_ready squares_ready
        ssx_ready rx_root h_ready h_transposed hT_ready cst_ready
        proj_ready side_ready
        conv_ready conv_sig qkv_ready gate_sig gate_ready beta_ready dec_exp g_in g_ready rn_root rn_ready
        q_normed k_normed gsum_ready gsum_exp g_scaled grow_pre grow_exp qdec_ready a_ready attnT_ready
        tok_ready b1_ready Y_ready TT_ready T_ready u_ready wT_ready
        dq_ready dk_ready dv_ready mg_ready
        negmax_ready exps_ready lam_in lam_exp aT_in aT_ready oa_out oa_squares oa_root ya_ready yaT_ready
        S_ready vn_ready ob_out ob_squares ob_root yb_ready ybT_ready
        branch_ready branch_used merged_ready mix_out x1_ready ss1_ready r1_root h2_ready h2_transposed h2T_ready
        logits_ready gexp_in gexp_out texp_in texp_out picks_ready ranks_ready offsets_ready onehot_ready comb_ready
        gathered HgT_ready
        window_ready gu_ready gate_sigmoid gated act_ready act_turned actT_ready S_half Se_ready down_ready out_copied row_in_ready
        scattered rows_turned rows_ready experts_used slot_of_ready ss2_in ss2_ready r2_root out_ready
        dve_chain act_chain pool_chain side_free0 side_free1 pair_free0 pair_free1 stage_loaded0 stage_loaded1""".split()
    c.s = {n: sem(n) for n in for_names}
    for i in range(RING):
        c.s[f"gateup{i}"] = sem(f"gateup{i}")
        c.s[f"down{i}"] = sem(f"down{i}")
    return c


def sync_program(sp, c, io):
    s = c.s
    sp.dma_start(c.x, io["x"].rearrange("b (t p) d -> p (b t) d", p=P)).then_inc(s["x_loaded"], 16)
    w_in = io["w_in"][0].rearrange("(k p) n -> p k n", p=P)

    def stage_free(i):
        if 2 <= i < NCH + 2:
            sp.wait_ge(s["proj_ready"], parts_before(i - 1))
            if i - 2 == CI["bdg"]:
                sp.wait_ge(s["side_ready"], SI["bd"] + 1)
        elif i >= NCH + 2:
            sp.wait_ge(s["branch_ready"], 2 * (i - NCH - 1))

    def load_chunk(i):
        _, col, n, _ = CHUNKS[i]
        stage_free(i)
        sp.dma_start(c.stage[i % 2][:, 0:KD * n].rearrange("p (k n) -> p k n", k=KD),
                     w_in[:, :, col:col + n]).then_inc(s[f"stage_loaded{i % 2}"], 16)

    def load_expert(e):
        slot = e % RING
        for flat, name, sem in ((c.gate_flat, "moe_w_gate", "gateup"), (c.up_flat, "moe_w_up", "gateup"),
                                (c.down_flat, "moe_w_down", "down")):
            k = 2 if name == "moe_w_down" else KD
            sp.dma_start(flat[slot], io[name][0, e].rearrange("(p k) f -> p (k f)", k=k)).then_inc(s[f"{sem}{slot}"], 16)

    for i in range(4):
        load_chunk(i)
    load_expert(0)
    load_chunk(4)
    load_expert(1)
    load_chunk(5)
    load_expert(2)
    for i in range(6, NCH):
        load_chunk(i)
    for j, name in enumerate(("w_branch_attn", "w_branch_gdn")):
        i = NCH + j
        stage_free(i)
        sp.dma_start(c.stage[i % 2][:, 0:4096].rearrange("p (k n) -> p k n", k=H),
                     io[name][0].rearrange("(k p) n -> p k n", p=P)).then_inc(s[f"stage_loaded{i % 2}"], 16)
    for j in range(2):
        i = NCH + 2 + j
        stage_free(i)
        sp.dma_start(c.stage[i % 2][:, 0:4096].rearrange("p (k n) -> p k n", k=KD),
                     io["w_out"][0].rearrange("(k p) n -> p k n", p=P)[:, :, j * 512:(j + 1) * 512])\
            .then_inc(s[f"stage_loaded{i % 2}"], 16)
    sp.wait_ge(s["ybT_ready"], 1)
    sp.wait_ge(s["side_ready"], len(SIDE))
    sp.wait_ge(s["yaT_ready"], 1)
    sp.dma_start(c.gffn, io["norm_ffn_gain"][0:1, :].partition_broadcast(P).rearrange("p a d -> p (a d)"))\
        .then_inc(s["gffn_loaded"], 16)
    load_expert(3)
    gate_d = io["moe_w_gate"][0].rearrange("e (p k) f -> p e (k f)", k=KD)
    up_d = io["moe_w_up"][0].rearrange("e (p k) f -> p e (k f)", k=KD)
    down_d = io["moe_w_down"][0].rearrange("e (p k) d -> p e (k d)", k=2)
    with sp.Fori(0, EXPERTS // RING - 1) as it:
        for j in range(RING):
            sp.wait_ge(s["experts_used"], it * RING + (j + 1))
            e = it * RING + (RING + j)
            for flat, src, sem in ((c.gate_flat, gate_d, "gateup"), (c.up_flat, up_d, "gateup"),
                                   (c.down_flat, down_d, "down")):
                sp.dma_start(flat[j], src[:, bass.ds(e, 1), :].rearrange("p a f -> p (a f)")).then_inc(s[f"{sem}{j}"], 16)
    outv = io["out"].rearrange("b (t p) d -> p (b t) d", p=P)
    for t in range(NT):
        sp.wait_ge(s["out_ready"], t + 1)
        sp.dma_start(outv[:, t, :], c.y[:, t, :]).then_inc(s["out_stored"], 16)
    sp.wait_ge(s["out_stored"], 16 * NT)


def gpsimd_program(pool, c, io):
    s = c.s
    n = [0]

    def settle(ins):
        n[0] += 1
        ins.then_inc(s["pool_chain"], 1)
        pool.wait_ge(s["pool_chain"], n[0])
    settle(pool.memset(c.masks[:, :, :], 0.0))
    pool.affine_select(out=c.ident, in_=c.ident, compare_op=ALU.not_equal, fill=1.0, base=0,
                       pattern=[[-1, P]], channel_multiplier=1).then_inc(s["ident_ready"], 1)
    odd = c.m1.rearrange("p (a b) -> p a b", b=2)[:, :, 0]
    settle(pool.affine_select(out=odd, in_=odd, compare_op=ALU.not_equal, fill=1.0, base=-1,
                              pattern=[[-2, P // 2]], channel_multiplier=1))
    for v in (c.upper, c.lower, c.chunk, c.half0, c.half1, c.ones, c.before):
        pool.memset(v, 1.0)
    tops = []
    for lv in range(LEVELS):
        w = 2 << lv
        top = c.levelT[lv].rearrange("p (a b f) -> p a b f", b=2, f=w)[:, :, 1, :]
        pool.memset(top, 1.0)
        tops.append((top, w))
    settle(pool.memset(c.vn[0], 0.0))
    settle(pool.memset(c.vn[1], 0.0))

    def keep(v, pattern, base, mult):
        return pool.affine_select(out=v, in_=v, compare_op=ALU.is_ge, fill=0.0, base=base, pattern=pattern,
                                  channel_multiplier=mult)
    nc2 = P // CHUNK
    for v in (c.upper, c.lower, c.chunk):
        keep(v.rearrange("p (a f) -> p a f", a=nc2), [[-CHUNK, nc2], [0, CHUNK]], 0, 1)
    for top, w in tops:
        keep(top, [[-2 * w, P // (2 * w)], [0, w]], 0, 1)
    keep(c.half0, [[0, P]], CHUNK - 1, -1)
    keep(c.half1, [[0, P]], -CHUNK, 1)
    settle(keep(c.before, [[1, P]], -1, -1))
    for v in (c.upper, c.lower, c.chunk):
        keep(v.rearrange("p (a f) -> p a f", a=nc2), [[CHUNK, nc2], [0, CHUNK]], CHUNK - 1, -1)
    for top, w in tops:
        last = keep(top, [[2 * w, P // (2 * w)], [0, w]], w - 1, -1)
    settle(last)
    keep(c.upper, [[1, P]], 0, -1)
    keep(c.lower, [[-1, P]], -1, 1).then_inc(s["masks_ready"], 1)
    for m, _ in PATHS:
        for q in range(P // m):
            settle(pool.iota(c.row_in[m][m * q:m * (q + 1)], [[0, 1]], base=0, channel_multiplier=1,
                             allow_small_or_imprecise_dtypes=True))
    pool.sem_inc(s["row_in_ready"], 1)
    pool.wait_ge(s["h_transposed"], 1)
    for i, (src, dst) in enumerate(((c.ck, c.sqk), (c.cq, c.sqq))):
        pool.wait_ge(s["qkv_ready"], i + 1)
        pool.tensor_tensor(dst, src, src, ALU.mult).then_inc(s["squares_ready"], 1)
    pool.wait_ge(s["mix_out"], 2 * NT)
    pool.iota(c.iota[:, :], [[1, SLOTS]], base=0, channel_multiplier=0,
              allow_small_or_imprecise_dtypes=True).then_inc(s["iota_ready"], 1)


def scalar_program(act, c, io):
    s = c.s
    n = [0]

    def chain(ins):
        n[0] += 1
        ins.then_inc(s["act_chain"], 1)

    def settle():
        act.wait_ge(s["act_chain"], n[0])

    act.dma_start(c.cst_in[0:8, :], io["norm_mix_gain"][0].rearrange("(k p) -> k p", p=P)).then_inc(s["consts_loaded"], 16)
    act.dma_start(c.cst_in[8:56, :], io["gdn_conv_w"][0].rearrange("j (b p) -> (j b) p", p=P)).then_inc(s["consts_loaded"], 16)

    def row(dst, src, sem):
        act.dma_start(dst, src.partition_broadcast(P).rearrange("p a d -> p (a d)")).then_inc(s[sem], 16)
    row(c.alog, io["gdn_a_log"][0:1, :], "vectors_loaded")
    row(c.dtb, io["gdn_dt_bias"][0:1, :], "vectors_loaded")
    row(c.subln[:, :], io["diff_subln_gain"][0:1, :], "vectors_loaded")
    row(c.gdng[:, :], io["gdn_norm_gain"][0:1, :], "vectors_loaded")
    for i, nm in enumerate(("q1", "k1", "q2", "k2")):
        row(c.lamrows[:, i, :], io[f"diff_lambda_{nm}"][0:1, :], "lambda_loaded")
    row(c.rbias[:, 0:GROUPS], io["moe_b_group"][0:1, :], "router_loaded")
    row(c.rbias[:, GROUPS:], io["moe_b_expert"][0:1, :], "router_loaded")
    act.dma_start(c.rw[:, :, 0:GROUPS], io["moe_w_group"][0].rearrange("(k p) g -> p k g", p=P)).then_inc(s["router_loaded"], 16)
    act.dma_start(c.rw[:, :, GROUPS:], io["moe_w_expert"][0].rearrange("(k p) g -> p k g", p=P)).then_inc(s["router_loaded"], 16)

    act.wait_ge(s["x_loaded"], 16)
    for t in range(NT):
        act.activation(c.hT[:, 0:4, :] if t == 0 else c.hT[:, 4:8, :], c.x[:, t, :].rearrange("p (a b) -> p a b", a=4),
                       ACT.Square, accum_out=c.ssx[:, t:t + 1]).then_inc(s["ssx_ready"], 1)
    act.wait_ge(s["ss2_in"], 1)
    act.activation(c.rx, c.ssx, ACT.Sqrt).then_inc(s["rx_root"], 1)
    act.wait_ge(s["cst_ready"], 1)
    act.wait_ge(s["h_transposed"], 1)
    act.wait_ge(s["ssx_ready"], NT)
    for k in (2, 3, 6, 7):
        act.activation(c.hT[:, k, :], c.ps[:, k // 2, (k % 2) * 256:(k % 2 + 1) * 256], ACT.Copy, scale=c.cst[:, k:k + 1]).then_inc(s["hT_ready"], 1)

    def conv_sigmoid(i, name, src):
        act.wait_ge(s["conv_ready"], i + 1)
        act.activation(c.sig[name], src, ACT.Sigmoid).then_inc(s["conv_sig"], 1)
    conv_sigmoid(0, "gk", c.ck)
    conv_sigmoid(1, "gq", c.cq)
    i = CI["bdg"]
    act.wait_ge(s["proj_ready"], parts_before(i) + PARTS[i])
    act.activation(c.flat["gate"], c.pair[i % 2], ACT.Sigmoid).then_inc(s["gate_sig"], 1)
    act.wait_ge(s["side_ready"], SI["bd"] + 1)
    bd = c.side[side_pair("bd")][:, 0:16].rearrange("p (t a h) -> p t a h", t=NT, a=2)
    act.activation(c.beta.rearrange("p (t h) -> p t h", t=NT), bd[:, :, 0, :], ACT.Sigmoid).then_inc(s["beta_ready"], 1)
    act.wait_ge(s["rn_root"], 1)
    act.activation(c.rn, c.rn, ACT.Sqrt).then_inc(s["rn_root"], 1)
    act.wait_ge(s["g_in"], 1)
    act.activation(c.z, c.z, ACT.Exp).then_inc(s["dec_exp"], 1)
    act.wait_ge(s["vectors_loaded"], 64)
    act.activation(c.nea, c.alog, ACT.Exp).then_inc(s["dec_exp"], 1)
    act.wait_ge(s["dec_exp"], 2)
    act.activation(c.z, c.z, ACT.Ln, bias=1.0).then_inc(s["dec_exp"], 1)
    act.wait_ge(s["lam_in"], 1)
    act.activation(c.lam[:, 2:4], c.lam[:, 0:2], ACT.Exp).then_inc(s["lam_exp"], 1)
    conv_sigmoid(2, "gv", c.cv)
    act.wait_ge(s["gsum_ready"], 1)
    act.activation(c.sums_exp, c.sums_in, ACT.Exp).then_inc(s["gsum_exp"], 1)
    act.wait_ge(s["grow_pre"], 2)
    act.activation(c.flat["EwT"], c.side[side_pair("grow")], ACT.Exp).then_inc(s[f"side_free{side_pair('grow')}"], 1)
    act.wait_ge(s["grow_pre"], 1)
    act.activation(c.flat["T"], c.flat["T"], ACT.Exp, scale=-1.0).then_inc(s["grow_exp"], 1)
    act.wait_ge(s["grow_pre"], 2)
    act.activation(c.flat["attnT"], c.flat["attnT"], ACT.Exp).then_inc(s["grow_exp"], 1)

    def evacuate(name, dst, sem, func):
        i = CI[name]
        act.wait_ge(s["proj_ready"], parts_before(i) + PARTS[i])
        act.activation(dst, c.pair[i % 2], func).then_inc(s[sem], 1)
        act.wait_ge(s[sem], {"dq_ready": 1, "dk_ready": 1, "dv_ready": 1}.get(sem, 0) or [None, "ma0", "ma1", "mb0", "mb1"].index(name))
        act.sem_inc(s[f"pair_free{i % 2}"], 1)
    evacuate("dq", c.flat["qT"], "dq_ready", ACT.Copy)
    evacuate("dk", c.flat["kT"], "dk_ready", ACT.Copy)
    evacuate("dv", c.flat["dv"], "dv_ready", ACT.Copy)
    evacuate("ma0", c.mg[0], "mg_ready", ACT.Sigmoid)

    def exps(qt):
        nk = P * (qt + 1)
        for m in range(2):
            act.wait_ge(s["negmax_ready"], 2 * qt + m + 1)
            pair = c.side[side_pair(f"s{qt}{m}")].rearrange("p (h k) -> p h k", h=H)
            for h in range(H):
                j = m * H + h
                ins = act.activation(c.es[:, j, 0:nk], pair[:, h, 0:nk], ACT.Exp, bias=c.negmax[:, 8 * qt + j:8 * qt + j + 1],
                                     scale=DH ** -0.5, accum_out=c.esum[:, 8 * qt + j:8 * qt + j + 1])
                ins.then_inc(s["exps_ready"], 1)
            act.wait_ge(s["exps_ready"], H * (2 * qt + m + 1))
            act.sem_inc(s[f"side_free{side_pair(f's{qt}{m}')}"], 1)
    act.wait_ge(s["TT_ready"], LEVELS + 1)
    exps(0)
    act.wait_ge(s["side_ready"], SI["wT"] + 1)
    evacuate("ma1", c.mg[1], "mg_ready", ACT.Sigmoid)
    act.wait_ge(s["aT_in"], 1)
    act.wait_ge(s["side_ready"], SI["aT0"] + 1)
    exps(1)
    evacuate("mb0", c.mg[2], "mg_ready", ACT.Sigmoid)

    def squares_root(src, sq, ss, ready, out_sem, root, rt):
        act.wait_ge(s[ready], 1)
        act.activation(sq, src, ACT.Square).then_inc(s[out_sem], 1)
        act.wait_ge(s[root], 1)
        act.activation(rt, ss, ACT.Sqrt).then_inc(s[root], 1)
    act.wait_ge(s["oa_out"], NT)
    act.activation(c.flat["Yb"], c.flat["F"], ACT.Square).then_inc(s["oa_squares"], 1)
    act.wait_ge(s["oa_root"], 1)
    act.activation(c.ra, c.ra, ACT.Sqrt).then_inc(s["oa_root"], 1)
    act.wait_ge(s["gate_ready"], 2)
    act.wait_ge(s["ob_out"], 4)
    act.activation(c.flat["A"], c.flat["TT"], ACT.Square).then_inc(s["ob_squares"], 1)
    act.wait_ge(s["ob_root"], 1)
    act.activation(c.rb, c.rb, ACT.Sqrt).then_inc(s["ob_root"], 1)
    act.wait_ge(s["yb_ready"], 1)
    evacuate("mb1", c.mg[3], "mg_ready", ACT.Sigmoid)
    act.wait_ge(s["side_ready"], SI["ybT"] + 1)
    act.activation(c.flat["kT"], c.side[side_pair("ybT")], ACT.Copy).then_inc(s["ybT_ready"], 1)

    for t in range(NT):
        act.wait_ge(s["x1_ready"], t + 1)
        act.activation(c.flat[("qT", "kT")[t]], c.x[:, t, :], ACT.Square, accum_out=c.ssx[:, t:t + 1])\
            .then_inc(s["ss1_ready"], 1)
    act.wait_ge(s["r1_root"], 1)
    act.activation(c.rx, c.ssx, ACT.Sqrt).then_inc(s["r1_root"], 1)
    act.wait_ge(s["ss1_ready"], 2)
    act.wait_ge(s["h2_transposed"], 1)
    for b in (1, 3):
        act.activation(c.h2T[:, 2 * b:2 * b + 2, :].rearrange("p a b -> p (a b)"), c.ps[:, 4 + b, :], ACT.Copy).then_inc(s["h2T_ready"], 1)
    act.wait_ge(s["gexp_in"], 1)
    act.activation(c.r[:, 72:80], c.r[:, 72:80], ACT.Exp).then_inc(s["gexp_out"], 1)
    act.wait_ge(s["texp_in"], 1)
    act.activation(c.r[:, 144:146], c.r[:, 144:146], ACT.Exp).then_inc(s["texp_out"], 1)
    for k in range(1, KD, 2):
        act.wait_ge(s["gathered"], k + 1)
        act.activation(c.HgT[:, k, 0:SLOTS], c.ps[:, k, :], ACT.Copy).then_inc(s["HgT_ready"], 1)

    act.wait_ge(s["offsets_ready"], 1)
    act.wait_ge(s["HgT_ready"], KD + 1)
    wide = act.value_load(c.offs[0:1, EXPERTS:EXPERTS + 1], min_val=0, max_val=TOK)

    def windows(m, nwin):
        n = HID * m // P
        nq = P // m

        def copy_window(expert, w, buf):
            off = act.value_load(c.offs[0:1, expert], min_val=0, max_val=SLOTS)
            act.activation(c.window[buf][:, 0:KD * m].rearrange("p (k s) -> p k s", k=KD),
                           c.HgT[:, :, bass.ds(off + w * m, m)], ACT.Copy).then_inc(s["window_ready"], 1)

        def units(base, first):
            for u in range(RING * nwin):
                act.wait_ge(s["gu_ready"], base * nwin + (u + 1))
                need(act, s["act_ready"], base * nwin + (u - 1), first)
                act.activation(c.sg[u % 2][:, 0:n], c.ps[:, u % 2, 0:n], ACT.Sigmoid).then_inc(s["gate_sigmoid"], 1)
                nxt = u + 1
                e = base + nxt // nwin
                copy_window(slice(e, e + 1) if first else bass.ds(e, 1), nxt % nwin, nxt % 2)
                act.wait_ge(s["act_turned"], base * nwin + (u + 1))
                need(act, s["down_ready"], base * nwin + (u - 1), first)
                if nq == 4:
                    act.activation(c.actT[u % 2][0:64, 0:64], c.ps[0:64, u % 2, 0:64], ACT.Copy)
                    act.activation(c.actT[u % 2][64:P, 0:64], c.ps[64:P, u % 2, 64:P], ACT.Copy).then_inc(s["actT_ready"], 1)
                else:
                    act.activation(c.actT[u % 2][:, 0:2 * m], c.ps[:, u % 2, 0:2 * m], ACT.Copy).then_inc(s["actT_ready"], 1)
                act.wait_ge(s["down_ready"], base * nwin + (u + 1))
                stack_rows(act.activation, c, m, u, range(nq // 2, nq) if nq > 1 else (1,), s["out_copied"], ACT.Copy)
        copy_window(slice(0, 1), 0, 0)
        units(0, True)
        with act.Fori(1, EXPERTS // RING) as it:
            units(it * RING, False)
    by_count(act, wide, windows)

    for t in range(NT):
        act.wait_ge(s["ss2_in"], t + 2)
        act.activation(c.HgT[:, 2 * t:2 * t + 2, 0:512],
                       c.x[:, t, :].rearrange("p (a b) -> p a b", a=2), ACT.Square, accum_out=c.ssx[:, t:t + 1])\
            .then_inc(s["ss2_ready"], 1)
        act.wait_ge(s["r2_root"], 2 * t + 1)
        act.activation(c.rx[:, t:t + 1], c.ssx[:, t:t + 1], ACT.Sqrt).then_inc(s["r2_root"], 1)


def stack_buffer(nq, u):
    return u // nq % 2 if nq < RING else 0


def stack_rows(copy, c, m, u, parts, done, *func):
    nq = P // m
    if nq == 1:
        (i,) = parts
        copy(c.Y[u % 2][:, 512 * i:512 * (i + 1)], c.ps[:, 2 + i, :], *func).then_inc(done, 1)
        return
    w = D // nq
    at = u % nq * m
    for q in parts:
        last = copy(c.Y[stack_buffer(nq, u)][at:at + m, w * q:w * (q + 1)], c.ps[q * m:(q + 1) * m, 2 + u % 2, 0:w], *func)
    last.then_inc(done, 1)


def need(eng, sem, value, first):
    if not first or value > 0:
        eng.wait_ge(sem, value)


def by_count(eng, largest, windows):
    (m0, n0), (m1, n1), (m2, n2) = PATHS
    with eng.If(largest <= m0):
        windows(m0, n0)
    with eng.Else():
        with eng.If(largest <= m1):
            windows(m1, n1)
        with eng.Else():
            windows(m2, n2)


def tensor_program(pe, c, io):
    s = c.s
    T4 = [(t, h) for t in range(NT) for h in range(H)]

    def side(name):
        v = side_reuse(name)
        if v:
            pe.wait_ge(s[f"side_free{side_pair(name)}"], v)
        return c.side[side_pair(name)]

    def blk(ap, i, n=P):
        return ap[:, i * n:(i + 1) * n]

    pe.wait_ge(s["ident_ready"], 1)
    pe.wait_ge(s["consts_loaded"], 32)
    ps = side("consts")
    pe.transpose(ps[:, 0:56], c.cst_in[:, :], c.ident[0:56, 0:56]).then_inc(s["side_ready"], 1)
    for t in range(NT):
        pe.wait_ge(s["h_ready"], t + 1)
        for k in range(KD):
            last = pe.transpose(c.ps[:, k // 2, (k % 2) * 256 + t * P:(k % 2) * 256 + (t + 1) * P],
                                c.h[:, t, k * P:(k + 1) * P], c.ident)
    last.then_inc(s["h_transposed"], 1)

    def project(name, part):
        i = CI[name]
        _, _, n, kind = CHUNKS[i]
        w = c.stage[i % 2][:, 0:KD * n].rearrange("p (k n) -> p k n", k=KD)
        if part == 0:
            pe.wait_ge(s[f"stage_loaded{i % 2}"], 16 * (i // 2 + 1))
            if i >= 2:
                pe.wait_ge(s[f"pair_free{i % 2}"], i // 2)
        for k in range(KD):
            if kind == "T":
                out, lhs, rhs = blk(c.pair[i % 2], part, TOK), w[:, k, part * P:(part + 1) * P], c.hT[:, k, :]
            else:
                out, lhs, rhs = blk(c.pair[i % 2], part, 512), c.hT[:, k, part * P:(part + 1) * P], w[:, k, n - 512:n]
            last = pe.matmul(out, lhs, rhs, start=(k == 0), stop=(k == KD - 1))
        last.then_inc(s["proj_ready"], 1)

    def turn(name, src):
        ps = side(name)
        for i in range(8):
            last = pe.transpose(blk(ps, i), src(i), c.ident)
        last.then_inc(s["side_ready"], 1)

    def each(name, lhs, rhs):
        ps = side(name)
        for i, (t, h) in enumerate(T4):
            last = pe.matmul(blk(ps, i), lhs(t, h), rhs(t, h), start=True, stop=True)
        last.then_inc(s["side_ready"], 1)

    def tile(ap, h, t):
        return ap[:, h, t * P:(t + 1) * P]

    pe.wait_ge(s["hT_ready"], KD)
    for name in ("gk", "gq"):
        for b in range(4):
            project(name, b)
    project("bdg", 0)
    project("bdg", 1)
    i = CI["bdg"]
    wbd = c.stage[i % 2][:, 0:KD * 520].rearrange("p (k n) -> p k n", k=KD)
    ps = side("bd")
    for t in range(NT):
        for k in range(KD):
            last = pe.matmul(ps[:, 8 * t:8 * t + 8], c.hT[:, k, t * P:(t + 1) * P], wbd[:, k, 0:8],
                             start=(k == 0), stop=(k == KD - 1))
    last.then_inc(s["side_ready"], 1)
    project("gv", 0)
    project("gv", 1)
    ps = side("ss")
    pe.wait_ge(s["masks_ready"], 1)
    for j, sq in enumerate((c.sqk, c.sqq)):
        pe.wait_ge(s["squares_ready"], j + 1)
        for i, (t, h) in enumerate(T4):
            last = pe.matmul(ps[:, 8 * j + i:8 * j + i + 1], tile(sq, h, t), c.ones[:, 0:1], start=True, stop=True)
    last.then_inc(s["side_ready"], 1)
    project("gv", 2)
    pe.wait_ge(s["rn_ready"], 1)
    for j, name in enumerate(("rnk", "rnq")):
        each(name, lambda t, h, j=j: c.rn[:, 8 * j + 4 * t + h:8 * j + 4 * t + h + 1].to_broadcast([P, P]), lambda t, h: c.ident)
    project("gv", 3)
    ps = side("gsum")
    pe.wait_ge(s["g_ready"], 1)
    for t in range(NT):
        g = c.g[:, 4 * t:4 * t + 4]
        pe.matmul(ps[:, 4 * t:4 * t + 4], c.upper, g, start=True, stop=True)
        pe.matmul(ps[:, 8 + 4 * t:12 + 4 * t], c.chunk, g, start=True, stop=True)
        pe.matmul(ps[:, 16 + 8 * t:20 + 8 * t], c.half0, g, start=True, stop=True)
        last = pe.matmul(ps[:, 20 + 8 * t:24 + 8 * t], c.half1, g, start=True, stop=True)
    last.then_inc(s["side_ready"], 1)
    each("grow", lambda t, h: c.g[:, 4 * t + h:4 * t + h + 1].to_broadcast([P, P]), lambda t, h: c.upper)
    project("dq", 0)
    pe.wait_ge(s["k_normed"], 1)
    each("gram", lambda t, h: tile(c.ck, h, t), lambda t, h: tile(c.ck, h, t))
    project("dq", 1)
    pe.wait_ge(s["q_normed"], 1)
    each("intra", lambda t, h: tile(c.ck, h, t), lambda t, h: tile(c.cq, h, t))
    project("dq", 2)
    turn("ktok", lambda i: tile(c.ck, i % 4, i // 4))
    project("dq", 3)
    pe.wait_ge(s["qkv_ready"], 3)
    turn("vtok", lambda i: tile(c.cv, i % 4, i // 4))
    project("dk", 0)
    pe.wait_ge(s["b1_ready"], 1)
    turn("b1", lambda i: c.Yb[:, i // 4, i % 4, :])
    project("dk", 1)

    def level_y(lv):
        pe.wait_ge(s["TT_ready"], lv)
        each(f"Y{lv}", lambda t, h: c.A[:, t, h, :], lambda t, h: c.TT[:, t, h, :])

    def level_t(lv):
        pe.wait_ge(s["Y_ready"], lv)
        pe.wait_ge(s["T_ready"], lv)
        each(f"TT{lv}", lambda t, h: c.T[:, t, h, :], lambda t, h: c.Yb[:, t, h, :])
        if lv < LEVELS:
            each(f"T{lv}", lambda t, h: c.Yb[:, t, h, :], lambda t, h: c.T[:, t, h, :])
    level_y(1)
    project("dk", 2)
    level_t(1)
    project("dk", 3)
    level_y(2)
    project("dv", 0)
    level_t(2)
    project("dv", 1)
    level_y(3)
    project("ma0", 0)
    level_t(3)
    project("ma0", 1)
    level_y(4)
    project("ma0", 2)
    level_t(4)
    project("ma0", 3)
    level_y(5)
    project("ma1", 0)
    level_t(5)
    project("ma1", 1)
    pe.wait_ge(s["TT_ready"], LEVELS + 1)
    pe.wait_ge(s["tok_ready"], 3)
    each("u", lambda t, h: c.TT[:, t, h, :], lambda t, h: c.vb[:, t, h, :])
    each("wT", lambda t, h: c.wrhs[:, t, h, :], lambda t, h: c.TT[:, t, h, :])

    def scores(qt):
        pe.wait_ge(s["dq_ready"], 1)
        pe.wait_ge(s["dk_ready"], 1)
        for m in range(2):
            ps = side(f"s{qt}{m}").rearrange("p (h k) -> p h k", h=H)
            rows = slice(DH * m, DH * (m + 1))
            for h in range(H):
                last = pe.matmul(ps[:, h, 0:P * (qt + 1)], c.qT[rows, h, qt * P:(qt + 1) * P],
                                 c.kT[rows, h, 0:P * (qt + 1)], start=True, stop=True)
            last.then_inc(s["side_ready"], 1)

    def turn_probs(qt):
        ps = side(f"aT{qt}")
        pe.wait_ge(s["aT_in"], qt + 1)
        for h in range(H):
            for kt in range(qt + 1):
                last = pe.transpose(blk(ps, h * (qt + 1) + kt), c.es[:, h, kt * P:(kt + 1) * P], c.ident)
        last.then_inc(s["side_ready"], 1)

    def weigh_values(qt):
        ps = side(f"oa{qt}")
        pe.wait_ge(s["aT_ready"], qt + 1)
        pe.wait_ge(s["dv_ready"], 1)
        for h in range(H):
            for kt in range(qt + 1):
                last = pe.matmul(blk(ps, h), blk(c.aT, h * (qt + 1) + kt), c.dv[:, kt, h * P:(h + 1) * P],
                                 start=(kt == 0), stop=(kt == qt))
        last.then_inc(s["side_ready"], 1)

    def state_in(n):
        ps = side(f"ws{n}")
        pe.wait_ge(s["S_ready"], n)
        for h in range(H):
            last = pe.matmul(blk(ps, h), c.wT[:, n // 2, h, :], c.S[:, h, :], start=True, stop=True)
        last.then_inc(s["side_ready"], 1)

    def state_out(n):
        t = n // 2
        ps = side(f"so{n}")
        pe.wait_ge(s["vn_ready"], n + 1)
        for h in range(H):
            if n:
                pe.matmul(blk(ps, h), c.qdec[:, t, h, :], c.S[:, h, :], start=True, stop=False)
            last = pe.matmul(blk(ps, h), c.attnT[:, t, h, :], c.vn[n % 2][:, h, :], start=(n == 0), stop=True)
        if n < 3:
            for h in range(H):
                last = pe.matmul(blk(ps, H + h), c.kdec[:, t, h, :], c.vn[n % 2][:, h, :], start=True, stop=True)
        last.then_inc(s["side_ready"], 1)

    scores(0)
    project("ma1", 2)
    pe.wait_ge(s["wT_ready"], 1)
    state_out(0)
    project("ma1", 3)
    turn_probs(0)
    state_in(1)
    project("mb0", 0)
    weigh_values(0)
    state_out(1)
    project("mb0", 1)
    scores(1)
    state_in(2)
    project("mb0", 2)
    state_out(2)
    turn_probs(1)
    project("mb0", 3)
    state_in(3)
    weigh_values(1)
    project("mb1", 0)
    state_out(3)
    project("mb1", 1)
    pe.wait_ge(s["ya_ready"], 1)
    turn("yaT", lambda i: c.oa[:, i % 2, (i // 2) * P:(i // 2 + 1) * P])
    project("mb1", 2)
    project("mb1", 3)
    pe.wait_ge(s["yb_ready"], 1)
    turn("ybT", lambda i: c.ob[:, i % 2, (i // 2) * P:(i // 2 + 1) * P])

    for j, yT in enumerate((c.yaT, c.ybT)):
        i = NCH + j
        w = c.stage[i % 2][:, 0:4096].rearrange("p (k n) -> p k n", k=H)
        pe.wait_ge(s[f"stage_loaded{i % 2}"], 16 * (i // 2 + 1))
        pe.wait_ge(s["yaT_ready" if j == 0 else "ybT_ready"], 1)
        if j == 0:
            for q in range(2):
                pe.wait_ge(s[f"pair_free{q}"], (NCH + 1 - q) // 2)
        for half in range(2):
            n = 2 * j + half
            if n >= 2:
                pe.wait_ge(s["branch_used"], n - 1)
            for b in range(4):
                for k in range(H):
                    last = pe.matmul(blk(c.pair[half], b, TOK), w[:, k, (4 * half + b) * P:(4 * half + b + 1) * P], yT[:, k, :],
                                     start=(k == 0), stop=(k == H - 1))
            last.then_inc(s["branch_ready"], 1)
    pe.wait_ge(s["ybT_ready"], 1)
    pe.wait_ge(s["yaT_ready"], 1)
    pe.wait_ge(s["merged_ready"], 2)
    for half in range(2):
        i = NCH + 2 + half
        w = c.stage[i % 2][:, 0:4096].rearrange("p (k n) -> p k n", k=KD)
        pe.wait_ge(s[f"stage_loaded{i % 2}"], 16 * (i // 2 + 1))
        for t in range(NT):
            for k in range(KD):
                mg = c.mg[k // 4][:, (k % 4) * TOK + t * P:(k % 4) * TOK + (t + 1) * P]
                last = pe.matmul(c.ps[:, 4 + 2 * t + half, :], mg, w[:, k, :], start=(k == 0), stop=(k == KD - 1))
            last.then_inc(s["mix_out"], 1)

    for t in range(NT):
        pe.wait_ge(s["h2_ready"], t + 1)
        for k in range(KD):
            last = pe.transpose(c.ps[:, 4 + k // 2, (k % 2) * 256 + t * P:(k % 2) * 256 + (t + 1) * P],
                                c.h2[:, t, k * P:(k + 1) * P], c.ident)
    last.then_inc(s["h2_transposed"], 1)
    pe.wait_ge(s["h2T_ready"], 4)
    pe.wait_ge(s["router_loaded"], 64)
    for t in range(NT):
        for k in range(KD):
            last = pe.matmul(c.ps[:, 0, 36 * t:36 * (t + 1)], c.h2T[:, k, t * P:(t + 1) * P], c.rw[:, k, :],
                             start=(k == 0), stop=(k == KD - 1))
    last.then_inc(s["logits_ready"], 1)
    pe.wait_ge(s["picks_ready"], 1)
    picks = c.r[:, 240:304]
    pe.matmul(c.ps[:, 1, 0:32], c.before, picks[:, 0:32], start=True, stop=True)
    pe.matmul(c.ps[:, 1, 32:64], c.before, picks[:, 32:64], start=True, stop=False)
    pe.matmul(c.ps[:, 1, 32:64], c.ones, picks[:, 0:32], start=False, stop=True)
    pe.matmul(c.ps[:, 1, 64:96], c.ones, picks[:, 0:32], start=True, stop=False)
    pe.matmul(c.ps[:, 1, 64:96], c.ones, picks[:, 32:64], start=False, stop=True).then_inc(s["ranks_ready"], 1)
    pe.wait_ge(s["onehot_ready"], 2)
    for k in range(KD):
        for t in range(NT):
            last = pe.matmul(c.ps[:, k, :], c.h2[:, t, k:D:KD], c.onehot[:, t, :], start=(t == 0), stop=(t == NT - 1))
        last.then_inc(s["gathered"], 1)

    pe.wait_ge(s["HgT_ready"], KD + 1)
    for i in range(8):
        last = pe.matmul(blk(c.side[0], i), c.r[:, 480 + i:481 + i].to_broadcast([P, P]), c.ident, start=True, stop=True)
    last.then_inc(s["rows_turned"], 1)
    pe.wait_ge(s["rows_ready"], 1)
    any_row = c.masks[:, 1:5, :].rearrange("p a f -> p (a f)")
    for b in range(4):
        pe.matmul(c.ps[:, 4 + b, :], c.levelT[0], any_row, start=True, stop=False, skip_group_check=True)
    wide = pe.value_load(c.offs[0:1, EXPERTS:EXPERTS + 1], min_val=0, max_val=TOK)

    def windows(m, nwin):
        nq = P // m
        n = HID // nq

        def quad(q):
            return slice(q * m, (q + 1) * m)

        def hidden(base, u, first):
            j = u // nwin % RING
            pe.wait_ge(s["window_ready"], base * nwin + (u + 1))
            if u % nwin == 0:
                rnd = u // nwin // RING
                pe.wait_ge(s[f"gateup{j}"], base * (32 // RING) + 32 * (rnd + 1))
            need(pe, s["actT_ready"], base * nwin + (u - 1), first)
            for k in range(KD):
                for q in range(nq):
                    start, step = {4: (P * (q // 2) + q % 2, 2), 2: (q, 2), 1: (0, 1)}[nq]
                    last = pe.matmul(c.ps[quad(q), u % 2, 0:2 * n], c.window[u % 2][:, k * m:(k + 1) * m],
                                     c.gu_w[j][:, :, k, start:start + step * (n - 1) + 1:step],
                                     start=(k == 0), stop=(k == KD - 1))
            last.then_inc(s["gu_ready"], 1)

        def turn_act(base, u):
            pe.wait_ge(s["act_ready"], base * nwin + (u + 1))
            act, bank = c.act[u % 2], u % 2
            if nq == 4:
                for r in range(2):
                    last = pe.matmul(c.ps[64 * r:64 * r + 64, bank, 0:P], act[:, 0:64], c.ident, start=True, stop=True)
            elif nq == 2:
                last = pe.transpose(c.ps[:, bank, 0:P], act[:, 0:P], c.ident)
            else:
                for kk in range(2):
                    last = pe.transpose(c.ps[:, bank, kk * P:(kk + 1) * P], act[:, kk:HID:2], c.ident)
            last.then_inc(s["act_turned"], 1)

        def down(base, u, first):
            j = u // nwin % RING
            if u % nwin == 0:
                pe.wait_ge(s[f"down{j}"], base * (16 // RING) + 16)
            pe.wait_ge(s["actT_ready"], base * nwin + (u + 1))
            need(pe, s["out_copied"], 2 * base * nwin + 2 * (u - 1 if m < P else u), first)
            width = min(512, D // nq)
            for piece in range(D // nq // width):
                for kk in range(2):
                    for q in range(nq):
                        at = q * (D // nq) + piece * width
                        last = pe.matmul(c.ps[quad(q), out_bank(m, u) + piece, 0:width], c.actT[u % 2][:, kk * m:(kk + 1) * m],
                                         c.down_w[j][:, kk, at:at + width], start=(kk == 0), stop=(kk == 1))
            last.then_inc(s["down_ready"], 1)

        def scatter(rnd, u):
            pe.wait_ge(s["out_copied"], rnd * (2 * RING * nwin) + 2 * (u + 1))
            pe.wait_ge(s["Se_ready"], rnd * (RING * nwin // nq) + (u + 1) // nq)
            i = stack_buffer(nq, u % (RING * nwin))
            for half in range(2):
                for t in range(NT):
                    last = pe.matmul(y_out(c, half, t), c.S_e[i][:, t * P:(t + 1) * P], c.Y[i][:, 512 * half:512 * (half + 1)],
                                     start=False, stop=False, skip_group_check=True)
            last.then_inc(s["scattered"], 1)

        def units(rnd, first, final):
            nu = RING * nwin
            base = rnd * RING
            for u in range(nu):
                if not (final and u == nu - 1):
                    hidden(base, u + 1, first)
                turn_act(base, u)
                if u % nq == 0 and not (first and base + u == 0):
                    scatter(rnd, u - 1)
                down(base, u, first)
            if final:
                scatter(rnd, nu - 1)
        hidden(0, 0, True)
        units(0, True, False)
        with pe.Fori(1, EXPERTS // RING - 1) as it:
            units(it, False, False)
        units(EXPERTS // RING - 1, True, True)
    by_count(pe, wide, windows)


def y_out(c, half, t):
    return c.ps[:, 4 + 2 * t + half, :]


def out_bank(m, u):
    return 2 + u % 2 if m < P else 2


def vector_program(v, c, io):
    s = c.s
    n = [0]

    def chain(ins):
        n[0] += 1
        ins.then_inc(s["dve_chain"], 1)

    def settle():
        v.wait_ge(s["dve_chain"], n[0])

    def col(ap, i):
        return ap[:, i:i + 1]

    def blk(ap, i, w=P):
        return ap[:, i * w:(i + 1) * w]

    def side(name):
        v.wait_ge(s["side_ready"], SI[name] + 1)
        return c.side[side_pair(name)]

    def side_done(name, ins):
        ins.then_inc(s[f"side_free{side_pair(name)}"], 1)

    v.wait_ge(s["ssx_ready"], NT)
    v.tensor_scalar(c.ssx, c.ssx, 1.0 / D, EPS, ALU.mult, ALU.add).then_inc(s["ss2_in"], 1)
    v.wait_ge(s["rx_root"], 1)
    chain(v.reciprocal(c.rx, c.rx))
    settle()
    for t in range(NT):
        v.tensor_scalar(c.h[:, t, :], c.x[:, t, :], col(c.rx, t), None, ALU.mult).then_inc(s["h_ready"], 1)
    ps = side("consts")
    v.tensor_copy(c.cst, ps[:, 0:56]).then_inc(s["cst_ready"], 1)
    v.wait_ge(s["cst_ready"], 1)
    v.sem_inc(s[f"side_free{side_pair('consts')}"], 1)
    v.wait_ge(s["h_transposed"], 1)
    for k in (0, 1, 4, 5):
        v.tensor_scalar(c.hT[:, k, :], c.ps[:, k // 2, (k % 2) * 256:(k % 2 + 1) * 256], col(c.cst, k), None, ALU.mult).then_inc(s["hT_ready"], 1)

    def conv(name, dst, first):
        i = CI[name]
        v.wait_ge(s["proj_ready"], parts_before(i) + 4)
        src = c.pair[i % 2]
        for back in range(TAPS):
            for b in range(4):
                w = col(c.cst, 8 + 12 * (TAPS - 1 - back) + first + b)
                if back == 0:
                    ins = v.tensor_scalar(dst[:, b, :], blk(src, b, TOK), w, None, ALU.mult)
                else:
                    o = dst[:, b, back:TOK]
                    ins = v.scalar_tensor_tensor(out=o, in0=src[:, b * TOK:(b + 1) * TOK - back], scalar=w, in1=o,
                                                 op0=ALU.mult, op1=ALU.add)
                if back == TAPS - 1 and b == 3:
                    ins.then_inc(s[f"pair_free{i % 2}"], 1)
                else:
                    chain(ins)
            if back < TAPS - 1:
                settle()
        v.wait_ge(s[f"pair_free{i % 2}"], i // 2 + 1)
        settle()
        v.sem_inc(s["conv_ready"], 1)

    def silu(j, name, dst):
        v.wait_ge(s["conv_sig"], j + 1)
        v.tensor_tensor(dst, dst, c.sig[name], ALU.mult).then_inc(s["qkv_ready"], 1)
    conv("gk", c.ck, 4)
    silu(0, "gk", c.ck)
    conv("gq", c.cq, 0)
    silu(1, "gq", c.cq)
    i = CI["bdg"]
    v.wait_ge(s["gate_sig"], 1)
    v.tensor_tensor(c.flat["gate"], c.flat["gate"], c.pair[i % 2], ALU.mult).then_inc(s["gate_ready"], 1)
    v.wait_ge(s["gate_ready"], 1)
    v.sem_inc(s[f"pair_free{i % 2}"], 1)
    v.wait_ge(s["vectors_loaded"], 64)
    bd = side("bd")[:, 0:16].rearrange("p (t a h) -> p t a h", t=NT, a=2)
    v.wait_ge(s["beta_ready"], 1)
    for t in range(NT):
        chain(v.tensor_tensor(blk(c.z, t, 4), bd[:, t, 1, :], c.dtb, ALU.add))
    settle()
    v.sem_inc(s[f"side_free{side_pair('bd')}"], 1)
    chain(v.tensor_scalar(c.zm, c.z, 0.0, None, ALU.max))
    settle()
    v.scalar_tensor_tensor(out=c.z, in0=c.zm, scalar=-2.0, in1=c.z, op0=ALU.mult, op1=ALU.add).then_inc(s["g_in"], 1)
    v.wait_ge(s["lambda_loaded"], 64)
    chain(v.tensor_tensor(c.lamrows[:, 0, :], c.lamrows[:, 0, :], c.lamrows[:, 1, :], ALU.mult))
    chain(v.tensor_tensor(c.lamrows[:, 2, :], c.lamrows[:, 2, :], c.lamrows[:, 3, :], ALU.mult))
    settle()
    v.tensor_reduce(c.lam[:, 0:2], c.lamrows[:, 0:4:2, :], AX_X, ALU.add).then_inc(s["lam_in"], 1)
    ps = side("ss")
    v.tensor_scalar(c.rn, ps[:, 0:16], EPS, None, ALU.add).then_inc(s["rn_root"], 1)
    v.wait_ge(s["rn_root"], 2)
    chain(v.reciprocal(c.rn, c.rn))
    settle()
    v.tensor_scalar(c.rn[:, 8:16], c.rn[:, 8:16], float(P) ** -0.5, None, ALU.mult).then_inc(s["rn_ready"], 1)
    v.sem_inc(s[f"side_free{side_pair('ss')}"], 1)
    v.wait_ge(s["dec_exp"], 3)
    chain(v.tensor_tensor(c.sp, c.zm, c.z, ALU.add))
    settle()
    for t in range(NT):
        last = v.scalar_tensor_tensor(out=blk(c.g, t, 4), in0=blk(c.sp, t, 4), scalar=-1.0, in1=c.nea, op0=ALU.mult, op1=ALU.mult)
        if t == 0:
            chain(last)
    last.then_inc(s["g_ready"], 1)
    conv("gv", c.cv, 8)
    silu(2, "gv", c.cv)
    for name, dst, sem in (("rnk", c.ck, "k_normed"), ("rnq", c.cq, "q_normed")):
        ps = side(name).rearrange("p (t h f) -> p t h f", t=NT, h=H)
        for t in range(NT):
            d = dst[:, :, t * P:(t + 1) * P]
            last = v.tensor_tensor(d, d, ps[:, t], ALU.mult)
            if t == 0:
                chain(last)
        side_done(name, last)
        v.wait_ge(s[f"side_free{side_pair(name)}"], side_reuse(name) + 1)
        settle()
        v.sem_inc(s[sem], 1)
    ps = side("gsum")
    chain(v.tensor_copy(c.run_sum, ps[:, 0:8]))
    chain(v.tensor_copy(c.chunk_sum, ps[:, 8:16]))
    chain(v.tensor_copy(c.sums_in[:, 0:8], ps[:, 0:8]))
    side_done("gsum", v.tensor_copy(c.sums_in[:, 16:32], ps[:, 16:32]))
    settle()
    v.wait_ge(s[f"side_free{side_pair('gsum')}"], side_reuse("gsum") + 1)
    v.tensor_tensor(c.sums_in[:, 8:16], c.chunk_sum, c.run_sum, ALU.subtract).then_inc(s["gsum_ready"], 1)
    ps = side("grow")
    v.wait_ge(s["squares_ready"], 2)
    v.wait_ge(s["side_ready"], SI["ss"] + 1)
    for j, (buf, op) in enumerate((("T", ALU.max), ("attnT", ALU.min))):
        for i in range(8):
            last = v.tensor_scalar(blk(c.flat[buf], i), blk(ps, i), col(c.run_sum, i), 0.0, ALU.subtract, op)
            if i < 7:
                chain(last)
        last.then_inc(s["grow_pre"], 1)
    def masked(buf, mask):
        return v.tensor_tensor(c.flat[buf].rearrange("p (a f) -> p a f", a=8), c.flat[buf].rearrange("p (a f) -> p a f", a=8),
                               mask.rearrange("p (a f) -> p a f", a=1).to_broadcast([P, 8, P]), ALU.mult)
    v.wait_ge(s["grow_exp"], 1)
    v.wait_ge(s["masks_ready"], 1)
    chain(masked("T", c.lower))
    v.wait_ge(s["grow_exp"], 2)
    chain(masked("attnT", c.upper))
    settle()
    v.wait_ge(s["gsum_exp"], 1)
    chain(v.tensor_tensor(c.bexp, c.beta, c.sums_exp[:, 0:8], ALU.mult))
    ps = side("gram")
    for i in range(8):
        last = v.scalar_tensor_tensor(out=blk(c.flat["A"], i), in0=blk(ps, i), scalar=col(c.beta, i), in1=blk(c.flat["T"], i),
                                      op0=ALU.mult, op1=ALU.mult)
        if i < 7:
            chain(last)
    side_done("gram", last)
    ps = side("intra")
    side_done("intra", v.tensor_tensor(c.flat["attnT"], c.flat["attnT"], ps, ALU.mult))
    v.wait_ge(s[f"side_free{side_pair('gram')}"], side_reuse("gram") + 1)
    settle()
    A8, Y8 = (c.flat[x].rearrange("p (a f) -> p a f", a=8) for x in ("A", "Yb"))
    T8, TT8 = (c.flat[x].rearrange("p (a f) -> p a f", a=8) for x in ("T", "TT"))

    def all8(m):
        return m.rearrange("p (a f) -> p a f", a=1).to_broadcast([P, 8, P])
    v.tensor_tensor(Y8, A8, all8(c.m1), ALU.mult).then_inc(s["b1_ready"], 1)
    cq4 = c.cq.rearrange("p h (t f) -> p h t f", t=NT)
    ps = side("ktok")
    for i in range(8):
        chain(v.tensor_scalar(blk(c.flat["wrhs"], i), blk(ps, i), col(c.bexp, i), None, ALU.mult))
    for i in range(8):
        last = v.tensor_scalar(blk(c.flat["kdec"], i), blk(ps, i), col(c.sums_exp, 8 + i), None, ALU.mult)
        if i < 7:
            chain(last)
    side_done("ktok", last)
    v.wait_ge(s[f"side_free{side_pair('ktok')}"], side_reuse("ktok") + 1)
    settle()
    v.sem_inc(s["tok_ready"], 2)
    ps = side("vtok")
    for i in range(8):
        last = v.tensor_scalar(blk(c.flat["vb"], i), blk(ps, i), col(c.beta, i), None, ALU.mult)
        if i < 7:
            chain(last)
    side_done("vtok", last)
    v.wait_ge(s[f"side_free{side_pair('vtok')}"], side_reuse("vtok") + 1)
    settle()
    v.sem_inc(s["tok_ready"], 1)
    v.wait_ge(s["b1_ready"], 1)
    v.tensor_tensor(T8, all8(c.ident), Y8, ALU.subtract).then_inc(s["T_ready"], 1)
    ps = side("b1")
    last = v.tensor_tensor(TT8, all8(c.ident), ps.rearrange("p (a f) -> p a f", a=8), ALU.subtract)
    last.then_inc(s["TT_ready"], 1)
    v.wait_ge(s["TT_ready"], 1)
    v.sem_inc(s[f"side_free{side_pair('b1')}"], 1)
    for lv in range(1, LEVELS + 1):
        ps = side(f"Y{lv}").rearrange("p (a f) -> p a f", a=8)
        v.tensor_tensor(Y8, ps, all8(c.levelT[lv - 1]), ALU.mult).then_inc(s["Y_ready"], 1)
        v.wait_ge(s["Y_ready"], lv)
        v.sem_inc(s[f"side_free{side_pair(f'Y{lv}')}"], 1)
        ps = side(f"TT{lv}")
        v.tensor_tensor(c.flat["TT"], c.flat["TT"], ps, ALU.subtract).then_inc(s["TT_ready"], 1)
        v.wait_ge(s["TT_ready"], lv + 1)
        v.sem_inc(s[f"side_free{side_pair(f'TT{lv}')}"], 1)
        if lv < LEVELS:
            ps = side(f"T{lv}")
            v.tensor_tensor(c.flat["T"], c.flat["T"], ps, ALU.subtract).then_inc(s["T_ready"], 1)
            v.wait_ge(s["T_ready"], lv + 1)
            v.sem_inc(s[f"side_free{side_pair(f'T{lv}')}"], 1)
        if lv == 1:
            for t in range(NT):
                chain(v.tensor_tensor(c.E[:, t], c.E[:, t], c.cq[:, :, t * P:(t + 1) * P], ALU.mult))
            settle()
            v.tensor_copy(c.flat["cq"], c.flat["EwT"]).then_inc(s["qdec_ready"], 1)
    side_done("u", v.tensor_copy(c.flat["cv"], side("u")))
    v.wait_ge(s["qdec_ready"], 1)
    side_done("wT", v.tensor_copy(c.flat["EwT"], side("wT")))
    v.wait_ge(s[f"side_free{side_pair('wT')}"], side_reuse("wT") + 1)
    v.wait_ge(s[f"side_free{side_pair('u')}"], side_reuse("u") + 1)
    v.sem_inc(s["wT_ready"], 1)

    def maxima(qt):
        nk = P * (qt + 1)
        for m in range(2):
            ps = side(f"s{qt}{m}").rearrange("p (h k) -> p h k", h=H)
            chain(v.memset(ps[0:CHUNK, :, nk - CHUNK:nk], -BIG))
            settle()
            nm = c.negmax[:, 8 * qt + 4 * m:8 * qt + 4 * m + 4]
            chain(v.tensor_reduce(nm, ps[:, :, 0:nk], AX_X, ALU.max))
            settle()
            v.tensor_scalar(nm, nm, -DH ** -0.5, None, ALU.mult).then_inc(s["negmax_ready"], 1)

    def combine(qt):
        nk = P * (qt + 1)
        v.wait_ge(s["exps_ready"], 8 * (qt + 1))
        cf = c.coef[:, 8 * qt:8 * qt + 8]
        chain(v.reciprocal(cf, c.esum[:, 8 * qt:8 * qt + 8]))
        settle()
        chain(v.tensor_scalar(cf[:, 4:8], cf[:, 4:8], c.lamw[:, 0:1], None, ALU.mult))
        settle()
        for h in range(H):
            chain(v.tensor_scalar(c.es[:, 4 + h, 0:nk], c.es[:, 4 + h, 0:nk], col(cf, 4 + h), None, ALU.mult))
        settle()
        for h in range(H):
            last = v.scalar_tensor_tensor(out=c.es[:, h, 0:nk], in0=c.es[:, h, 0:nk], scalar=col(cf, h), in1=c.es[:, 4 + h, 0:nk],
                                          op0=ALU.mult, op1=ALU.add)
            if h < H - 1:
                chain(last)
        last.then_inc(s["aT_in"], 1)

    def probs_turned(qt):
        w = 512 * (qt + 1)
        v.tensor_copy(c.aT[:, 0:w], side(f"aT{qt}")[:, 0:w]).then_inc(s["aT_ready"], 1)
        v.wait_ge(s["aT_ready"], qt + 1)
        v.sem_inc(s[f"side_free{side_pair(f'aT{qt}')}"], 1)

    def attended(qt):
        v.tensor_copy(c.oa[:, qt, :], side(f"oa{qt}")[:, 0:512]).then_inc(s["oa_out"], 1)
        v.wait_ge(s["oa_out"], qt + 1)
        v.sem_inc(s[f"side_free{side_pair(f'oa{qt}')}"], 1)

    def new_values(n_):
        rows = slice(CHUNK * (n_ % 2), CHUNK * (n_ % 2) + CHUNK)
        dst = c.vn[n_ % 2][rows]
        u = c.u[rows, n_ // 2]
        if n_ == 0:
            v.tensor_copy(dst, u).then_inc(s["vn_ready"], 1)
        else:
            ps = side(f"ws{n_}")[rows, 0:512].rearrange("p (h f) -> p h f", h=H)
            v.tensor_tensor(dst, u, ps, ALU.subtract).then_inc(s["vn_ready"], 1)
            v.wait_ge(s["vn_ready"], n_ + 1)
            v.sem_inc(s[f"side_free{side_pair(f'ws{n_}')}"], 1)

    def new_state(n_):
        rows = slice(CHUNK * (n_ % 2), CHUNK * (n_ % 2) + CHUNK)
        ps = side(f"so{n_}")
        if n_ < 3:
            if n_ == 0:
                chain(v.tensor_copy(c.S.rearrange("p h f -> p (h f)"), ps[:, 512:1024]))
            else:
                for h in range(H):
                    chain(v.scalar_tensor_tensor(out=c.S[:, h, :], in0=c.S[:, h, :], scalar=col(c.sums_exp, 16 + 4 * n_ + h),
                                                 in1=blk(ps, H + h), op0=ALU.mult, op1=ALU.add))
            settle()
            v.sem_inc(s["S_ready"], 1)
        v.tensor_copy(c.ob[rows, n_ // 2, :], ps[rows, 0:512]).then_inc(s["ob_out"], 1)
        v.wait_ge(s["ob_out"], n_ + 1)
        v.sem_inc(s[f"side_free{side_pair(f'so{n_}')}"], 1)

    v.wait_ge(s["lam_exp"], 1)
    chain(v.tensor_tensor(c.lamw[:, 0:1], c.lam[:, 3:4], c.lam[:, 2:3], ALU.subtract))
    settle()
    chain(v.tensor_scalar(c.lamw[:, 0:1], c.lamw[:, 0:1], LAMBDA_INIT, None, ALU.subtract))
    new_values(0)
    maxima(0)
    new_state(0)
    combine(0)
    probs_turned(0)
    new_values(1)
    attended(0)
    new_state(1)
    maxima(1)
    new_values(2)
    combine(1)
    new_state(2)
    probs_turned(1)
    new_values(3)
    attended(1)
    new_state(3)

    def head_norm(squares, ss, sq_flat, root, buf, gain, name):
        v.wait_ge(s[squares], 1)
        chain(v.tensor_reduce(ss, sq_flat.rearrange("p (a f) -> p a f", a=8), AX_X, ALU.add))
        settle()
        v.tensor_scalar(ss, ss, 1.0 / P, EPS, ALU.mult, ALU.add).then_inc(s[root], 1)
        v.wait_ge(s[root], 2)
        chain(v.reciprocal(ss, ss))
        settle()
    chain(v.tensor_scalar(c.subln[:, :], c.subln[:, :], 1.0 - LAMBDA_INIT, None, ALU.mult))
    head_norm("oa_squares", c.ra, c.flat["Yb"], "oa_root", None, None, None)
    for i in range(8):
        b = blk(c.flat["F"], i)
        last = v.scalar_tensor_tensor(out=b, in0=b, scalar=col(c.ra, i), in1=c.subln[:, :], op0=ALU.mult, op1=ALU.mult)
        if i < 7:
            chain(last)
    last.then_inc(s["ya_ready"], 1)
    g8 = c.flat["gate"].rearrange("p (a f) -> p a f", a=8)
    v.tensor_tensor(g8, g8, all8(c.gdng[:, :]), ALU.mult).then_inc(s["gate_ready"], 1)
    head_norm("ob_squares", c.rb, c.flat["A"], "ob_root", None, None, None)
    v.wait_ge(s["gate_ready"], 2)
    for i in range(8):
        b = blk(c.flat["TT"], i)
        last = v.scalar_tensor_tensor(out=b, in0=b, scalar=col(c.rb, i), in1=blk(c.flat["gate"], i), op0=ALU.mult, op1=ALU.mult)
        if i < 7:
            chain(last)
    last.then_inc(s["yb_ready"], 1)
    side_done("yaT", v.tensor_copy(c.flat["qT"], side("yaT")))
    v.wait_ge(s[f"side_free{side_pair('yaT')}"], side_reuse("yaT") + 1)
    v.sem_inc(s["yaT_ready"], 1)

    v.wait_ge(s["mg_ready"], 4)
    for q in range(4):
        v.wait_ge(s["branch_ready"], q + 1)
        v.tensor_tensor(c.mg[q], c.mg[q], c.pair[q % 2], ALU.mult).then_inc(s["branch_used"], 1)
        if q >= 2:
            v.wait_ge(s["branch_used"], q + 1)
            v.tensor_tensor(c.mg[q - 2], c.mg[q - 2], c.mg[q], ALU.add).then_inc(s["merged_ready"], 1)
    for t in range(NT):
        v.wait_ge(s["mix_out"], 3 + t)
        v.tensor_tensor(c.x[:, t, :], c.x[:, t, :], c.ps[:, 4 + 2 * t:6 + 2 * t, :].rearrange("p b f -> p (b f)"), ALU.add)\
            .then_inc(s["x1_ready"], 1)
    v.wait_ge(s["ss1_ready"], NT)
    v.tensor_scalar(c.ssx, c.ssx, 1.0 / D, EPS, ALU.mult, ALU.add).then_inc(s["r1_root"], 1)
    v.wait_ge(s["r1_root"], 2)
    chain(v.reciprocal(c.rx, c.rx))
    settle()
    v.wait_ge(s["gffn_loaded"], 16)
    v.wait_ge(s["x1_ready"], NT)
    for t in range(NT):
        v.scalar_tensor_tensor(out=c.h2[:, t, :], in0=c.x[:, t, :], scalar=col(c.rx, t), in1=c.gffn, op0=ALU.mult, op1=ALU.mult)\
            .then_inc(s["h2_ready"], 1)
    v.wait_ge(s["h2_transposed"], 1)
    for b in (0, 2):
        v.tensor_copy(c.h2T[:, 2 * b:2 * b + 2, :].rearrange("p a b -> p (a b)"), c.ps[:, 4 + b, :]).then_inc(s["h2T_ready"], 1)

    route(v, c, chain, settle)

    for k in range(0, KD, 2):
        v.wait_ge(s["gathered"], k + 1)
        v.tensor_copy(c.HgT[:, k, 0:SLOTS], c.ps[:, k, :]).then_inc(s["HgT_ready"], 1)
    v.wait_ge(s["rows_turned"], 1)
    v.tensor_copy(c.rows, c.side[0]).then_inc(s["rows_ready"], 1)
    v.wait_ge(s["row_in_ready"], 1)
    largest = v.value_load(c.offs[0:1, EXPERTS:EXPERTS + 1], min_val=0, max_val=TOK)

    def windows(m, nwin):
        n = HID * m // P
        nq = P // m
        counts, scan, valid = c.r[:, 488:520], c.r[:, 432:464], c.r[:, 168:200]
        row = c.row_in[m]
        steps = 0
        for w in range(nwin):
            dst = c.slot_of[:, EXPERTS * w:EXPERTS * (w + 1)]
            for ins in (lambda: v.tensor_scalar(valid, counts, float(w * m), row, ALU.subtract, ALU.is_gt),
                        lambda: v.tensor_scalar(dst, scan, row, float(w * m + 1), ALU.add, ALU.add),
                        lambda: v.tensor_tensor(dst, dst, valid, ALU.mult),
                        lambda: v.tensor_scalar(dst, dst, 1.0, None, ALU.subtract)):
                ins().then_inc(s["slot_of_ready"], 1)
                steps += 1
                v.wait_ge(s["slot_of_ready"], steps)

        for w in range(nwin):
            for j in range(nq):
                rows = slice(j * m, (j + 1) * m)
                v.tensor_copy(c.slot_at[rows, EXPERTS * w:EXPERTS * w + EXPERTS // nq],
                              c.slot_of[rows, EXPERTS * w + j:EXPERTS * (w + 1):nq]).then_inc(s["slot_of_ready"], 1)
                steps += 1
        v.wait_ge(s["slot_of_ready"], steps)

        def units(rnd, first):
            for u in range(RING * nwin):
                g = rnd * (RING * nwin)
                act, bank = c.act[u % 2][:, 0:n], c.ps[:, u % 2, :]
                v.wait_ge(s["gate_sigmoid"], g + (u + 1))
                need(v, s["act_turned"], g + (u - 1), first)
                v.tensor_tensor(act, bank[:, 0:n], c.sg[u % 2][:, 0:n], ALU.mult).then_inc(s["gated"], 1)
                v.wait_ge(s["gated"], g + (u + 1))
                v.tensor_tensor(act, act, bank[:, n:2 * n], ALU.mult).then_inc(s["act_ready"], 1)
                if u % nq == 0:
                    k = rnd * (RING // nq) + u // nwin // nq
                    col0 = c.slot_at[:, EXPERTS * (u % nwin):EXPERTS * (u % nwin + 1)]
                    this = col0[:, k:k + 1] if first else col0[:, bass.ds(k, 1)]
                    st = rnd * (RING * nwin // nq) + u // nq
                    need(v, s["Se_ready"], st, first)
                    v.scalar_tensor_tensor(out=c.S_tmp, in0=c.rows[:, 0:512], scalar=this, in1=c.rows[:, 512:1024],
                                           op0=ALU.is_equal, op1=ALU.mult).then_inc(s["S_half"], 1)
                    v.wait_ge(s["S_half"], st + 1)
                    need(v, s["scattered"], st if nq == RING else st - 1, first)
                    v.tensor_tensor(c.S_e[stack_buffer(nq, u)], c.S_tmp[:, 0:256], c.S_tmp[:, 256:512], ALU.add).then_inc(s["Se_ready"], 1)
                v.wait_ge(s["down_ready"], g + (u + 1))
                if u % nwin == nwin - 1:
                    v.sem_inc(s["experts_used"], 1)
                stack_rows(v.tensor_copy, c, m, u, range(nq // 2) if nq > 1 else (0,), s["out_copied"])
        units(0, True)
        with v.Fori(1, EXPERTS // RING) as it:
            units(it, False)
        v.wait_ge(s["scattered"], EXPERTS * nwin // nq)
    by_count(v, largest, windows)
    v.wait_ge(s["gfin_loaded"], 16)
    for t in range(NT):
        v.tensor_tensor(c.x[:, t, :], c.x[:, t, :], c.side[t], ALU.add).then_inc(s["ss2_in"], 1)
        v.wait_ge(s["ss2_ready"], t + 1)
        v.tensor_scalar(col(c.ssx, t), col(c.ssx, t), 1.0 / D, EPS, ALU.mult, ALU.add).then_inc(s["r2_root"], 1)
        v.wait_ge(s["r2_root"], 2 * t + 2)
        chain(v.reciprocal(col(c.rx, t), col(c.rx, t)))
        settle()
        v.scalar_tensor_tensor(out=c.y[:, t, :], in0=c.x[:, t, :], scalar=col(c.rx, t), in1=c.gfin, op0=ALU.mult, op1=ALU.mult)\
            .then_inc(s["out_ready"], 1)


def route(v, c, chain, settle):
    s = c.s
    r = c.r
    lg = r[:, 0:72].rearrange("p (t n) -> p t n", t=NT)
    gsh = r[:, 72:80].rearrange("p (t n) -> p t n", t=NT)
    one = {"g": r[:, 80:88].rearrange("p (t n) -> p t n", t=NT), 0: r[:, 88:104].rearrange("p (t n) -> p t n", t=NT),
           1: r[:, 104:120].rearrange("p (t n) -> p t n", t=NT)}
    cand = {4: r[:, 120:128].rearrange("p (t n) -> p t n", t=NT), 8: r[:, 120:136].rearrange("p (t n) -> p t n", t=NT)}
    mx = {"g": r[:, 136:138], 0: r[:, 138:140], 1: r[:, 140:142]}
    low = r[:, 142:144]
    dif = r[:, 144:146]
    gw = r[:, 146:148]
    ing = r[:, 152:168].rearrange("p (t n) -> p t n", t=NT)
    prod = r[:, 168:232].rearrange("p (t e g) -> p t e g", t=NT, e=PER_GROUP)
    picks = r[:, 240:304]
    pick = {0: r[:, 304:368], 1: r[:, 368:432]}
    scan = r[:, 432:464]
    pos, wk = r[:, 480:484], r[:, 484:488]
    base = r[:, 168:232]
    counts = r[:, 488:520]

    def over(ap, n):
        return ap.rearrange("p (t a) -> p t a", a=1).to_broadcast([P, NT, n])

    def ids(n):
        return c.iota[:, 0:n].rearrange("p (a n) -> p a n", a=1).to_broadcast([P, NT, n])

    def link(ins):
        chain(ins)
        settle()

    def first_max(vals, n, key):
        link(v.tensor_reduce(mx[key], vals, AX_X, ALU.max))
        link(v.tensor_tensor(cand[n], vals, over(mx[key], n), ALU.is_equal))
        for t in range(NT):
            chain(v.scalar_tensor_tensor(out=cand[n][:, t, :], in0=cand[n][:, t, :], scalar=-1000.0, in1=c.iota[:, 0:n],
                                         op0=ALU.mult, op1=ALU.add))
        settle()
        link(v.tensor_reduce(low, cand[n], AX_X, ALU.min))
        link(v.tensor_tensor(one[key], cand[n], over(low, n), ALU.is_equal))
    v.wait_ge(s["logits_ready"], 1)
    v.wait_ge(s["iota_ready"], 1)
    v.wait_ge(s["router_loaded"], 64)
    link(v.tensor_tensor(lg, c.ps[:, 0, 0:72].rearrange("p (t n) -> p t n", t=NT),
                         c.rbias.rearrange("p (a n) -> p a n", a=1).to_broadcast([P, NT, 36]), ALU.add))
    first_max(lg[:, :, 0:GROUPS], GROUPS, "g")
    v.tensor_tensor(gsh, lg[:, :, 0:GROUPS], over(mx["g"], GROUPS), ALU.subtract).then_inc(s["gexp_in"], 1)
    for t in range(NT):
        chain(v.tensor_tensor(prod[:, t], lg[:, t, GROUPS:].rearrange("p (g e) -> p e g", g=GROUPS),
                              one["g"][:, t, :].rearrange("p (a g) -> p a g", a=1).to_broadcast([P, PER_GROUP, GROUPS]), ALU.mult))
    settle()
    link(v.tensor_reduce(ing, prod, AX_X, ALU.add))
    first_max(ing, PER_GROUP, 0)
    link(v.scalar_tensor_tensor(out=ing, in0=one[0], scalar=-BIG, in1=ing, op0=ALU.mult, op1=ALU.add))
    first_max(ing, PER_GROUP, 1)
    for k in range(2):
        for t in range(NT):
            chain(v.tensor_tensor(pick[k][:, 32 * t:32 * (t + 1)].rearrange("p (g e) -> p g e", g=GROUPS),
                                  one["g"][:, t, :].rearrange("p (g a) -> p g a", a=1).to_broadcast([P, GROUPS, PER_GROUP]),
                                  one[k][:, t, :].rearrange("p (a e) -> p a e", a=1).to_broadcast([P, GROUPS, PER_GROUP]), ALU.mult))
    v.tensor_tensor(dif, mx[1], mx[0], ALU.subtract).then_inc(s["texp_in"], 1)
    settle()
    v.tensor_tensor(picks, pick[0], pick[1], ALU.add).then_inc(s["picks_ready"], 1)
    v.wait_ge(s["gexp_out"], 1)
    link(v.tensor_reduce(gw, gsh, AX_X, ALU.add))
    link(v.reciprocal(gw, gw))
    v.wait_ge(s["texp_out"], 1)
    link(v.tensor_scalar(wk[:, 0:2], dif, 1.0, None, ALU.add))
    link(v.reciprocal(wk[:, 0:2], wk[:, 0:2]))
    link(v.tensor_tensor(wk[:, 0:2], wk[:, 0:2], gw, ALU.mult))
    chain(v.tensor_tensor(wk[:, 2:4], wk[:, 0:2], dif, ALU.mult))
    v.wait_ge(s["ranks_ready"], 1)
    chain(v.tensor_copy(counts, c.ps[:, 1, 64:96]))
    settle()
    chain(v.tensor_tensor_scan(scan, counts, counts, 0.0, ALU.add, ALU.bypass))
    chain(v.tensor_reduce(low[:, 0:1], counts, AX_X, ALU.max))
    settle()
    link(v.tensor_tensor(scan, scan, counts, ALU.subtract))
    link(v.tensor_tensor(base.rearrange("p (t e) -> p t e", t=NT), c.ps[:, 1, 0:64].rearrange("p (t e) -> p t e", t=NT),
                         scan.rearrange("p (a e) -> p a e", a=1).to_broadcast([P, NT, EXPERTS]), ALU.add))
    for k in range(2):
        chain(v.tensor_tensor(pick[k], pick[k], base, ALU.mult))
    settle()
    for k in range(2):
        chain(v.tensor_reduce(pos[:, 2 * k:2 * k + 2], pick[k].rearrange("p (t e) -> p t e", t=NT), AX_X, ALU.add))
    chain(v.tensor_copy(c.offs[:, 0:EXPERTS], scan[0:1, :]))
    settle()
    v.tensor_copy(c.offs[:, EXPERTS:EXPERTS + 1], low[0:1, 0:1]).then_inc(s["offsets_ready"], 1)
    for t in range(NT):
        chain(v.tensor_scalar(c.onehot[:, t, :], c.iota[:, :], pos[:, t:t + 1], None, ALU.is_equal))
    settle()
    for t in range(NT):
        v.scalar_tensor_tensor(out=c.onehot[:, t, :], in0=c.iota[:, :], scalar=pos[:, 2 + t:3 + t], in1=c.onehot[:, t, :],
                               op0=ALU.is_equal, op1=ALU.add).then_inc(s["onehot_ready"], 1)
    chain(v.memset(c.levelT[0], 0.0))
    v.memset(c.HgT[:, :, SLOTS:SLOTS + TOK], 0.0).then_inc(s["HgT_ready"], 1)


def build(nc, io):
    with ExitStack() as ctx:
        c = lay_out(nc, ctx)
        block = ctx.enter_context(nc.Block())

        @block.sync
        def _(sp):
            sync_program(sp, c, io)

        @block.gpsimd
        def _(pool):
            gpsimd_program(pool, c, io)
            pool.wait_ge(c.s["gathered"], KD)
            pool.dma_start(c.gfin, io["norm_final_gain"].rearrange("(a d) -> a d", a=1).partition_broadcast(P)
                           .rearrange("p a d -> p (a d)")).then_inc(c.s["gfin_loaded"], 16)

        @block.scalar
        def _(act):
            scalar_program(act, c, io)

        @block.tensor
        def _(pe):
            tensor_program(pe, c, io)

        @block.vector
        def _(v):
            vector_program(v, c, io)


_INS = ["x", "norm_mix_gain", "w_in", "diff_lambda_q1", "diff_lambda_k1", "diff_lambda_q2", "diff_lambda_k2",
        "diff_subln_gain", "gdn_conv_w", "gdn_a_log", "gdn_dt_bias", "gdn_norm_gain", "w_branch_attn", "w_branch_gdn",
        "w_out", "norm_ffn_gain", "moe_w_group", "moe_b_group", "moe_w_expert", "moe_b_expert", "moe_w_gate",
        "moe_w_up", "moe_w_down", "norm_final_gain"]


def kernel(**inputs):
    import numpy as _np
    import concourse.bacc as _bacc
    from concourse import mybir as _mybir
    from concourse.bass_utils import run_bass_kernel_spmd as _run

    nc = _bacc.Bacc("TRN2", target_bir_lowering=False, num_devices=1)
    arrays, io = {}, {}
    for name in _INS:
        a = _np.ascontiguousarray(inputs[name])
        arrays[f"in_{name}"] = a
        io[name] = nc.dram_tensor(f"in_{name}", a.shape, _mybir.dt.from_np(a.dtype), kind="ExternalInput").ap()
    io["out"] = nc.dram_tensor("out_y", (1, TOK, D), _mybir.dt.from_np(_np.dtype("float32")), kind="ExternalOutput").ap()
    build(nc, io)
    r = _run(nc, [arrays], core_ids=[0])
    return r.results[0]["out_y"]
```

```python
from contextlib import ExitStack

import concourse.bass as bass
from concourse import mybir

F32 = mybir.dt.float32
BF16 = mybir.dt.bfloat16
I32 = mybir.dt.int32
ALU = mybir.AluOpType
ACT = mybir.ActivationFunctionType
AX_X = mybir.AxisListType.X

P = 128
D = 1024
TOK = 256
NT = TOK // P
KD = D // P
EPS = 1e-6
H = 4
DH = 64
W4 = H * P
CHUNK = 64
TAPS = 4
GROUPS, PER_GROUP = 4, 8
EXPERTS = GROUPS * PER_GROUP
HID = 256
SLOTS = 2 * TOK
PATHS = [(32, 1), (64, 1), (128, 2)]
RING = 4
SPARES = 2
EXP_F = 3 * D * HID // P
BIG = 1e30
LAMBDA_INIT = 0.2

CHUNKS = [("gk", 2048, 512, "T"), ("gq", 1536, 512, "T"), ("bdg", 3072, 520, "N"), ("gv", 2560, 512, "T"),
          ("dq", 0, 512, "T"), ("dk", 512, 512, "T"), ("dv", 1024, 512, "N"),
          ("ma0", 3592, 512, "T"), ("ma1", 4104, 512, "T"), ("mb0", 4616, 512, "T"), ("mb1", 5128, 512, "T")]
NCH = len(CHUNKS)
CI = {c[0]: i for i, c in enumerate(CHUNKS)}


def place(e):
    if e < RING + SPARES:
        return e, 1
    return (e - SPARES) % RING, (e - SPARES) // RING + 1


PARTS = [4 if c[3] == "T" else 2 for c in CHUNKS]

LEVELS = 5
SIDE = [("consts", 1), ("bd", 1), ("ss", 1), ("rnk", 1), ("rnq", 1), ("gsum", 1), ("grow", 1), ("gram", 1),
        ("intra", 1), ("ktok", 1), ("vtok", 1), ("b1", 1)]
for _l in range(1, LEVELS + 1):
    SIDE += [(f"Y{_l}", 1), (f"TT{_l}", 1)] + ([(f"T{_l}", 1)] if _l < LEVELS else [])
SIDE += [("u", 1), ("wT", 1), ("s00", 1), ("s01", 1), ("so0", 1), ("aT0", 1), ("ws1", 1), ("oa0", 1), ("so1", 1),
         ("s10", 1), ("s11", 1), ("ws2", 1), ("so2", 1), ("aT1", 1), ("ws3", 1), ("oa1", 1), ("so3", 1),
         ("yaT", 1), ("ybT", 1)]
SI = {n: i for i, (n, _) in enumerate(SIDE)}


PIECES = [(half, t) for half in range(2) for t in range(NT)]


def side_pair(name):
    return SI[name] % 2


def side_reuse(name):
    i = SI[name]
    return sum(c for j, (_, c) in enumerate(SIDE[:i]) if j % 2 == i % 2)


def parts_before(i):
    return sum(PARTS[:i])


class Core:
    pass


def lay_out(nc, ctx):
    c = Core()
    stage_f = KD * 520
    names = {}

    def sb(name, shape, dt=F32):
        return ctx.enter_context(nc.sbuf_tensor(name, shape, dt))

    ring = sb("ring", [P, RING - 1, EXP_F])
    sizes = [("x", 2048), ("hT", 2048), ("stage0", stage_f), ("stage1", stage_f),
             ("ck", 1024), ("wrhs", 1024), ("vb", 1024), ("gate", 1024), ("qT", 1024), ("kT", 1024), ("S", 512),
             ("dv", 1024), ("cv", 1024), ("cq", 1024), ("kdec", 1024), ("F", 1024), ("vn", 1024),
             ("A", 1024), ("T", 1024), ("TT", 1024), ("Yb", 1024), ("attnT", 1024), ("EwT", 1024)]
    total = sum(n for _, n in sizes)
    arena = sb("arena", [P, total])
    off = 0
    for n, size in sizes:
        names[n] = off
        off += size

    def at(name, size, extra=0):
        return arena[:, names[name] + extra:names[name] + extra + size]

    c.ring = [ring[:, i, :] for i in range(RING - 1)] + [at("A", EXP_F), at("dv", EXP_F), at("stage1", EXP_F)]
    c.gu_w = [r[:, 0:4096].rearrange("p (g k f) -> p g k f", g=2, k=KD) for r in c.ring]
    c.down_w = [r[:, 4096:6144].rearrange("p (k d) -> p k d", k=2) for r in c.ring]
    c.gate_flat = [r[:, 0:2048] for r in c.ring]
    c.up_flat = [r[:, 2048:4096] for r in c.ring]
    c.down_flat = [r[:, 4096:6144] for r in c.ring]

    def v3(ap, a):
        return ap.rearrange("p (a b) -> p a b", a=a)

    c.x = v3(at("x", 2048), NT)
    c.rx_row = at("A", TOK)
    c.hT = v3(at("hT", 2048), KD)
    c.stage = [at("stage0", stage_f), at("stage1", stage_f)]
    c.qT, c.kT = v3(at("qT", 1024), H), v3(at("kT", 1024), H)
    c.dv = v3(at("dv", 1024), NT)
    c.cq, c.ck, c.cv = (v3(at(n, 1024), H) for n in ("cq", "ck", "cv"))
    c.sig = {"gk": v3(at("F", 1024), H), "gq": v3(at("TT", 1024), H), "gv": v3(at("Yb", 1024), H)}
    c.sqk, c.sqq = v3(at("A", 1024), H), v3(at("T", 1024), H)
    c.gate = v3(at("gate", 1024), NT)

    def prob(name):
        return at(name, 1024).rearrange("p (t h f) -> p t h f", t=NT, h=H)
    c.A, c.T, c.TT, c.Yb, c.attnT, c.E, c.wT = (prob(n) for n in ("A", "T", "TT", "Yb", "attnT", "EwT", "EwT"))
    c.wrhs, c.vb, c.kdec, c.qdec, c.u = (prob(n) for n in ("wrhs", "vb", "kdec", "cq", "cv"))
    c.flat = {n: at(n, 1024) for n in ("A", "T", "TT", "Yb", "attnT", "EwT", "wrhs", "vb", "kdec", "cq", "ck", "cv",
                                       "F", "gate", "qT", "kT", "dv")}
    c.S = v3(at("S", 512), H)
    c.vn = [v3(at("vn", 512, 512 * i), H) for i in range(2)]
    c.ob = v3(at("TT", 1024), NT)
    c.oa = v3(at("F", 1024), NT)
    c.es = v3(at("A", 2048), 2 * H)
    c.aT = at("Yb", 1024)
    c.yaT, c.ybT = v3(at("qT", 1024), H), v3(at("kT", 1024), H)
    c.mg = [at(n, 1024) for n in ("ck", "vb", "wrhs", "gate")]

    c.h2 = v3(at("hT", 2048), NT)
    c.iota = at("S", SLOTS)
    base2 = names["stage0"]

    def at2(off2, size):
        return arena[:, base2 + off2:base2 + off2 + size]
    c.x1T = v3(at("qT", 2048), KD)
    c.squares = at("hT", 512)
    c.onehot = v3(at("qT", 512).bitcast(BF16), NT)
    c.high = v3(at("kT", 1024).bitcast(BF16), NT)
    c.HgT = v3(at("stage0", KD * SLOTS), KD)
    o2 = stage_f + EXP_F
    c.rows = at2(o2, 1024)
    c.gfin = c.rows
    o2 += 1024
    c.S_tmp = at2(o2, 512)
    c.mid = [c.S_tmp.bitcast(BF16), at("qT", 512, 512).bitcast(BF16)]
    o2 += 512
    c.r = at2(o2, 520)
    o2 += 520
    assert base2 + o2 <= names["qT"], (base2 + o2, names["qT"])
    c.Y = [at("qT", 1024), at("kT", 1024)]
    c.slot_of = at("S", 2 * EXPERTS)
    c.slot_at = at("S", 2 * EXPERTS, 2 * EXPERTS)
    c.y = v3(at("hT", 2048), NT)
    c.window = [at("hT", 1024), at("hT", 1024, 1024)]

    m = sb("masks", [P, 14, P])
    c.ident, c.ones, c.before, c.upper, c.lower, c.chunk, c.half0, c.half1, c.m1 = (m[:, i, :] for i in range(9))
    c.levelT = [m[:, 9 + i, :] for i in range(LEVELS)]
    c.masks = m
    gains = sb("gains", [P, 2 * P])
    c.subln, c.gdng = gains[:, 0:P], gains[:, P:2 * P]
    dead = m[:, 3:14, :].rearrange("p a f -> p (a f)")
    c.act, c.actT = ([dead[:, i + 256 * j:i + 256 * j + 256] for j in range(2)] for i in (0, 512))
    c.sg = [dead[:, 1024:1280], gains[:, 0:256]]
    c.low = v3(dead[:, 0:1024].bitcast(BF16), NT)
    c.small = sb("small", [P, 384])
    so = [0]

    def sm(n):
        so[0] += n
        assert so[0] <= 384
        return c.small[:, so[0] - n:so[0]]
    c.cst_in = sb("cst_in", [64, P])
    c.cst = sm(64)
    c.eps, c.scratch = sm(1), sm(1)
    c.gffn = sm(KD)
    c.below = sm(PER_GROUP)
    c.ssx, c.rx, c.ss_piece = sm(2), sm(2), sm(4)
    c.alog, c.dtb, c.nea = sm(4), sm(4), sm(4)
    c.beta, c.z, c.zm, c.sp, c.g = (sm(8) for _ in range(5))
    c.rn = sm(16)
    c.run_sum, c.chunk_sum, c.bexp = sm(8), sm(8), sm(8)
    c.sums_exp = sm(32)
    c.sums_in = sm(32)
    c.negmax, c.esum, c.coef = sm(16), sm(16), sm(16)
    c.lam = sm(4)
    c.lamw = sm(2)
    c.row_in = {m: sm(1) for m, _ in PATHS}
    c.rb = sm(8)
    c.ra = sm(8)
    c.rbias = sm(36)
    lamrows, rw = sb("lamrows", [P, 4 * DH]), sb("rw", [P, KD * (GROUPS + EXPERTS)])
    c.lamrows = v3(lamrows[:, :], 4)
    c.rw = v3(rw[:, :], KD)
    c.S_e = [rw[:, 0:256], lamrows[:, 0:256]]
    c.zeros = sb("zeros", [1, P], BF16)
    c.largest = sb("largest", [1, 1], I32)
    starts = sb("starts", [1, sum(n for _, n in PATHS) * (EXPERTS + 2)], I32)
    c.starts, at_ = {}, 0
    for rows, nwin in PATHS:
        for w in range(nwin):
            c.starts[rows, w] = starts[:, at_:at_ + EXPERTS + 2]
            at_ += EXPERTS + 2
    c.all_starts = starts[:, :]
    c.ps = ctx.enter_context(nc.psum_tensor("ps", [P, 8, 512], F32))

    c.side = [c.ps[:, 4:6, :].rearrange("p b f -> p (b f)"), c.ps[:, 6:8, :].rearrange("p b f -> p (b f)")]
    c.pair = [c.ps[:, 0:2, :].rearrange("p b f -> p (b f)"), c.ps[:, 2:4, :].rearrange("p b f -> p (b f)")]

    def sem(name):
        return ctx.enter_context(nc.semaphore(name))
    for_names = """x_loaded0 x_loaded1 first_half_loaded eps_ready x_transposed rx_ready rx_turned rw_ready consts_loaded vectors_loaded lambda_loaded router_loaded gfin_loaded out_stored
        ident_ready masks_ready iota_ready squares_ready
        ssx_ready rx_root hT_ready cst_ready
        proj_ready side_ready
        conv_ready conv_sig qkv_ready gate_sig gate_ready beta_ready dec_exp g_in g_ready rn_root rn_ready
        q_normed k_normed gsum_ready gsum_exp grow_pre grow_exp qdec_ready 
        tok_ready b1_ready Y_ready TT_ready T_ready wT_ready
        dq_ready dk_ready dv_ready mg_ready
        negmax_ready exps_ready lam_in lam_exp aT_in aT_ready oa_out oa_squares oa_root ya_ready yaT_ready
        S_ready vn_ready ob_out ob_squares ob_root yb_ready ybT_ready
        branch_ready branch_used merged_ready mix_out x1_ready ss1_ready ss1_summed r1_root r1_ready h2_ready high_ready rest_ready mid_ready low_ready x1_transposed x1T_ready starts_zeroed starts_ready rows_dead zeros_ready
        logits_ready gexp_in gexp_out texp_in texp_out picks_ready ranks_ready offsets_ready onehot_ready 
        gathered HgT_even HgT_odd
        window_ready gu_ready gate_sigmoid gated act_ready act_turned actT_ready S_half Se_ready down_ready out_copied row_in_ready
        scattered rows_turned rows_ready gateup_used experts_used slot_of_ready x2_ready last_scatter ss2_ready r2_root r2_ready y_ready out_left_ready out_right_ready
        dve_chain act_chain pool_chain side_free0 side_free1 pair_free0 pair_free1 stage_loaded0 stage_loaded1""".split()
    c.s = {n: sem(n) for n in for_names}
    for i in range(RING + SPARES):
        c.s[f"gateup{i}"] = sem(f"gateup{i}")
        c.s[f"down{i}"] = sem(f"down{i}")
    return c


def sync_program(sp, c, io):
    s = c.s
    for t in range(NT):
        sp.dma_start(c.x[:, t, :], io["x"].rearrange("b (t p) d -> p (b t) d", p=P)[:, t, :]).then_inc(s[f"x_loaded{t}"], 16)
    w_in = io["w_in"][0].rearrange("(k p) n -> p k n", p=P)

    def stage_free(i):
        if 2 <= i < NCH + 2:
            sp.wait_ge(s["proj_ready"], parts_before(i - 1))
            if i - 2 == CI["bdg"]:
                sp.wait_ge(s["side_ready"], SI["bd"] + 1)
        elif i >= NCH + 2:
            sp.wait_ge(s["branch_ready"], 2 * (i - NCH - 1))

    def load_chunk(i):
        _, col, n, _ = CHUNKS[i]
        stage_free(i)
        dst = c.stage[i % 2][:, 0:KD * n].rearrange("p (k n) -> p k n", k=KD)
        k0 = 0
        if i == 0:
            k0 = KD // 2
            sp.dma_start(dst[:, 0:k0, :], w_in[:, 0:k0, col:col + n]).then_inc(s["first_half_loaded"], 16)
        sp.dma_start(dst[:, k0:, :], w_in[:, k0:, col:col + n]).then_inc(s[f"stage_loaded{i % 2}"], 16)

    def load_expert(e):
        slot, _ = place(e)
        for flat, name, sem in ((c.gate_flat, "moe_w_gate", "gateup"), (c.up_flat, "moe_w_up", "gateup"),
                                (c.down_flat, "moe_w_down", "down")):
            k = 2 if name == "moe_w_down" else KD
            if e == RING + SPARES - 1:
                sp.wait_ge(s["mix_out"], 2 if sem == "gateup" else 4)
            sp.dma_start(flat[slot], io[name][0, e].rearrange("(p k) f -> p (k f)", k=k)).then_inc(s[f"{sem}{slot}"], 16)

    for i in range(4):
        load_chunk(i)
    load_expert(0)
    load_chunk(4)
    load_expert(1)
    load_chunk(5)
    load_expert(2)
    for i in range(6, NCH):
        load_chunk(i)
    for j, name in enumerate(("w_branch_attn", "w_branch_gdn")):
        i = NCH + j
        stage_free(i)
        sp.dma_start(c.stage[i % 2][:, 0:4096].rearrange("p (k n) -> p k n", k=H),
                     io[name][0].rearrange("(k p) n -> p k n", p=P)).then_inc(s[f"stage_loaded{i % 2}"], 16)
    for j in range(2):
        i = NCH + 2 + j
        stage_free(i)
        sp.dma_start(c.stage[i % 2][:, 0:4096].rearrange("p (k n) -> p k n", k=KD),
                     io["w_out"][0].rearrange("(k p) n -> p k n", p=P)[:, :, j * 512:(j + 1) * 512])\
            .then_inc(s[f"stage_loaded{i % 2}"], 16)
    sp.wait_ge(s["ybT_ready"], 1)
    sp.wait_ge(s["side_ready"], len(SIDE))
    sp.wait_ge(s["yaT_ready"], 1)
    load_expert(3)
    load_expert(4)
    load_expert(5)
    gate_d = io["moe_w_gate"][0].rearrange("e (p k) f -> p e (k f)", k=KD)
    up_d = io["moe_w_up"][0].rearrange("e (p k) f -> p e (k f)", k=KD)
    down_d = io["moe_w_down"][0].rearrange("e (p k) d -> p e (k d)", k=2)

    def reload(e, slot, used):
        for flat, src, sem, free in ((c.gate_flat, gate_d, "gateup", "gateup_used"), (c.up_flat, up_d, "gateup", "gateup_used"),
                                     (c.down_flat, down_d, "down", "experts_used")):
            sp.wait_ge(s[free], used)
            sp.dma_start(flat[slot], src[:, e, :].rearrange("p a f -> p (a f)")).then_inc(s[f"{sem}{slot}"], 16)

    def one(e):
        return slice(e, e + 1)
    first = RING + SPARES
    for j in range(RING):
        reload(one(first + j), j, j + 1)
    rounds, rest = (EXPERTS - first) // RING, (EXPERTS - first) % RING
    with sp.Fori(1, rounds) as it:
        for j in range(RING):
            reload(bass.ds(it * RING + (first + j), 1), j, it * RING + (first + j - RING + 1))
    for j in range(rest):
        reload(one(first + rounds * RING + j), j, first + (rounds - 1) * RING + j + 1)
    outv = io["out"].rearrange("b (t p) d -> p (b t) d", p=P)
    for t in range(NT):
        sp.wait_ge(s["out_left_ready"], t + 1)
        sp.wait_ge(s["out_right_ready"], t + 1)
        sp.dma_start(outv[:, t, :], c.y[:, t, :]).then_inc(s["out_stored"], 16)
    sp.wait_ge(s["out_stored"], 16 * NT)


def gpsimd_program(pool, c, io):
    s = c.s
    n = [0]

    def settle(ins):
        n[0] += 1
        ins.then_inc(s["pool_chain"], 1)
        pool.wait_ge(s["pool_chain"], n[0])
    settle(pool.memset(c.masks[:, :, :], 0.0))
    pool.affine_select(out=c.ident, in_=c.ident, compare_op=ALU.not_equal, fill=1.0, base=0,
                       pattern=[[-1, P]], channel_multiplier=1).then_inc(s["ident_ready"], 1)
    odd = c.m1.rearrange("p (a b) -> p a b", b=2)[:, :, 0]
    settle(pool.affine_select(out=odd, in_=odd, compare_op=ALU.not_equal, fill=1.0, base=-1,
                              pattern=[[-2, P // 2]], channel_multiplier=1))
    for v in (c.upper, c.lower, c.chunk, c.half0, c.half1, c.ones, c.before):
        pool.memset(v, 1.0)
    tops = []
    for lv in range(LEVELS):
        w = 2 << lv
        top = c.levelT[lv].rearrange("p (a b f) -> p a b f", b=2, f=w)[:, :, 1, :]
        pool.memset(top, 1.0)
        tops.append((top, w))
    pool.memset(c.zeros[:, :], 0.0).then_inc(s["zeros_ready"], 1)
    pool.memset(c.all_starts, 0).then_inc(s["starts_zeroed"], 1)
    settle(pool.memset(c.vn[0], 0.0))
    settle(pool.memset(c.vn[1], 0.0))

    def keep(v, pattern, base, mult):
        return pool.affine_select(out=v, in_=v, compare_op=ALU.is_ge, fill=0.0, base=base, pattern=pattern,
                                  channel_multiplier=mult)
    nc2 = P // CHUNK
    for v in (c.upper, c.lower, c.chunk):
        keep(v.rearrange("p (a f) -> p a f", a=nc2), [[-CHUNK, nc2], [0, CHUNK]], 0, 1)
    for top, w in tops:
        keep(top, [[-2 * w, P // (2 * w)], [0, w]], 0, 1)
    keep(c.half0, [[0, P]], CHUNK - 1, -1)
    keep(c.half1, [[0, P]], -CHUNK, 1)
    settle(keep(c.before, [[1, P]], -1, -1))
    for v in (c.upper, c.lower, c.chunk):
        keep(v.rearrange("p (a f) -> p a f", a=nc2), [[CHUNK, nc2], [0, CHUNK]], CHUNK - 1, -1)
    for top, w in tops:
        last = keep(top, [[2 * w, P // (2 * w)], [0, w]], w - 1, -1)
    settle(last)
    keep(c.upper, [[1, P]], 0, -1)
    keep(c.lower, [[-1, P]], -1, 1).then_inc(s["masks_ready"], 1)
    for m, _ in PATHS:
        for q in range(P // m):
            settle(pool.iota(c.row_in[m][m * q:m * (q + 1)], [[0, 1]], base=0, channel_multiplier=1,
                             allow_small_or_imprecise_dtypes=True))
    settle(pool.iota(c.below, [[1, PER_GROUP]], base=-PER_GROUP, channel_multiplier=0, allow_small_or_imprecise_dtypes=True))
    pool.sem_inc(s["row_in_ready"], 1)
    for i, (src, dst) in enumerate(((c.ck, c.sqk), (c.cq, c.sqq))):
        pool.wait_ge(s["qkv_ready"], i + 1)
        pool.tensor_tensor(dst, src, src, ALU.mult).then_inc(s["squares_ready"], 1)
    pool.wait_ge(s["ob_out"], 4)
    pool.iota(c.iota[:, :], [[1, SLOTS]], base=0, channel_multiplier=0,
              allow_small_or_imprecise_dtypes=True).then_inc(s["iota_ready"], 1)
    for t in range(NT):
        pool.wait_ge(s["high_ready"], t + 1)
        pool.tensor_tensor(c.h2[:, t, :], c.h2[:, t, :], c.high[:, t, :], ALU.subtract).then_inc(s["rest_ready"], 1)
    for t in range(NT):
        pool.wait_ge(s["mid_ready"], t + 1)
        pool.wait_ge(s["rest_ready"], t + 1)
        pool.tensor_tensor(c.low[:, t, :], c.h2[:, t, :], c.mid[t], ALU.subtract).then_inc(s["low_ready"], 1)


def scalar_program(act, c, io):
    s = c.s
    n = [0]

    def chain(ins):
        n[0] += 1
        ins.then_inc(s["act_chain"], 1)

    def settle():
        act.wait_ge(s["act_chain"], n[0])

    act.dma_start(c.cst_in[0:8, :], io["norm_mix_gain"][0].rearrange("(k p) -> k p", p=P)).then_inc(s["consts_loaded"], 16)
    act.dma_start(c.cst_in[8:56, :], io["gdn_conv_w"][0].rearrange("j (b p) -> (j b) p", p=P)).then_inc(s["consts_loaded"], 16)
    act.dma_start(c.cst_in[56:64, :], io["norm_ffn_gain"][0].rearrange("(k p) -> k p", p=P)).then_inc(s["consts_loaded"], 16)
    act.wait_ge(s["eps_ready"], 1)
    act.activation(c.scratch, c.eps, ACT.Sqrt)
    for t in range(NT):
        act.wait_ge(s[f"x_loaded{t}"], 16)
        act.activation(c.hT[:, 4 * t:4 * t + 4, :], c.x[:, t, :].rearrange("p (a b) -> p a b", a=4),
                       ACT.Square, accum_out=c.ssx[:, t:t + 1]).then_inc(s["ssx_ready"], 1)
    act.wait_ge(s["ssx_ready"], NT)
    act.activation(c.rx, c.ssx, ACT.Sqrt, scale=1.0 / D, bias=c.eps).then_inc(s["rx_root"], 1)

    def row(dst, src, sem):
        act.dma_start(dst, src.partition_broadcast(P).rearrange("p a d -> p (a d)")).then_inc(s[sem], 16)
    row(c.alog, io["gdn_a_log"][0:1, :], "vectors_loaded")
    row(c.dtb, io["gdn_dt_bias"][0:1, :], "vectors_loaded")
    row(c.subln, io["diff_subln_gain"][0:1, :], "vectors_loaded")
    row(c.gdng, io["gdn_norm_gain"][0:1, :], "vectors_loaded")
    for i, nm in enumerate(("q1", "k1", "q2", "k2")):
        row(c.lamrows[:, i, :], io[f"diff_lambda_{nm}"][0:1, :], "lambda_loaded")
    row(c.rbias[:, 0:GROUPS], io["moe_b_group"][0:1, :], "router_loaded")
    row(c.rbias[:, GROUPS:], io["moe_b_expert"][0:1, :], "router_loaded")
    act.dma_start(c.rw[:, :, 0:GROUPS], io["moe_w_group"][0].rearrange("(k p) g -> p k g", p=P)).then_inc(s["router_loaded"], 16)
    act.dma_start(c.rw[:, :, GROUPS:], io["moe_w_expert"][0].rearrange("(k p) g -> p k g", p=P)).then_inc(s["router_loaded"], 16)
    act.dma_start(c.gffn, io["norm_ffn_gain"][0].rearrange("(p k) -> p k", k=KD)).then_inc(s["router_loaded"], 16)

    def conv_sigmoid(i, name, src):
        act.wait_ge(s["conv_ready"], i + 1)
        act.activation(c.sig[name], src, ACT.Sigmoid).then_inc(s["conv_sig"], 1)
    conv_sigmoid(0, "gk", c.ck)
    conv_sigmoid(1, "gq", c.cq)
    i = CI["bdg"]
    act.wait_ge(s["proj_ready"], parts_before(i) + PARTS[i])
    act.activation(c.flat["gate"], c.pair[i % 2], ACT.Sigmoid).then_inc(s["gate_sig"], 1)
    act.wait_ge(s["side_ready"], SI["bd"] + 1)
    bd = beta_decay_out(c)
    act.activation(c.beta.rearrange("p (t h) -> p t h", t=NT), bd[:, :, 0, :], ACT.Sigmoid).then_inc(s["beta_ready"], 1)
    act.wait_ge(s["rn_root"], 1)
    act.activation(c.rn, c.rn, ACT.Sqrt).then_inc(s["rn_root"], 1)
    act.wait_ge(s["g_in"], 1)
    act.activation(c.z, c.z, ACT.Exp).then_inc(s["dec_exp"], 1)
    act.wait_ge(s["vectors_loaded"], 64)
    act.activation(c.nea, c.alog, ACT.Exp).then_inc(s["dec_exp"], 1)
    act.wait_ge(s["dec_exp"], 2)
    act.activation(c.z, c.z, ACT.Ln, bias=1.0).then_inc(s["dec_exp"], 1)
    act.wait_ge(s["lam_in"], 1)
    act.activation(c.lam[:, 2:4], c.lam[:, 0:2], ACT.Exp).then_inc(s["lam_exp"], 1)
    act.wait_ge(s["gsum_ready"], 1)
    act.activation(c.sums_exp, c.sums_in, ACT.Exp).then_inc(s["gsum_exp"], 1)
    act.wait_ge(s["grow_pre"], 2)
    act.activation(c.flat["EwT"], c.side[side_pair("grow")], ACT.Exp).then_inc(s[f"side_free{side_pair('grow')}"], 1)
    act.wait_ge(s["grow_pre"], 1)
    act.activation(c.flat["T"], c.flat["T"], ACT.Exp, scale=-1.0).then_inc(s["grow_exp"], 1)
    act.wait_ge(s["grow_pre"], 2)
    act.activation(c.flat["attnT"], c.flat["attnT"], ACT.Exp).then_inc(s["grow_exp"], 1)

    conv_sigmoid(2, "gv", c.cv)

    def evacuate(name, dst, sem, func):
        i = CI[name]
        act.wait_ge(s["proj_ready"], parts_before(i) + PARTS[i])
        act.activation(dst, c.pair[i % 2], func).then_inc(s[sem], 1)
        act.wait_ge(s[sem], {"dq_ready": 1, "dk_ready": 1, "dv_ready": 1}.get(sem, 0) or [None, "ma0", "ma1", "mb0", "mb1"].index(name))
        act.sem_inc(s[f"pair_free{i % 2}"], 1)
    evacuate("dq", c.flat["qT"], "dq_ready", ACT.Copy)
    evacuate("dk", c.flat["kT"], "dk_ready", ACT.Copy)
    evacuate("dv", c.flat["dv"], "dv_ready", ACT.Copy)
    evacuate("ma0", c.mg[0], "mg_ready", ACT.Sigmoid)

    def exps(qt):
        nk = P * (qt + 1)
        for m in range(2):
            act.wait_ge(s["negmax_ready"], 2 * qt + m + 1)
            pair = c.side[side_pair(f"s{qt}{m}")].rearrange("p (h k) -> p h k", h=H)
            for h in range(H):
                j = m * H + h
                ins = act.activation(c.es[:, j, 0:nk], pair[:, h, 0:nk], ACT.Exp, bias=c.negmax[:, 8 * qt + j:8 * qt + j + 1],
                                     scale=DH ** -0.5, accum_out=c.esum[:, 8 * qt + j:8 * qt + j + 1])
                ins.then_inc(s["exps_ready"], 1)
            act.wait_ge(s["exps_ready"], H * (2 * qt + m + 1))
            act.sem_inc(s[f"side_free{side_pair(f's{qt}{m}')}"], 1)
    act.wait_ge(s["TT_ready"], LEVELS + 1)
    exps(0)
    act.wait_ge(s["side_ready"], SI["wT"] + 1)
    evacuate("ma1", c.mg[1], "mg_ready", ACT.Sigmoid)
    act.wait_ge(s["aT_in"], 1)
    act.wait_ge(s["side_ready"], SI["aT0"] + 1)
    exps(1)
    evacuate("mb0", c.mg[2], "mg_ready", ACT.Sigmoid)

    def squares_root(src, sq, ss, ready, out_sem, root, rt):
        act.wait_ge(s[ready], 1)
        act.activation(sq, src, ACT.Square).then_inc(s[out_sem], 1)
        act.wait_ge(s[root], 1)
        act.activation(rt, ss, ACT.Sqrt).then_inc(s[root], 1)
    act.wait_ge(s["oa_out"], NT)
    act.activation(c.flat["Yb"], c.flat["F"], ACT.Square).then_inc(s["oa_squares"], 1)
    act.wait_ge(s["oa_root"], 1)
    act.activation(c.ra, c.ra, ACT.Sqrt).then_inc(s["oa_root"], 1)
    act.wait_ge(s["gate_ready"], 2)
    act.wait_ge(s["ob_out"], 4)
    act.activation(c.flat["A"], c.flat["TT"], ACT.Square).then_inc(s["ob_squares"], 1)
    act.wait_ge(s["ob_root"], 1)
    act.activation(c.rb, c.rb, ACT.Sqrt).then_inc(s["ob_root"], 1)
    act.wait_ge(s["side_ready"], SI["yaT"] + 1)
    act.activation(c.flat["qT"], c.side[side_pair("yaT")], ACT.Copy).then_inc(s["yaT_ready"], 1)
    act.wait_ge(s["yb_ready"], 1)
    evacuate("mb1", c.mg[3], "mg_ready", ACT.Sigmoid)
    act.wait_ge(s["side_ready"], SI["ybT"] + 1)
    act.activation(c.flat["kT"], c.side[side_pair("ybT")], ACT.Copy).then_inc(s["ybT_ready"], 1)

    for n_, (half, t) in enumerate(PIECES):
        act.wait_ge(s["x1_ready"], n_ + 1)
        act.activation(c.squares, c.x[:, t, 512 * half:512 * (half + 1)], ACT.Square, accum_out=c.ss_piece[:, n_:n_ + 1])\
            .then_inc(s["ss1_ready"], 1)
        if n_ == len(PIECES) - 2:
            act.activation(c.scratch, c.eps, ACT.Sqrt)
        act.wait_ge(s["x1_transposed"], n_ + 1)
        act.activation(c.x1T[:, 4 * half:4 * half + 4, t * P:(t + 1) * P], x1T_out(c, half, t), ACT.Copy).then_inc(s["x1T_ready"], 1)
        act.wait_ge(s["ss1_ready"], n_ + 1)
    act.wait_ge(s["ss1_summed"], 1)
    act.activation(c.rx, c.ssx, ACT.Sqrt, scale=1.0 / D, bias=c.eps).then_inc(s["r1_root"], 1)
    act.wait_ge(s["r1_ready"], 1)
    for t in range(NT):
        act.activation(c.h2[:, t, :], c.x[:, t, :], ACT.Copy, scale=c.rx[:, t:t + 1]).then_inc(s["h2_ready"], 1)
    act.wait_ge(s["logits_ready"], len(PIECES))
    for t in range(NT):
        act.wait_ge(s["h2_ready"], t + 1)
        act.activation(c.high[:, t, :], c.h2[:, t, :], ACT.Copy).then_inc(s["high_ready"], 1)
    act.wait_ge(s["gexp_in"], 1)
    act.activation(c.r[:, 72:80], c.r[:, 72:80], ACT.Exp).then_inc(s["gexp_out"], 1)
    act.wait_ge(s["texp_in"], 1)
    act.activation(c.r[:, 144:146], c.r[:, 144:146], ACT.Exp).then_inc(s["texp_out"], 1)
    for t in range(NT):
        act.wait_ge(s["rest_ready"], t + 1)
        act.activation(c.mid[t], c.h2[:, t, :], ACT.Copy).then_inc(s["mid_ready"], 1)
    for k in range(0, KD, 2):
        act.wait_ge(s["gathered"], k + 1)
        act.activation(c.HgT[:, k, :], c.ps[:, k, :], ACT.Copy, scale=c.gffn[:, k:k + 1]).then_inc(s["HgT_even"], 1)

    act.wait_ge(s["starts_ready"], 1)
    wide = act.value_load(c.largest[0:1, 0:1], min_val=0, max_val=TOK)

    def windows(m, nwin):
        n = HID * m // P
        nq = P // m

        def window_start(expert, w):
            return act.value_load(c.starts[m, w][0:1, expert], min_val=0, max_val=SLOTS - m)

        def copy_window(start, buf):
            act.activation(c.window[buf][:, 0:KD * m].rearrange("p (k s) -> p k s", k=KD),
                           c.HgT[:, :, bass.ds(start, m)], ACT.Copy).then_inc(s["window_ready"], 1)

        def sigmoid(base, u, first):
            act.wait_ge(s["gu_ready"], base * nwin + (u + 1))
            need(act, s["act_ready"], base * nwin + (u - 1), first)
            act.activation(c.sg[u % 2][:, 0:n], c.ps[:, u % 2, 0:n], ACT.Sigmoid).then_inc(s["gate_sigmoid"], 1)

        def units(base, first, final):
            for u in range(RING * nwin):
                act.wait_ge(s["act_turned"], base * nwin + (u + 1))
                need(act, s["down_ready"], base * nwin + (u - 1), first)
                if nq == 4:
                    act.activation(c.actT[u % 2][0:64, 0:64], c.ps[0:64, u % 2, 0:64], ACT.Copy)
                    act.activation(c.actT[u % 2][64:P, 0:64], c.ps[64:P, u % 2, 64:P], ACT.Copy).then_inc(s["actT_ready"], 1)
                else:
                    act.activation(c.actT[u % 2][:, 0:2 * m], c.ps[:, u % 2, 0:2 * m], ACT.Copy).then_inc(s["actT_ready"], 1)
                nxt = u + 2
                if not (final and nxt >= RING * nwin):
                    e = base + nxt // nwin
                    copy_window(window_start(slice(e, e + 1) if first else bass.ds(e, 1), nxt % nwin), nxt % 2)
                if not (final and u == RING * nwin - 1):
                    sigmoid(base, u + 1, first)
                act.wait_ge(s["down_ready"], base * nwin + (u + 1))
                stack_rows(act.activation, c, m, u, range(nq // 2, nq) if nq > 1 else (1,), s["out_copied"], ACT.Copy)
        start = window_start(slice(0, 1), 0)
        act.wait_ge(s["HgT_even"], KD // 2)
        act.wait_ge(s["HgT_odd"], KD // 2)
        copy_window(start, 0)
        copy_window(window_start(slice(1 // nwin, 1 // nwin + 1), 1 % nwin), 1)
        sigmoid(0, 0, True)
        units(0, True, False)
        with act.Fori(1, EXPERTS // RING - 1) as it:
            units(it * RING, False, False)
        units(EXPERTS - RING, True, True)
    by_count(act, wide, windows)

    act.activation(c.scratch, c.eps, ACT.Sqrt)
    for t in range(NT):
        act.wait_ge(s["x2_ready"], t + 1)
        act.activation(c.HgT[:, 2 * t:2 * t + 2, 0:512],
                       c.x[:, t, :].rearrange("p (a b) -> p a b", a=2), ACT.Square, accum_out=c.ssx[:, t:t + 1])\
            .then_inc(s["ss2_ready"], 1)
        act.wait_ge(s["ss2_ready"], t + 1)
        act.activation(c.rx[:, t:t + 1], c.ssx[:, t:t + 1], ACT.Sqrt, scale=1.0 / D, bias=c.eps).then_inc(s["r2_root"], 1)
    for t in range(NT):
        act.wait_ge(s["r2_ready"], t + 1)
        act.wait_ge(s["y_ready"], t + 1)
        act.activation(c.y[:, t, 0:512], c.y[:, t, 0:512], ACT.Copy, scale=c.rx[:, t:t + 1]).then_inc(s["out_left_ready"], 1)


def stack_buffer(nq, u):
    return u // nq % 2 if nq < RING else 0


def stack_rows(copy, c, m, u, parts, done, *func):
    nq = P // m
    if nq == 1:
        (i,) = parts
        copy(c.Y[u % 2][:, 512 * i:512 * (i + 1)], c.ps[:, 2 + i, :], *func).then_inc(done, 1)
        return
    w = D // nq
    at = u % nq * m
    for q in parts:
        last = copy(c.Y[stack_buffer(nq, u)][at:at + m, w * q:w * (q + 1)], c.ps[q * m:(q + 1) * m, 2 + u % 2, 0:w], *func)
    last.then_inc(done, 1)


def need(eng, sem, value, first):
    if not first or value > 0:
        eng.wait_ge(sem, value)


def by_count(eng, largest, windows):
    (m0, n0), (m1, n1), (m2, n2) = PATHS
    with eng.If(largest <= m0):
        windows(m0, n0)
    with eng.Else():
        with eng.If(largest <= m1):
            windows(m1, n1)
        with eng.Else():
            windows(m2, n2)


def tensor_program(pe, c, io):
    s = c.s
    T4 = [(t, h) for t in range(NT) for h in range(H)]

    def side(name):
        v = side_reuse(name)
        if v:
            pe.wait_ge(s[f"side_free{side_pair(name)}"], v)
        return c.side[side_pair(name)]

    def blk(ap, i, n=P):
        return ap[:, i * n:(i + 1) * n]

    pe.wait_ge(s["ident_ready"], 1)
    for t in range(NT):
        pe.wait_ge(s[f"x_loaded{t}"], 16)
        for k in range(KD):
            last = pe.transpose(c.ps[:, k // 2, (k % 2) * 256 + t * P:(k % 2) * 256 + (t + 1) * P],
                                c.x[:, t, k * P:(k + 1) * P], c.ident)
    last.then_inc(s["x_transposed"], 1)
    pe.wait_ge(s["consts_loaded"], 48)
    ps = side("consts")
    pe.transpose(ps[:, 0:64], c.cst_in[:, :], c.ident[0:64, 0:64]).then_inc(s["side_ready"], 1)
    pe.wait_ge(s["rx_ready"], 1)
    for t in range(NT):
        last = pe.matmul(blk(c.side[1], t), c.rx[:, t:t + 1].to_broadcast([P, P]), c.ident, start=True, stop=True)
    last.then_inc(s["rx_turned"], 1)

    def project(name, part, ks=range(KD), between=None):
        i = CI[name]
        _, _, n, kind = CHUNKS[i]
        w = c.stage[i % 2][:, 0:KD * n].rearrange("p (k n) -> p k n", k=KD)
        if part == 0 and ks[0] == 0 and i > 0:
            pe.wait_ge(s[f"stage_loaded{i % 2}"], 16 * (i // 2 + 1))
            if i >= 2:
                pe.wait_ge(s[f"pair_free{i % 2}"], i // 2)
        for k in ks:
            if part == 0 and i == 0:
                pe.wait_ge(s["hT_ready"], max(k + 1, 2))
                if k == 0:
                    pe.wait_ge(s["first_half_loaded"], 16)
                elif k == KD // 2:
                    pe.wait_ge(s["stage_loaded0"], 16)
            if kind == "T":
                out, lhs, rhs = blk(c.pair[i % 2], part, TOK), w[:, k, part * P:(part + 1) * P], c.hT[:, k, :]
            else:
                out, lhs, rhs = blk(c.pair[i % 2], part, 512), c.hT[:, k, part * P:(part + 1) * P], w[:, k, n - 512:n]
            last = pe.matmul(out, lhs, rhs, start=(k == 0), stop=(k == KD - 1))
            if between:
                between(k)
        if ks[-1] == KD - 1:
            last.then_inc(s["proj_ready"], 1)

    def turn(name, src):
        ps = side(name)
        for i in range(8):
            last = pe.transpose(blk(ps, i), src(i), c.ident)
        last.then_inc(s["side_ready"], 1)

    def each(name, lhs, rhs):
        ps = side(name)
        for i, (t, h) in enumerate(T4):
            last = pe.matmul(blk(ps, i), lhs(t, h), rhs(t, h), start=True, stop=True)
        last.then_inc(s["side_ready"], 1)

    def tile(ap, h, t):
        return ap[:, h, t * P:(t + 1) * P]

    for name in ("gk", "gq"):
        for b in range(4):
            project(name, b)
    project("bdg", 0)
    project("bdg", 1)
    i = CI["bdg"]
    wbd = c.stage[i % 2][:, 0:KD * 520].rearrange("p (k n) -> p k n", k=KD)
    side("bd")

    def beta_and_decay(k):
        for t in range(NT):
            last = pe.matmul(c.side[side_pair("bd")][:, 512 * t:512 * t + 8], c.hT[:, k, t * P:(t + 1) * P], wbd[:, k, 0:8],
                             start=(k == 0), stop=(k == KD - 1))
        if k == KD - 1:
            last.then_inc(s["side_ready"], 1)
    project("gv", 0, between=beta_and_decay)
    project("gv", 1)
    side("ss")
    pe.wait_ge(s["masks_ready"], 1)
    pe.wait_ge(s["squares_ready"], 2)

    def lengths(k):
        for i in (2 * k, 2 * k + 1):
            t, h = T4[i % 8]
            last = pe.matmul(c.side[side_pair("ss")][:, i:i + 1], tile((c.sqk, c.sqq)[i // 8], h, t), c.ones[:, 0:1], start=True, stop=True)
        if k == KD - 1:
            last.then_inc(s["side_ready"], 1)
    project("gv", 2, between=lengths)
    pe.wait_ge(s["rn_ready"], 1)
    for j, name in enumerate(("rnk", "rnq")):
        each(name, lambda t, h, j=j: c.rn[:, 8 * j + 4 * t + h:8 * j + 4 * t + h + 1].to_broadcast([P, P]), lambda t, h: c.ident)
    project("gv", 3)
    ps = side("gsum")
    pe.wait_ge(s["g_ready"], 1)
    for t in range(NT):
        g = c.g[:, 4 * t:4 * t + 4]
        pe.matmul(ps[:, 4 * t:4 * t + 4], c.upper, g, start=True, stop=True)
        pe.matmul(ps[:, 8 + 4 * t:12 + 4 * t], c.chunk, g, start=True, stop=True)
        pe.matmul(ps[:, 16 + 8 * t:20 + 8 * t], c.half0, g, start=True, stop=True)
        last = pe.matmul(ps[:, 20 + 8 * t:24 + 8 * t], c.half1, g, start=True, stop=True)
    last.then_inc(s["side_ready"], 1)
    each("grow", lambda t, h: c.g[:, 4 * t + h:4 * t + h + 1].to_broadcast([P, P]), lambda t, h: c.upper)
    project("dq", 0)
    pe.wait_ge(s["k_normed"], 1)
    each("gram", lambda t, h: tile(c.ck, h, t), lambda t, h: tile(c.ck, h, t))
    project("dq", 1)
    pe.wait_ge(s["q_normed"], 1)
    each("intra", lambda t, h: tile(c.ck, h, t), lambda t, h: tile(c.cq, h, t))
    project("dq", 2)
    project("dq", 3)
    turn("ktok", lambda i: tile(c.ck, i % 4, i // 4))
    project("dk", 0)
    pe.wait_ge(s["qkv_ready"], 3)
    turn("vtok", lambda i: tile(c.cv, i % 4, i // 4))
    project("dk", 1)
    pe.wait_ge(s["b1_ready"], 1)
    turn("b1", lambda i: c.Yb[:, i // 4, i % 4, :])
    project("dk", 2)

    def level_y(lv):
        pe.wait_ge(s["TT_ready"], lv)
        each(f"Y{lv}", lambda t, h: c.A[:, t, h, :], lambda t, h: c.TT[:, t, h, :])

    def level_t(lv):
        pe.wait_ge(s["Y_ready"], lv)
        pe.wait_ge(s["T_ready"], lv)
        each(f"TT{lv}", lambda t, h: c.T[:, t, h, :], lambda t, h: c.Yb[:, t, h, :])
        if lv < LEVELS:
            each(f"T{lv}", lambda t, h: c.Yb[:, t, h, :], lambda t, h: c.T[:, t, h, :])
    level_y(1)
    project("dk", 3, range(KD // 2))
    level_t(1)
    project("dk", 3, range(KD // 2, KD))
    level_y(2)
    project("dv", 0)
    level_t(2)
    project("dv", 1)
    level_y(3)
    project("ma0", 0)
    level_t(3)
    project("ma0", 1)
    level_y(4)
    project("ma0", 2)
    level_t(4)
    project("ma0", 3)
    level_y(5)
    project("ma1", 0)
    level_t(5)
    project("ma1", 1)
    pe.wait_ge(s["TT_ready"], LEVELS + 1)
    pe.wait_ge(s["tok_ready"], 3)
    each("u", lambda t, h: c.TT[:, t, h, :], lambda t, h: c.vb[:, t, h, :])
    each("wT", lambda t, h: c.wrhs[:, t, h, :], lambda t, h: c.TT[:, t, h, :])

    def scores(qt):
        pe.wait_ge(s["dq_ready"], 1)
        pe.wait_ge(s["dk_ready"], 1)
        for m in range(2):
            ps = side(f"s{qt}{m}").rearrange("p (h k) -> p h k", h=H)
            rows = slice(DH * m, DH * (m + 1))
            for h in range(H):
                last = pe.matmul(ps[:, h, 0:P * (qt + 1)], c.qT[rows, h, qt * P:(qt + 1) * P],
                                 c.kT[rows, h, 0:P * (qt + 1)], start=True, stop=True)
            last.then_inc(s["side_ready"], 1)

    def turn_probs(qt):
        ps = side(f"aT{qt}")
        pe.wait_ge(s["aT_in"], qt + 1)
        for h in range(H):
            for kt in range(qt + 1):
                last = pe.transpose(blk(ps, h * (qt + 1) + kt), c.es[:, h, kt * P:(kt + 1) * P], c.ident)
        last.then_inc(s["side_ready"], 1)

    def weigh_values(qt):
        ps = side(f"oa{qt}")
        pe.wait_ge(s["aT_ready"], qt + 1)
        pe.wait_ge(s["dv_ready"], 1)
        for h in range(H):
            for kt in range(qt + 1):
                last = pe.matmul(blk(ps, h), blk(c.aT, h * (qt + 1) + kt), c.dv[:, kt, h * P:(h + 1) * P],
                                 start=(kt == 0), stop=(kt == qt))
        last.then_inc(s["side_ready"], 1)

    def state_in(n):
        ps = side(f"ws{n}")
        pe.wait_ge(s["S_ready"], n)
        for h in range(H):
            last = pe.matmul(blk(ps, h), c.wT[:, n // 2, h, :], c.S[:, h, :], start=True, stop=True)
        last.then_inc(s["side_ready"], 1)

    def state_out(n):
        t = n // 2
        ps = side(f"so{n}")
        pe.wait_ge(s["vn_ready"], n + 1)
        for h in range(H):
            if n:
                pe.matmul(blk(ps, h), c.qdec[:, t, h, :], c.S[:, h, :], start=True, stop=False)
            last = pe.matmul(blk(ps, h), c.attnT[:, t, h, :], c.vn[n % 2][:, h, :], start=(n == 0), stop=True)
        if n < 3:
            for h in range(H):
                last = pe.matmul(blk(ps, H + h), c.kdec[:, t, h, :], c.vn[n % 2][:, h, :], start=True, stop=True)
        last.then_inc(s["side_ready"], 1)

    scores(0)
    project("ma1", 2)
    pe.wait_ge(s["wT_ready"], 1)
    state_out(0)
    project("ma1", 3)
    turn_probs(0)
    state_in(1)
    project("mb0", 0)
    weigh_values(0)
    state_out(1)
    project("mb0", 1)
    scores(1)
    project("mb0", 2)
    state_in(2)
    project("mb0", 3)
    state_out(2)
    turn_probs(1)
    project("mb1", 0)
    state_in(3)
    weigh_values(1)
    project("mb1", 1)
    state_out(3)
    project("mb1", 2)
    pe.wait_ge(s["ya_ready"], 1)
    turn("yaT", lambda i: c.oa[:, i % 2, (i // 2) * P:(i // 2 + 1) * P])
    project("mb1", 3)

    for n in range(4):
        j, half = n // 2, n % 2
        i = NCH + j
        w = c.stage[i % 2][:, 0:4096].rearrange("p (k n) -> p k n", k=H)
        yT = (c.yaT, c.ybT)[j]
        if n == 1:
            pe.wait_ge(s["yb_ready"], 1)
            turn("ybT", lambda i: c.ob[:, i % 2, (i // 2) * P:(i // 2 + 1) * P])
        pe.wait_ge(s[f"stage_loaded{i % 2}"], 16 * (i // 2 + 1))
        pe.wait_ge(s["yaT_ready" if j == 0 else "ybT_ready"], 1)
        if j == 0:
            pe.wait_ge(s[f"pair_free{1 - half}"], (NCH + half) // 2)
        else:
            pe.wait_ge(s["branch_used"], n - 1)
        for b in range(4):
            for k in range(H):
                last = pe.matmul(blk(branch_out(c, half), b, TOK), w[:, k, (4 * half + b) * P:(4 * half + b + 1) * P], yT[:, k, :],
                                 start=(k == 0), stop=(k == H - 1))
        last.then_inc(s["branch_ready"], 1)
    pe.wait_ge(s["ybT_ready"], 1)
    pe.wait_ge(s["yaT_ready"], 1)
    def mix(n_, ks):
        half, t = PIECES[n_]
        i = NCH + 2 + half
        w = c.stage[i % 2][:, 0:4096].rearrange("p (k n) -> p k n", k=KD)
        pe.wait_ge(s[f"stage_loaded{i % 2}"], 16 * (i // 2 + 1))
        for k in ks:
            if n_ == 0 and k % 4 == 0:
                pe.wait_ge(s["merged_ready"], k // 4 + 1)
            mg = c.mg[k // 4][:, (k % 4) * TOK + t * P:(k % 4) * TOK + (t + 1) * P]
            last = pe.matmul(c.ps[:, 4 + 2 * t + half, :], mg, w[:, k, :], start=(k == 0), stop=(k == KD - 1))
        if ks[-1] == KD - 1:
            last.then_inc(s["mix_out"], 1)

    def turn_x1(n_):
        half, t = PIECES[n_]
        pe.wait_ge(s["x1_ready"], n_ + 1)
        if n_:
            pe.wait_ge(s["x1T_ready"], n_)
        out = x1T_out(c, half, t)
        for b in range(4):
            last = pe.transpose(out[:, b, :], c.x[:, t, (4 * half + b) * P:(4 * half + b + 1) * P], c.ident)
        last.then_inc(s["x1_transposed"], 1)

    def logits(n_):
        half, t = PIECES[n_]
        pe.wait_ge(s["x1T_ready"], n_ + 1)
        for k in range(4 * half, 4 * half + 4):
            last = pe.matmul(logits_out(c, t), c.x1T[:, k, t * P:(t + 1) * P], c.rw[:, k, :], start=(k == 0), stop=(k == KD - 1))
        last.then_inc(s["logits_ready"], 1)
    ks = list(range(KD))
    pe.wait_ge(s["rw_ready"], 1)
    mix(0, ks)
    mix(1, ks)
    turn_x1(0)
    mix(2, ks)
    turn_x1(1)
    logits(0)
    mix(3, ks[:4])
    turn_x1(2)
    logits(1)
    mix(3, ks[4:])
    logits(2)
    turn_x1(3)
    logits(3)
    pe.wait_ge(s["picks_ready"], 1)
    picks = c.r[:, 240:304]
    pe.matmul(c.ps[:, 1, 0:64], c.before, picks, start=True, stop=False)
    pe.matmul(c.ps[:, 1, 32:64], c.ones, picks[:, 0:32], start=False, stop=True)
    pe.matmul(c.ps[:, 1, 64:96], c.ones, picks[:, 0:32], start=True, stop=False)
    pe.matmul(c.ps[:, 1, 64:96], c.ones, picks[:, 32:64], start=False, stop=True).then_inc(s["ranks_ready"], 1)
    pe.wait_ge(s["onehot_ready"], 2)
    pe.wait_ge(s["high_ready"], NT)
    pe.wait_ge(s["mid_ready"], NT)
    pe.wait_ge(s["low_ready"], NT)
    parts = [(t, part) for t in range(NT) for part in (c.high[:, t, :], c.mid[t], c.low[:, t, :])]
    for k in range(KD):
        if k == 2:
            for i in range(8):
                last = pe.matmul(blk(c.side[1], i), c.r[:, 480 + i:481 + i].to_broadcast([P, P]), c.ident, start=True, stop=True)
            last.then_inc(s["rows_turned"], 1)
        if k == 6:
            pe.wait_ge(s["rows_ready"], 1)
        for j, (t, part) in enumerate(parts):
            last = pe.matmul(c.ps[:, k, :], part[:, k:D:KD], c.onehot[:, t, :], start=(j == 0), stop=(j == len(parts) - 1))
        last.then_inc(s["gathered"], 1)

    wide = pe.value_load(c.largest[0:1, 0:1], min_val=0, max_val=TOK)

    def windows(m, nwin):
        nq = P // m
        n = HID // nq

        def quad(q):
            return slice(q * m, (q + 1) * m)

        def at_place(base, u, first):
            j = u // nwin
            if first:
                return place(base + j)
            return (j - SPARES) % RING, (j - SPARES) // RING + 1

        def hidden(base, u, first, ks=range(KD)):
            j, more = at_place(base, u, first)
            if ks[0] == 0:
                pe.wait_ge(s["window_ready"], base * nwin + (u + 1))
                if u % nwin == 0:
                    pe.wait_ge(s[f"gateup{j}"], (0 if first else base * (32 // RING)) + 32 * more)
                need(pe, s["actT_ready"], base * nwin + (u - 1), first)
            for k in ks:
                for q in range(nq):
                    start, step = {4: (P * (q // 2) + q % 2, 2), 2: (q, 2), 1: (0, 1)}[nq]
                    last = pe.matmul(c.ps[quad(q), u % 2, 0:2 * n], c.window[u % 2][:, k * m:(k + 1) * m],
                                     c.gu_w[j][:, :, k, start:start + step * (n - 1) + 1:step],
                                     start=(k == 0), stop=(k == KD - 1))
            if ks[-1] == KD - 1:
                last.then_inc(s["gu_ready"], 1)

        def turn_act(base, u):
            pe.wait_ge(s["act_ready"], base * nwin + (u + 1))
            act, bank = c.act[u % 2], u % 2
            if nq == 4:
                for r in range(2):
                    last = pe.matmul(c.ps[64 * r:64 * r + 64, bank, 0:P], act[:, 0:64], c.ident, start=True, stop=True)
            elif nq == 2:
                last = pe.transpose(c.ps[:, bank, 0:P], act[:, 0:P], c.ident)
            else:
                for kk in range(2):
                    last = pe.transpose(c.ps[:, bank, kk * P:(kk + 1) * P], act[:, kk:HID:2], c.ident)
            last.then_inc(s["act_turned"], 1)

        def down(base, u, first):
            j, more = at_place(base, u, first)
            if u % nwin == 0:
                pe.wait_ge(s[f"down{j}"], (0 if first else base * (16 // RING)) + 16 * more)
            pe.wait_ge(s["actT_ready"], base * nwin + (u + 1))
            need(pe, s["out_copied"], 2 * base * nwin + 2 * (u - 1 if m < P else u), first)
            width = min(512, D // nq)
            for piece in range(D // nq // width):
                for kk in range(2):
                    for q in range(nq):
                        at = q * (D // nq) + piece * width
                        last = pe.matmul(c.ps[quad(q), out_bank(m, u) + piece, 0:width], c.actT[u % 2][:, kk * m:(kk + 1) * m],
                                         c.down_w[j][:, kk, at:at + width], start=(kk == 0), stop=(kk == 1))
            last.then_inc(s["down_ready"], 1)

        def scatter(rnd, u, end=False):
            pe.wait_ge(s["out_copied"], rnd * (2 * RING * nwin) + 2 * (u + 1))
            pe.wait_ge(s["Se_ready"], rnd * (RING * nwin // nq) + (u + 1) // nq)
            i = stack_buffer(nq, u % (RING * nwin))
            for t in range(NT):
                for half in range(2):
                    last = pe.matmul(y_out(c, half, t), c.S_e[i][:, t * P:(t + 1) * P], c.Y[i][:, 512 * half:512 * (half + 1)],
                                     start=False, stop=False, skip_group_check=True)
                if end:
                    last.then_inc(s["last_scatter"], 1)
            if not end:
                last.then_inc(s["scattered"], 1)

        def units(rnd, first, final):
            nu = RING * nwin
            base = rnd * RING
            for u in range(nu):
                more = not (final and u == nu - 1)
                if more:
                    hidden(base, u + 1, first, range(KD // 2))
                turn_act(base, u)
                if more:
                    hidden(base, u + 1, first, range(KD // 2, KD))
                if u % nq == 0 and not (first and base + u == 0):
                    scatter(rnd, u - 1)
                down(base, u, first)
            if final:
                scatter(rnd, nu - 1, True)
        pe.wait_ge(s["zeros_ready"], 1)
        pe.wait_ge(s["HgT_even"], KD // 2)
        pe.wait_ge(s["HgT_odd"], KD // 2)
        for b in range(4):
            pe.matmul(c.ps[:, 4 + b, :].rearrange("p (a f) -> p a f", a=4), c.zeros[0:1, :],
                      c.zeros[0:1, :].rearrange("p (a f) -> p a f", a=1).to_broadcast([1, 4, P]),
                      start=True, stop=False, skip_group_check=True)
        hidden(0, 0, True)
        units(0, True, False)
        units(1, True, False)
        with pe.Fori(2, EXPERTS // RING - 1) as it:
            units(it, False, False)
        units(EXPERTS // RING - 1, True, True)
    by_count(pe, wide, windows)


def beta_decay_out(c):
    return c.side[side_pair("bd")].rearrange("p (t f) -> p t f", t=NT)[:, :, 0:8].rearrange("p t (a h) -> p t a h", a=2)


def branch_out(c, half):
    return c.pair[1 - half]


def x1T_out(c, half, t):
    return c.ps[:, 2 * half:2 * half + 2, :].rearrange("p b (a f) -> p (b a) f", a=2)[:, :, t * P:(t + 1) * P]


def logits_out(c, t):
    return c.ps[:, 4 + 2 * t, 0:GROUPS + EXPERTS]


def y_out(c, half, t):
    return c.ps[:, 4 + 2 * t + half, :]


def out_bank(m, u):
    return 2 + u % 2 if m < P else 2


def vector_program(v, c, io):
    s = c.s
    n = [0]

    def chain(ins):
        n[0] += 1
        ins.then_inc(s["dve_chain"], 1)

    def settle():
        v.wait_ge(s["dve_chain"], n[0])

    def col(ap, i):
        return ap[:, i:i + 1]

    def blk(ap, i, w=P):
        return ap[:, i * w:(i + 1) * w]

    def side(name):
        v.wait_ge(s["side_ready"], SI[name] + 1)
        return c.side[side_pair(name)]

    def side_done(name, ins):
        ins.then_inc(s[f"side_free{side_pair(name)}"], 1)

    v.memset(c.eps, EPS).then_inc(s["eps_ready"], 1)
    v.wait_ge(s["rx_root"], 1)
    v.reciprocal(c.rx, c.rx).then_inc(s["rx_ready"], 1)
    ps = side("consts")
    v.tensor_copy(c.cst, ps[:, 0:64]).then_inc(s["cst_ready"], 1)
    v.wait_ge(s["cst_ready"], 1)
    v.sem_inc(s[f"side_free{side_pair('consts')}"], 1)
    v.wait_ge(s["rx_turned"], 1)
    chain(v.tensor_copy(c.rx_row, c.side[1][:, 0:TOK]))
    settle()
    v.wait_ge(s["x_transposed"], 1)
    v.wait_ge(s["ssx_ready"], NT)
    for k in range(KD):
        v.scalar_tensor_tensor(out=c.hT[:, k, :], in0=c.ps[:, k // 2, (k % 2) * TOK:(k % 2 + 1) * TOK], scalar=col(c.cst, k),
                               in1=c.rx_row, op0=ALU.mult, op1=ALU.mult).then_inc(s["hT_ready"], 1)
    v.wait_ge(s["router_loaded"], 80)
    v.tensor_tensor(c.rw[:, :, :], c.rw[:, :, :], c.cst[:, 56:64].rearrange("p (k a) -> p k a", a=1).to_broadcast([P, KD, GROUPS + EXPERTS]),
                    ALU.mult).then_inc(s["rw_ready"], 1)

    def conv(name, dst, first):
        i = CI[name]
        v.wait_ge(s["proj_ready"], parts_before(i) + 4)
        src = c.pair[i % 2]
        for back in range(TAPS):
            for b in range(4):
                w = col(c.cst, 8 + 12 * (TAPS - 1 - back) + first + b)
                if back == 0:
                    ins = v.tensor_scalar(dst[:, b, :], blk(src, b, TOK), w, None, ALU.mult)
                else:
                    o = dst[:, b, back:TOK]
                    ins = v.scalar_tensor_tensor(out=o, in0=src[:, b * TOK:(b + 1) * TOK - back], scalar=w, in1=o,
                                                 op0=ALU.mult, op1=ALU.add)
                if back == TAPS - 1 and b == 3:
                    ins.then_inc(s[f"pair_free{i % 2}"], 1)
                else:
                    chain(ins)
            if back < TAPS - 1:
                settle()
        v.wait_ge(s[f"pair_free{i % 2}"], i // 2 + 1)
        settle()
        v.sem_inc(s["conv_ready"], 1)

    def silu(j, name, dst):
        v.wait_ge(s["conv_sig"], j + 1)
        v.tensor_tensor(dst, dst, c.sig[name], ALU.mult).then_inc(s["qkv_ready"], 1)
    conv("gk", c.ck, 4)
    silu(0, "gk", c.ck)
    conv("gq", c.cq, 0)
    silu(1, "gq", c.cq)
    i = CI["bdg"]
    v.wait_ge(s["gate_sig"], 1)
    v.tensor_tensor(c.flat["gate"], c.flat["gate"], c.pair[i % 2], ALU.mult).then_inc(s["gate_ready"], 1)
    v.wait_ge(s["gate_ready"], 1)
    v.sem_inc(s[f"pair_free{i % 2}"], 1)
    v.wait_ge(s["vectors_loaded"], 64)
    side("bd")
    bd = beta_decay_out(c)
    v.wait_ge(s["beta_ready"], 1)
    for t in range(NT):
        chain(v.tensor_tensor(blk(c.z, t, 4), bd[:, t, 1, :], c.dtb, ALU.add))
    settle()
    v.sem_inc(s[f"side_free{side_pair('bd')}"], 1)
    chain(v.tensor_scalar(c.zm, c.z, 0.0, None, ALU.max))
    settle()
    v.scalar_tensor_tensor(out=c.z, in0=c.zm, scalar=-2.0, in1=c.z, op0=ALU.mult, op1=ALU.add).then_inc(s["g_in"], 1)
    v.wait_ge(s["lambda_loaded"], 64)
    chain(v.tensor_tensor(c.lamrows[:, 0, :], c.lamrows[:, 0, :], c.lamrows[:, 1, :], ALU.mult))
    chain(v.tensor_tensor(c.lamrows[:, 2, :], c.lamrows[:, 2, :], c.lamrows[:, 3, :], ALU.mult))
    settle()
    v.tensor_reduce(c.lam[:, 0:2], c.lamrows[:, 0:4:2, :], AX_X, ALU.add).then_inc(s["lam_in"], 1)
    ps = side("ss")
    v.tensor_scalar(c.rn, ps[:, 0:16], EPS, None, ALU.add).then_inc(s["rn_root"], 1)
    v.wait_ge(s["rn_root"], 2)
    chain(v.reciprocal(c.rn, c.rn))
    settle()
    v.tensor_scalar(c.rn[:, 8:16], c.rn[:, 8:16], float(P) ** -0.5, None, ALU.mult).then_inc(s["rn_ready"], 1)
    v.sem_inc(s[f"side_free{side_pair('ss')}"], 1)
    v.wait_ge(s["dec_exp"], 3)
    chain(v.tensor_tensor(c.sp, c.zm, c.z, ALU.add))
    settle()
    for t in range(NT):
        last = v.scalar_tensor_tensor(out=blk(c.g, t, 4), in0=blk(c.sp, t, 4), scalar=-1.0, in1=c.nea, op0=ALU.mult, op1=ALU.mult)
        if t == 0:
            chain(last)
    last.then_inc(s["g_ready"], 1)
    for name, dst, sem in (("rnk", c.ck, "k_normed"), ("rnq", c.cq, "q_normed")):
        ps = side(name).rearrange("p (t h f) -> p t h f", t=NT, h=H)
        for t in range(NT):
            d = dst[:, :, t * P:(t + 1) * P]
            last = v.tensor_tensor(d, d, ps[:, t], ALU.mult)
            if t == 0:
                chain(last)
        side_done(name, last)
        v.wait_ge(s[f"side_free{side_pair(name)}"], side_reuse(name) + 1)
        settle()
        v.sem_inc(s[sem], 1)
    ps = side("gsum")
    chain(v.tensor_copy(c.run_sum, ps[:, 0:8]))
    chain(v.tensor_copy(c.chunk_sum, ps[:, 8:16]))
    chain(v.tensor_copy(c.sums_in[:, 0:8], ps[:, 0:8]))
    side_done("gsum", v.tensor_copy(c.sums_in[:, 16:32], ps[:, 16:32]))
    settle()
    v.wait_ge(s[f"side_free{side_pair('gsum')}"], side_reuse("gsum") + 1)
    v.tensor_tensor(c.sums_in[:, 8:16], c.chunk_sum, c.run_sum, ALU.subtract).then_inc(s["gsum_ready"], 1)
    ps = side("grow")
    v.wait_ge(s["squares_ready"], 2)
    v.wait_ge(s["side_ready"], SI["ss"] + 1)
    for j, (buf, op) in enumerate((("T", ALU.max), ("attnT", ALU.min))):
        for i in range(8):
            last = v.tensor_scalar(blk(c.flat[buf], i), blk(ps, i), col(c.run_sum, i), 0.0, ALU.subtract, op)
            if i < 7:
                chain(last)
        last.then_inc(s["grow_pre"], 1)
    conv("gv", c.cv, 8)
    silu(2, "gv", c.cv)
    def masked(buf, mask):
        return v.tensor_tensor(c.flat[buf].rearrange("p (a f) -> p a f", a=8), c.flat[buf].rearrange("p (a f) -> p a f", a=8),
                               mask.rearrange("p (a f) -> p a f", a=1).to_broadcast([P, 8, P]), ALU.mult)
    v.wait_ge(s["grow_exp"], 1)
    v.wait_ge(s["masks_ready"], 1)
    chain(masked("T", c.lower))
    v.wait_ge(s["grow_exp"], 2)
    chain(masked("attnT", c.upper))
    settle()
    v.wait_ge(s["gsum_exp"], 1)
    chain(v.tensor_tensor(c.bexp, c.beta, c.sums_exp[:, 0:8], ALU.mult))
    ps = side("gram")
    for i in range(8):
        last = v.scalar_tensor_tensor(out=blk(c.flat["A"], i), in0=blk(ps, i), scalar=col(c.beta, i), in1=blk(c.flat["T"], i),
                                      op0=ALU.mult, op1=ALU.mult)
        if i < 7:
            chain(last)
    side_done("gram", last)
    ps = side("intra")
    side_done("intra", v.tensor_tensor(c.flat["attnT"], c.flat["attnT"], ps, ALU.mult))
    v.wait_ge(s[f"side_free{side_pair('gram')}"], side_reuse("gram") + 1)
    settle()
    A8, Y8 = (c.flat[x].rearrange("p (a f) -> p a f", a=8) for x in ("A", "Yb"))
    T8, TT8 = (c.flat[x].rearrange("p (a f) -> p a f", a=8) for x in ("T", "TT"))

    def all8(m):
        return m.rearrange("p (a f) -> p a f", a=1).to_broadcast([P, 8, P])
    v.tensor_tensor(Y8, A8, all8(c.m1), ALU.mult).then_inc(s["b1_ready"], 1)
    cq4 = c.cq.rearrange("p h (t f) -> p h t f", t=NT)
    ps = side("ktok")
    for i in range(8):
        chain(v.tensor_scalar(blk(c.flat["wrhs"], i), blk(ps, i), col(c.bexp, i), None, ALU.mult))
    for i in range(8):
        last = v.tensor_scalar(blk(c.flat["kdec"], i), blk(ps, i), col(c.sums_exp, 8 + i), None, ALU.mult)
        if i < 7:
            chain(last)
    side_done("ktok", last)
    v.wait_ge(s[f"side_free{side_pair('ktok')}"], side_reuse("ktok") + 1)
    settle()
    v.sem_inc(s["tok_ready"], 2)
    ps = side("vtok")
    for i in range(8):
        last = v.tensor_scalar(blk(c.flat["vb"], i), blk(ps, i), col(c.beta, i), None, ALU.mult)
        if i < 7:
            chain(last)
    side_done("vtok", last)
    v.wait_ge(s[f"side_free{side_pair('vtok')}"], side_reuse("vtok") + 1)
    settle()
    v.sem_inc(s["tok_ready"], 1)
    v.wait_ge(s["b1_ready"], 1)
    v.tensor_tensor(T8, all8(c.ident), Y8, ALU.subtract).then_inc(s["T_ready"], 1)
    ps = side("b1")
    last = v.tensor_tensor(TT8, all8(c.ident), ps.rearrange("p (a f) -> p a f", a=8), ALU.subtract)
    last.then_inc(s["TT_ready"], 1)
    v.wait_ge(s["TT_ready"], 1)
    v.sem_inc(s[f"side_free{side_pair('b1')}"], 1)
    for lv in range(1, LEVELS + 1):
        ps = side(f"Y{lv}").rearrange("p (a f) -> p a f", a=8)
        v.tensor_tensor(Y8, ps, all8(c.levelT[lv - 1]), ALU.mult).then_inc(s["Y_ready"], 1)
        v.wait_ge(s["Y_ready"], lv)
        v.sem_inc(s[f"side_free{side_pair(f'Y{lv}')}"], 1)
        ps = side(f"TT{lv}")
        v.tensor_tensor(c.flat["TT"], c.flat["TT"], ps, ALU.subtract).then_inc(s["TT_ready"], 1)
        v.wait_ge(s["TT_ready"], lv + 1)
        v.sem_inc(s[f"side_free{side_pair(f'TT{lv}')}"], 1)
        if lv < LEVELS:
            ps = side(f"T{lv}")
            v.tensor_tensor(c.flat["T"], c.flat["T"], ps, ALU.subtract).then_inc(s["T_ready"], 1)
            v.wait_ge(s["T_ready"], lv + 1)
            v.sem_inc(s[f"side_free{side_pair(f'T{lv}')}"], 1)
        if lv == 1:
            for t in range(NT):
                chain(v.tensor_tensor(c.E[:, t], c.E[:, t], c.cq[:, :, t * P:(t + 1) * P], ALU.mult))
            settle()
            v.tensor_copy(c.flat["cq"], c.flat["EwT"]).then_inc(s["qdec_ready"], 1)
    side_done("u", v.tensor_copy(c.flat["cv"], side("u")))
    v.wait_ge(s["qdec_ready"], 1)
    side_done("wT", v.tensor_copy(c.flat["EwT"], side("wT")))
    v.wait_ge(s[f"side_free{side_pair('wT')}"], side_reuse("wT") + 1)
    v.wait_ge(s[f"side_free{side_pair('u')}"], side_reuse("u") + 1)
    v.sem_inc(s["wT_ready"], 1)

    def maxima(qt):
        nk = P * (qt + 1)
        for m in range(2):
            ps = side(f"s{qt}{m}").rearrange("p (h k) -> p h k", h=H)
            chain(v.memset(ps[0:CHUNK, :, nk - CHUNK:nk], -BIG))
            settle()
            nm = c.negmax[:, 8 * qt + 4 * m:8 * qt + 4 * m + 4]
            chain(v.tensor_reduce(nm, ps[:, :, 0:nk], AX_X, ALU.max))
            settle()
            v.tensor_scalar(nm, nm, -DH ** -0.5, None, ALU.mult).then_inc(s["negmax_ready"], 1)

    def combine(qt):
        nk = P * (qt + 1)
        v.wait_ge(s["exps_ready"], 8 * (qt + 1))
        cf = c.coef[:, 8 * qt:8 * qt + 8]
        chain(v.reciprocal(cf, c.esum[:, 8 * qt:8 * qt + 8]))
        settle()
        chain(v.tensor_scalar(cf[:, 4:8], cf[:, 4:8], c.lamw[:, 0:1], None, ALU.mult))
        settle()
        for h in range(H):
            chain(v.tensor_scalar(c.es[:, 4 + h, 0:nk], c.es[:, 4 + h, 0:nk], col(cf, 4 + h), None, ALU.mult))
        settle()
        for h in range(H):
            last = v.scalar_tensor_tensor(out=c.es[:, h, 0:nk], in0=c.es[:, h, 0:nk], scalar=col(cf, h), in1=c.es[:, 4 + h, 0:nk],
                                          op0=ALU.mult, op1=ALU.add)
            if h < H - 1:
                chain(last)
        last.then_inc(s["aT_in"], 1)

    def probs_turned(qt):
        w = 512 * (qt + 1)
        v.tensor_copy(c.aT[:, 0:w], side(f"aT{qt}")[:, 0:w]).then_inc(s["aT_ready"], 1)
        v.wait_ge(s["aT_ready"], qt + 1)
        v.sem_inc(s[f"side_free{side_pair(f'aT{qt}')}"], 1)

    def attended(qt):
        v.tensor_copy(c.oa[:, qt, :], side(f"oa{qt}")[:, 0:512]).then_inc(s["oa_out"], 1)
        v.wait_ge(s["oa_out"], qt + 1)
        v.sem_inc(s[f"side_free{side_pair(f'oa{qt}')}"], 1)

    def new_values(n_):
        rows = slice(CHUNK * (n_ % 2), CHUNK * (n_ % 2) + CHUNK)
        dst = c.vn[n_ % 2][rows]
        u = c.u[rows, n_ // 2]
        if n_ == 0:
            v.tensor_copy(dst, u).then_inc(s["vn_ready"], 1)
        else:
            ps = side(f"ws{n_}")[rows, 0:512].rearrange("p (h f) -> p h f", h=H)
            v.tensor_tensor(dst, u, ps, ALU.subtract).then_inc(s["vn_ready"], 1)
            v.wait_ge(s["vn_ready"], n_ + 1)
            v.sem_inc(s[f"side_free{side_pair(f'ws{n_}')}"], 1)

    def new_state(n_):
        rows = slice(CHUNK * (n_ % 2), CHUNK * (n_ % 2) + CHUNK)
        ps = side(f"so{n_}")
        if n_ < 3:
            if n_ == 0:
                chain(v.tensor_copy(c.S.rearrange("p h f -> p (h f)"), ps[:, 512:1024]))
            else:
                for h in range(H):
                    chain(v.scalar_tensor_tensor(out=c.S[:, h, :], in0=c.S[:, h, :], scalar=col(c.sums_exp, 16 + 4 * n_ + h),
                                                 in1=blk(ps, H + h), op0=ALU.mult, op1=ALU.add))
            settle()
            v.sem_inc(s["S_ready"], 1)
        v.tensor_copy(c.ob[rows, n_ // 2, :], ps[rows, 0:512]).then_inc(s["ob_out"], 1)
        v.wait_ge(s["ob_out"], n_ + 1)
        v.sem_inc(s[f"side_free{side_pair(f'so{n_}')}"], 1)

    v.wait_ge(s["lam_exp"], 1)
    chain(v.tensor_tensor(c.lamw[:, 0:1], c.lam[:, 3:4], c.lam[:, 2:3], ALU.subtract))
    settle()
    chain(v.tensor_scalar(c.lamw[:, 0:1], c.lamw[:, 0:1], LAMBDA_INIT, None, ALU.subtract))
    new_values(0)
    maxima(0)
    new_state(0)
    combine(0)
    probs_turned(0)
    new_values(1)
    attended(0)
    new_state(1)
    maxima(1)
    new_values(2)
    combine(1)
    new_state(2)
    probs_turned(1)

    def head_norm(squares, ss, sq_flat, root):
        v.wait_ge(s[squares], 1)
        chain(v.tensor_reduce(ss, sq_flat.rearrange("p (a f) -> p a f", a=8), AX_X, ALU.add))
        settle()
        v.tensor_scalar(ss, ss, 1.0 / P, EPS, ALU.mult, ALU.add).then_inc(s[root], 1)
        v.wait_ge(s[root], 2)
        chain(v.reciprocal(ss, ss))
        settle()
    new_values(3)
    attended(1)
    chain(v.tensor_scalar(c.subln, c.subln, 1.0 - LAMBDA_INIT, None, ALU.mult))
    head_norm("oa_squares", c.ra, c.flat["Yb"], "oa_root")
    for i in range(8):
        b = blk(c.flat["F"], i)
        last = v.scalar_tensor_tensor(out=b, in0=b, scalar=col(c.ra, i), in1=c.subln, op0=ALU.mult, op1=ALU.mult)
        if i < 7:
            chain(last)
    last.then_inc(s["ya_ready"], 1)
    new_state(3)
    g8 = c.flat["gate"].rearrange("p (a f) -> p a f", a=8)
    v.tensor_tensor(g8, g8, all8(c.gdng), ALU.mult).then_inc(s["gate_ready"], 1)
    head_norm("ob_squares", c.rb, c.flat["A"], "ob_root")
    v.wait_ge(s["gate_ready"], 2)
    for i in range(8):
        b = blk(c.flat["TT"], i)
        last = v.scalar_tensor_tensor(out=b, in0=b, scalar=col(c.rb, i), in1=blk(c.flat["gate"], i), op0=ALU.mult, op1=ALU.mult)
        if i < 7:
            chain(last)
    last.then_inc(s["yb_ready"], 1)

    v.wait_ge(s["mg_ready"], 4)
    for q in range(4):
        v.wait_ge(s["branch_ready"], q + 1)
        v.tensor_tensor(c.mg[q], c.mg[q], branch_out(c, q % 2), ALU.mult).then_inc(s["branch_used"], 1)
        if q >= 2:
            v.wait_ge(s["branch_used"], q + 1)
            v.tensor_tensor(c.mg[q - 2], c.mg[q - 2], c.mg[q], ALU.add).then_inc(s["merged_ready"], 1)
    for n_, (half, t) in enumerate(PIECES):
        v.wait_ge(s["mix_out"], n_ + 1)
        piece = c.x[:, t, 512 * half:512 * (half + 1)]
        v.tensor_tensor(piece, piece, c.ps[:, 4 + 2 * t + half, :], ALU.add).then_inc(s["x1_ready"], 1)
    v.wait_ge(s["ss1_ready"], len(PIECES))
    v.tensor_tensor(c.ssx, c.ss_piece[:, 0:NT], c.ss_piece[:, NT:2 * NT], ALU.add).then_inc(s["ss1_summed"], 1)
    v.wait_ge(s["r1_root"], 1)
    v.reciprocal(c.rx, c.rx).then_inc(s["r1_ready"], 1)
    v.wait_ge(s["r1_ready"], 1)

    route(v, c, chain, settle)

    for k in range(1, KD, 2):
        if k == 3:
            v.wait_ge(s["rows_turned"], 1)
            v.tensor_copy(c.rows, c.side[1]).then_inc(s["rows_ready"], 1)
        v.wait_ge(s["gathered"], k + 1)
        v.tensor_scalar(c.HgT[:, k, :], c.ps[:, k, :], col(c.gffn, k), None, ALU.mult).then_inc(s["HgT_odd"], 1)
    v.wait_ge(s["row_in_ready"], 1)
    v.wait_ge(s["rows_ready"], 1)
    largest = v.value_load(c.largest[0:1, 0:1], min_val=0, max_val=TOK)

    def windows(m, nwin):
        n = HID * m // P
        nq = P // m
        counts, scan = c.r[:, 488:520], c.r[:, 432:464]
        own, end, valid = c.r[:, 168:200], c.r[:, 200:232], c.r[:, 240:272]
        row = c.row_in[m]
        steps = 0
        for w in range(nwin):
            dst = c.slot_of[:, EXPERTS * w:EXPERTS * (w + 1)]
            for ins in (lambda: v.tensor_scalar(own, scan, float(w * m), None, ALU.add),
                        lambda: v.tensor_tensor(end, scan, counts, ALU.add),
                        lambda: v.tensor_scalar(dst, own, float(SLOTS - m), row, ALU.min, ALU.add),
                        lambda: v.tensor_tensor(valid, end, dst, ALU.is_gt),
                        lambda: v.scalar_tensor_tensor(out=own, in0=dst, scalar=1.0, in1=own, op0=ALU.add, op1=ALU.is_gt),
                        lambda: v.tensor_tensor(valid, valid, own, ALU.mult),
                        lambda: v.scalar_tensor_tensor(out=dst, in0=dst, scalar=1.0, in1=valid, op0=ALU.add, op1=ALU.mult),
                        lambda: v.tensor_scalar(dst, dst, 1.0, None, ALU.subtract)):
                ins().then_inc(s["slot_of_ready"], 1)
                steps += 1
                v.wait_ge(s["slot_of_ready"], steps)

        for w in range(nwin):
            for j in range(nq):
                rows = slice(j * m, (j + 1) * m)
                v.tensor_copy(c.slot_at[rows, EXPERTS * w:EXPERTS * w + EXPERTS // nq],
                              c.slot_of[rows, EXPERTS * w + j:EXPERTS * (w + 1):nq]).then_inc(s["slot_of_ready"], 1)
                steps += 1
        v.wait_ge(s["slot_of_ready"], steps)

        def gate(rnd, u, first):
            g = rnd * (RING * nwin)
            act, bank = c.act[u % 2][:, 0:n], c.ps[:, u % 2, :]
            v.wait_ge(s["gate_sigmoid"], g + (u + 1))
            if u % nwin == nwin - 1:
                v.sem_inc(s["gateup_used"], 1)
            need(v, s["act_turned"], g + (u - 1), first)
            v.tensor_tensor(act, bank[:, 0:n], c.sg[u % 2][:, 0:n], ALU.mult).then_inc(s["gated"], 1)
            v.wait_ge(s["gated"], g + (u + 1))
            v.tensor_tensor(act, act, bank[:, n:2 * n], ALU.mult).then_inc(s["act_ready"], 1)

        def units(rnd, first, final):
            g = rnd * (RING * nwin)
            for u in range(RING * nwin):
                if not (final and u == RING * nwin - 1):
                    gate(rnd, u + 1, first)
                if u % nq == 0:
                    k = rnd * (RING // nq) + u // nwin // nq
                    col0 = c.slot_at[:, EXPERTS * (u % nwin):EXPERTS * (u % nwin + 1)]
                    this = col0[:, k:k + 1] if first else col0[:, bass.ds(k, 1)]
                    st = rnd * (RING * nwin // nq) + u // nq
                    need(v, s["Se_ready"], st, first)
                    v.scalar_tensor_tensor(out=c.S_tmp, in0=c.rows[:, 0:512], scalar=this, in1=c.rows[:, 512:1024],
                                           op0=ALU.is_equal, op1=ALU.mult).then_inc(s["S_half"], 1)
                    v.wait_ge(s["S_half"], st + 1)
                    if final and u == RING * nwin - nq:
                        v.sem_inc(s["rows_dead"], 1)
                    need(v, s["scattered"], st if nq == RING else st - 1, first)
                    v.tensor_tensor(c.S_e[stack_buffer(nq, u)], c.S_tmp[:, 0:256], c.S_tmp[:, 256:512], ALU.add).then_inc(s["Se_ready"], 1)
                v.wait_ge(s["down_ready"], g + (u + 1))
                if u % nwin == nwin - 1:
                    v.sem_inc(s["experts_used"], 1)
                stack_rows(v.tensor_copy, c, m, u, range(nq // 2) if nq > 1 else (0,), s["out_copied"])
        gate(0, 0, True)
        units(0, True, False)
        with v.Fori(1, EXPERTS // RING - 1) as it:
            units(it, False, False)
        units(EXPERTS // RING - 1, True, True)
    by_count(v, largest, windows)
    v.wait_ge(s["gfin_loaded"], 16)
    for t in range(NT):
        v.wait_ge(s["last_scatter"], t + 1)
        v.tensor_tensor(c.x[:, t, :], c.x[:, t, :], c.side[t], ALU.add).then_inc(s["x2_ready"], 1)
        v.wait_ge(s["x2_ready"], t + 1)
        v.tensor_tensor(c.y[:, t, :], c.x[:, t, :], c.gfin, ALU.mult).then_inc(s["y_ready"], 1)
    for t in range(NT):
        v.wait_ge(s["r2_root"], t + 1)
        v.reciprocal(col(c.rx, t), col(c.rx, t)).then_inc(s["r2_ready"], 1)
        v.wait_ge(s["r2_ready"], t + 1)
        v.wait_ge(s["y_ready"], t + 1)
        v.tensor_scalar(c.y[:, t, 512:D], c.y[:, t, 512:D], col(c.rx, t), None, ALU.mult).then_inc(s["out_right_ready"], 1)


def route(v, c, chain, settle):
    s = c.s
    r = c.r
    lg = r[:, 0:72].rearrange("p (t n) -> p t n", t=NT)
    gsh = r[:, 72:80].rearrange("p (t n) -> p t n", t=NT)
    one = {"g": r[:, 80:88].rearrange("p (t n) -> p t n", t=NT), 0: r[:, 88:104].rearrange("p (t n) -> p t n", t=NT),
           1: r[:, 104:120].rearrange("p (t n) -> p t n", t=NT)}
    cand = {4: r[:, 120:128].rearrange("p (t n) -> p t n", t=NT), 8: r[:, 120:136].rearrange("p (t n) -> p t n", t=NT)}
    mx = {"g": r[:, 136:138], 0: r[:, 138:140], 1: r[:, 140:142]}
    low = r[:, 142:144]
    dif = r[:, 144:146]
    gw = r[:, 146:148]
    ing = r[:, 152:168].rearrange("p (t n) -> p t n", t=NT)
    prod = r[:, 168:232].rearrange("p (t e g) -> p t e g", t=NT, e=PER_GROUP)
    picks = r[:, 240:304]
    pick = {0: r[:, 304:368], 1: r[:, 368:432]}
    scan = r[:, 432:464]
    pos, wk = r[:, 480:484], r[:, 484:488]
    base = r[:, 168:232]
    counts = r[:, 488:520]

    def over(ap, n):
        return ap.rearrange("p (t a) -> p t a", a=1).to_broadcast([P, NT, n])

    def link(ins):
        chain(ins)
        settle()

    def first_max(vals, n, key):
        link(v.tensor_reduce(mx[key], vals, AX_X, ALU.max))
        for t in range(NT):
            chain(v.scalar_tensor_tensor(out=cand[n][:, t, :], in0=vals[:, t, :], scalar=mx[key][:, t:t + 1],
                                         in1=c.below[:, 0:n], op0=ALU.is_equal, op1=ALU.mult))
        settle()
        link(v.tensor_reduce(low, cand[n], AX_X, ALU.min))
        link(v.tensor_tensor(one[key], cand[n], over(low, n), ALU.is_equal))
    v.wait_ge(s["logits_ready"], len(PIECES))
    v.wait_ge(s["iota_ready"], 1)
    v.wait_ge(s["row_in_ready"], 1)
    for t in range(NT):
        chain(v.scalar_tensor_tensor(out=lg[:, t, :], in0=logits_out(c, t), scalar=c.rx[:, t:t + 1], in1=c.rbias, op0=ALU.mult, op1=ALU.add))
    settle()
    first_max(lg[:, :, 0:GROUPS], GROUPS, "g")
    v.tensor_tensor(gsh, lg[:, :, 0:GROUPS], over(mx["g"], GROUPS), ALU.subtract).then_inc(s["gexp_in"], 1)
    for t in range(NT):
        chain(v.tensor_tensor(prod[:, t], lg[:, t, GROUPS:].rearrange("p (g e) -> p e g", g=GROUPS),
                              one["g"][:, t, :].rearrange("p (a g) -> p a g", a=1).to_broadcast([P, PER_GROUP, GROUPS]), ALU.mult))
    settle()
    link(v.tensor_reduce(ing, prod, AX_X, ALU.add))
    first_max(ing, PER_GROUP, 0)
    link(v.scalar_tensor_tensor(out=ing, in0=one[0], scalar=-BIG, in1=ing, op0=ALU.mult, op1=ALU.add))
    first_max(ing, PER_GROUP, 1)
    for k in range(2):
        for t in range(NT):
            chain(v.tensor_tensor(pick[k][:, 32 * t:32 * (t + 1)].rearrange("p (g e) -> p g e", g=GROUPS),
                                  one["g"][:, t, :].rearrange("p (g a) -> p g a", a=1).to_broadcast([P, GROUPS, PER_GROUP]),
                                  one[k][:, t, :].rearrange("p (a e) -> p a e", a=1).to_broadcast([P, GROUPS, PER_GROUP]), ALU.mult))
    v.tensor_tensor(dif, mx[1], mx[0], ALU.subtract).then_inc(s["texp_in"], 1)
    settle()
    v.tensor_tensor(picks, pick[0], pick[1], ALU.add).then_inc(s["picks_ready"], 1)
    v.wait_ge(s["gexp_out"], 1)
    link(v.tensor_reduce(gw, gsh, AX_X, ALU.add))
    link(v.reciprocal(gw, gw))
    v.wait_ge(s["texp_out"], 1)
    link(v.tensor_scalar(wk[:, 0:2], dif, 1.0, None, ALU.add))
    link(v.reciprocal(wk[:, 0:2], wk[:, 0:2]))
    link(v.tensor_tensor(wk[:, 0:2], wk[:, 0:2], gw, ALU.mult))
    chain(v.tensor_tensor(wk[:, 2:4], wk[:, 0:2], dif, ALU.mult))
    v.wait_ge(s["ranks_ready"], 1)
    chain(v.tensor_copy(counts, c.ps[:, 1, 64:96]))
    settle()
    chain(v.tensor_tensor_scan(scan, counts, counts, 0.0, ALU.add, ALU.bypass))
    chain(v.tensor_reduce(low[:, 0:1], counts, AX_X, ALU.max))
    settle()
    link(v.tensor_tensor(scan, scan, counts, ALU.subtract))
    link(v.tensor_tensor(base.rearrange("p (t e) -> p t e", t=NT), c.ps[:, 1, 0:64].rearrange("p (t e) -> p t e", t=NT),
                         scan.rearrange("p (a e) -> p a e", a=1).to_broadcast([P, NT, EXPERTS]), ALU.add))
    for k in range(2):
        chain(v.tensor_tensor(pick[k], pick[k], base, ALU.mult))
    settle()
    for k in range(2):
        chain(v.tensor_reduce(pos[:, 2 * k:2 * k + 2], pick[k].rearrange("p (t e) -> p t e", t=NT), AX_X, ALU.add))
    settle()
    v.tensor_copy(c.largest[:, :], low[0:1, 0:1]).then_inc(s["offsets_ready"], 1)
    for t in range(NT):
        chain(v.tensor_scalar(c.onehot[:, t, :], c.iota[:, :], pos[:, t:t + 1], None, ALU.is_equal))
    settle()
    for t in range(NT):
        v.scalar_tensor_tensor(out=c.onehot[:, t, :], in0=c.iota[:, :], scalar=pos[:, 2 + t:3 + t], in1=c.onehot[:, t, :],
                               op0=ALU.is_equal, op1=ALU.add).then_inc(s["onehot_ready"], 1)
    v.wait_ge(s["starts_zeroed"], 1)
    v.wait_ge(s["offsets_ready"], 1)
    for (m, w), dst in c.starts.items():
        chain(v.tensor_scalar(dst[:, 0:EXPERTS], scan[0:1, :], float(w * m), float(SLOTS - m), ALU.add, ALU.min))
    settle()
    v.sem_inc(s["starts_ready"], 1)


def build(nc, io):
    with ExitStack() as ctx:
        c = lay_out(nc, ctx)
        block = ctx.enter_context(nc.Block())

        @block.sync
        def _(sp):
            sync_program(sp, c, io)

        @block.gpsimd
        def _(pool):
            gpsimd_program(pool, c, io)
            pool.wait_ge(c.s["rows_dead"], 1)
            pool.dma_start(c.gfin, io["norm_final_gain"].rearrange("(a d) -> a d", a=1).partition_broadcast(P)
                           .rearrange("p a d -> p (a d)")).then_inc(c.s["gfin_loaded"], 16)

        @block.scalar
        def _(act):
            scalar_program(act, c, io)

        @block.tensor
        def _(pe):
            tensor_program(pe, c, io)

        @block.vector
        def _(v):
            vector_program(v, c, io)


_INS = ["x", "norm_mix_gain", "w_in", "diff_lambda_q1", "diff_lambda_k1", "diff_lambda_q2", "diff_lambda_k2",
        "diff_subln_gain", "gdn_conv_w", "gdn_a_log", "gdn_dt_bias", "gdn_norm_gain", "w_branch_attn", "w_branch_gdn",
        "w_out", "norm_ffn_gain", "moe_w_group", "moe_b_group", "moe_w_expert", "moe_b_expert", "moe_w_gate",
        "moe_w_up", "moe_w_down", "norm_final_gain"]


def kernel(**inputs):
    import numpy as _np
    import concourse.bacc as _bacc
    from concourse import mybir as _mybir
    from concourse.bass_utils import run_bass_kernel_spmd as _run

    nc = _bacc.Bacc("TRN2", target_bir_lowering=False, num_devices=1)
    arrays, io = {}, {}
    for name in _INS:
        a = _np.ascontiguousarray(inputs[name])
        arrays[f"in_{name}"] = a
        io[name] = nc.dram_tensor(f"in_{name}", a.shape, _mybir.dt.from_np(a.dtype), kind="ExternalInput").ap()
    io["out"] = nc.dram_tensor("out_y", (1, TOK, D), _mybir.dt.from_np(_np.dtype("float32")), kind="ExternalOutput").ap()
    build(nc, io)
    r = _run(nc, [arrays], core_ids=[0])
    return r.results[0]["out_y"]
```
